# Optimizing a Trainium2 kernel written in Bass

```python
import jax, jax.numpy as jnp
from jax import lax
import numpy as np
import functools
import math
import jax
import jax.numpy as jnp

D_MODEL = 1024
BATCH = 1
SEQ = 512
DEPTH = 1

CHUNK = 64
D_MIX = D_MODEL
N_GROUPS = 4
GW = D_MIX // N_GROUPS
HEAD_DIM = 64
N_HEADS_GROUP = GW // HEAD_DIM
ATTN_LEFT_CHUNKS = 8
N_BAND = ATTN_LEFT_CHUNKS + 1
REL_CLIP = 256
ATTN_SCALE = HEAD_DIM ** -0.5
NEG_INF = -1e30
RWKV_W_RANK = 32
RWKV_A_RANK = 32
RWKV_G_RANK = 64
RWKV_GN_EPS = HEAD_DIM * 1e-5
LRU_CONV = 4
LRU_C = 8.0
LRU_BLOCKS = N_HEADS_GROUP
LRU_BLOCK_DIM = GW // LRU_BLOCKS
ATTN_COLS = 3 * GW
HGRN_COLS = 4 * GW
RWKV_COLS = 3 * GW + RWKV_W_RANK + RWKV_A_RANK + RWKV_G_RANK
LRU_COLS = 2 * GW
D_IN = ATTN_COLS + HGRN_COLS + RWKV_COLS + LRU_COLS
MLP_HIDDEN = 4 * D_MODEL
RMS_EPS = 1e-6


def split_cols(t, sizes):
    offs = np.cumsum(sizes)[:-1].tolist()
    return jnp.split(t, offs, axis=-1)

def rms_norm(x, gain):
    xf = x.astype(jnp.float32)
    y = xf * lax.rsqrt(jnp.mean(xf * xf, axis=-1, keepdims=True) + RMS_EPS)
    return (y * gain.astype(jnp.float32)).astype(x.dtype)

def to_heads(t):
    return t.reshape(t.shape[0], t.shape[1], N_HEADS_GROUP, HEAD_DIM)

def to_chunks(t):
    b, s, _ = t.shape
    return t.reshape(b, s // CHUNK, CHUNK, N_HEADS_GROUP, HEAD_DIM).transpose(1, 0, 3, 2, 4)

def from_chunks(t):
    nc, b = t.shape[0], t.shape[1]
    return t.transpose(1, 0, 3, 2, 4).reshape(b, nc * CHUNK, GW)

def chunk_attention(q, k, v, rel_bias):
    b, s, _ = q.shape
    nc = s // CHUNK
    shp = (b, nc, CHUNK, N_HEADS_GROUP, HEAD_DIM)
    qc, kc, vc = q.reshape(shp), k.reshape(shp), v.reshape(shp)
    pad = ((0, 0), (ATTN_LEFT_CHUNKS, 0), (0, 0), (0, 0), (0, 0))
    band = jnp.arange(nc)[:, None] + jnp.arange(N_BAND)[None, :]
    kb = jnp.pad(kc, pad)[:, band].reshape(b, nc, N_BAND * CHUNK, N_HEADS_GROUP, HEAD_DIM)
    vb = jnp.pad(vc, pad)[:, band].reshape(b, nc, N_BAND * CHUNK, N_HEADS_GROUP, HEAD_DIM)
    scores = jnp.einsum('bcqhd,bckhd->bchqk', qc, kb) * ATTN_SCALE
    key_off = ((jnp.arange(N_BAND) - ATTN_LEFT_CHUNKS)[:, None] * CHUNK
               + jnp.arange(CHUNK)[None, :]).reshape(-1)
    rel = key_off[None, :] - jnp.arange(CHUNK)[:, None]
    bias = rel_bias.astype(jnp.float32)[:, jnp.clip(rel, -REL_CLIP, REL_CLIP) + REL_CLIP]
    valid = jnp.repeat(band >= ATTN_LEFT_CHUNKS, CHUNK, axis=1)
    scores = jnp.where(valid[None, :, None, None, :], scores + bias[None, None], NEG_INF)
    probs = jax.nn.softmax(scores, axis=-1)
    out = jnp.einsum('bchqk,bckhd->bcqhd', probs, vb)
    return out.reshape(b, s, GW)

def hgrn2(q_raw, f_raw, i_raw, g_raw, lb, norm_gain):
    b = q_raw.shape[0]
    log_f = jnp.logaddexp(jnp.log(lb), jnp.log1p(-lb) + jax.nn.log_sigmoid(f_raw))
    key = (1.0 - lb) * jax.nn.sigmoid(-f_raw)
    q = jax.nn.silu(q_raw)
    tri = jnp.tril(jnp.ones((CHUNK, CHUNK), dtype=bool))

    def step(state, inp):
        qc, kc, vc, gc = inp
        cum = jnp.cumsum(gc, axis=2)
        last = cum[:, :, -1:, :]
        o_inter = jnp.einsum('bhtk,bhkv->bhtv', qc * jnp.exp(cum), state)
        diff = cum[:, :, :, None, :] - cum[:, :, None, :, :]
        decay = jnp.exp(jnp.where(tri[None, None, :, :, None], diff, -jnp.inf))
        att = jnp.einsum('bhtk,bhsk,bhtsk->bhts', qc, kc, decay)
        o_intra = jnp.einsum('bhts,bhsv->bhtv', att, vc)
        new_state = (jnp.exp(last).transpose(0, 1, 3, 2) * state
                     + jnp.einsum('bhsk,bhsv->bhkv', kc * jnp.exp(last - cum), vc))
        return new_state, o_inter + o_intra

    state0 = jnp.zeros((b, N_HEADS_GROUP, HEAD_DIM, HEAD_DIM), jnp.float32)
    _, o = lax.scan(step, state0, (to_chunks(q), to_chunks(key), to_chunks(i_raw), to_chunks(log_f)))
    o = to_heads(from_chunks(o))
    o = o * lax.rsqrt(jnp.mean(o * o, axis=-1, keepdims=True) + RMS_EPS)
    return o.reshape(g_raw.shape) * norm_gain * jax.nn.silu(g_raw)

def rwkv7(pc, mu, w0, w2, a0, a2, g2, k_k, k_a, r_k, ln_w, ln_b):
    b, s, _ = pc.shape
    prev = jnp.pad(pc, ((0, 0), (1, 0), (0, 0)))[:, :-1]
    xs = pc + mu * (prev - pc)
    r, k, v, w_lo, a_lo, g_lo = split_cols(xs, [GW, GW, GW, RWKV_W_RANK, RWKV_A_RANK, RWKV_G_RANK])
    w_pre = -jax.nn.softplus(-(w0 + jnp.tanh(w_lo) @ w2)) - 0.5
    decay = jnp.exp(-jnp.exp(w_pre))
    a = jax.nn.sigmoid(a0 + a_lo @ a2)
    g = jax.nn.sigmoid(g_lo) @ g2
    kk = to_heads(k * k_k)
    kk = kk / jnp.maximum(jnp.sqrt(jnp.sum(kk * kk, axis=-1, keepdims=True)), 1e-12)
    k = k * (1.0 + (a - 1.0) * k_a)
    r_h, w_h, k_h, v_h, a_h = to_heads(r), to_heads(decay), to_heads(k), to_heads(v), to_heads(a)

    def step(state, inp):
        rt, wt, kt, vt, kkt, at = inp
        sa = jnp.einsum('bhvk,bhk->bhv', state, -kkt)
        state = (state * wt[:, :, None, :] + sa[..., None] * (kkt * at)[:, :, None, :]
                 + vt[..., None] * kt[:, :, None, :])
        return state, jnp.einsum('bhvk,bhk->bhv', state, rt)

    seq_first = lambda t: t.transpose(1, 0, 2, 3)
    state0 = jnp.zeros((b, N_HEADS_GROUP, HEAD_DIM, HEAD_DIM), jnp.float32)
    _, y = lax.scan(step, state0, (seq_first(r_h), seq_first(w_h), seq_first(k_h),
                                   seq_first(v_h), seq_first(kk), seq_first(a_h)))
    y = seq_first(y)
    mean = jnp.mean(y, axis=-1, keepdims=True)
    var = jnp.mean(jnp.square(y - mean), axis=-1, keepdims=True)
    y = ((y - mean) * lax.rsqrt(var + RWKV_GN_EPS)).reshape(b, s, GW) * ln_w + ln_b
    bonus = (jnp.sum(r_h * k_h * r_k, axis=-1, keepdims=True) * v_h).reshape(b, s, GW)
    return (y + bonus) * g

def rglru(xb, gb, conv_w, conv_b, wa, ba, wx, bx, lam):
    b, s, _ = xb.shape
    conv = lax.conv_general_dilated(xb, conv_w.astype(xb.dtype)[:, None, :], window_strides=(1,),
                                    padding=[(LRU_CONV - 1, 0)],
                                    dimension_numbers=('NWC', 'WIO', 'NWC'),
                                    feature_group_count=GW) + conv_b
    xh = conv.reshape(b, s, LRU_BLOCKS, LRU_BLOCK_DIM)
    gate_r = jax.nn.sigmoid(jnp.einsum('bsnd,nde->bsne', xh, wa).reshape(b, s, GW) + ba)
    gate_i = jax.nn.sigmoid(jnp.einsum('bsnd,nde->bsne', xh, wx).reshape(b, s, GW) + bx)
    log_a = -LRU_C * gate_r * jax.nn.softplus(-lam)
    a = jnp.exp(log_a)
    inp = jnp.sqrt(-jnp.expm1(2.0 * log_a)) * (gate_i * conv)

    def combine(c1, c2):
        a1, b1 = c1
        a2, b2 = c2
        return a1 * a2, a2 * b1 + b2

    _, h = lax.associative_scan(combine, (a, inp), axis=1)
    return h * jax.nn.gelu(gb)

def first_inputs(seed: int = 0) -> dict:
    key = jax.random.key(seed)
    ks = jax.random.split(key, 32)
    L = DEPTH

    def nrm(k, shape, scale):
        return jax.random.normal(k, shape, jnp.float32) * scale

    u = jax.random.uniform(ks[27], (L, GW), jnp.float32, 0.9, 0.999)
    a_root = u ** (1.0 / LRU_C)
    lam = jnp.log(a_root) - jnp.log1p(-a_root)
    return {
        'x': nrm(ks[0], (BATCH, SEQ, D_MODEL), 1.0),
        'norm_mix_pre': 1.0 + nrm(ks[1], (L, D_MODEL), 0.05),
        'norm_mix_post': 1.0 + nrm(ks[2], (L, D_MODEL), 0.05),
        'norm_mlp_pre': 1.0 + nrm(ks[3], (L, D_MODEL), 0.05),
        'norm_mlp_post': 1.0 + nrm(ks[4], (L, D_MODEL), 0.05),
        'w_in': nrm(ks[5], (L, D_MODEL, D_IN), D_MODEL ** -0.5),
        'w_out': nrm(ks[6], (L, D_MIX, D_MODEL), D_MIX ** -0.5),
        'attn_rel_bias': nrm(ks[7], (L, N_HEADS_GROUP, 2 * REL_CLIP + 1), 0.2),
        'hgrn_lb_logits': nrm(ks[8], (L, GW), 0.5),
        'hgrn_norm': 1.0 + nrm(ks[9], (L, GW), 0.05),
        'rwkv_mu': jax.random.uniform(ks[10], (L, RWKV_COLS), jnp.float32, 0.2, 0.8),
        'rwkv_w0': jax.random.uniform(ks[11], (L, GW), jnp.float32, -6.0, 1.0),
        'rwkv_w2': nrm(ks[12], (L, RWKV_W_RANK, GW), 0.5 * RWKV_W_RANK ** -0.5),
        'rwkv_a0': nrm(ks[13], (L, GW), 0.1),
        'rwkv_a2': nrm(ks[14], (L, RWKV_A_RANK, GW), 0.5 * RWKV_A_RANK ** -0.5),
        'rwkv_g2': nrm(ks[15], (L, RWKV_G_RANK, GW), RWKV_G_RANK ** -0.5),
        'rwkv_k_k': 0.85 + nrm(ks[16], (L, GW), 0.05),
        'rwkv_k_a': 1.0 + nrm(ks[17], (L, GW), 0.05),
        'rwkv_r_k': nrm(ks[18], (L, N_HEADS_GROUP, HEAD_DIM), 0.1),
        'rwkv_ln_w': 1.0 + nrm(ks[19], (L, GW), 0.05),
        'rwkv_ln_b': nrm(ks[20], (L, GW), 0.02),
        'lru_conv_w': nrm(ks[21], (L, LRU_CONV, GW), 0.5 * LRU_CONV ** -0.5),
        'lru_conv_b': nrm(ks[22], (L, GW), 0.02),
        'lru_wa': nrm(ks[23], (L, LRU_BLOCKS, LRU_BLOCK_DIM, LRU_BLOCK_DIM), LRU_BLOCK_DIM ** -0.5),
        'lru_ba': nrm(ks[24], (L, GW), 0.02),
        'lru_wx': nrm(ks[25], (L, LRU_BLOCKS, LRU_BLOCK_DIM, LRU_BLOCK_DIM), LRU_BLOCK_DIM ** -0.5),
        'lru_bx': nrm(ks[26], (L, GW), 0.02),
        'lru_lambda': lam,
        'mlp_w1': nrm(ks[28], (L, D_MODEL, MLP_HIDDEN), D_MODEL ** -0.5),
        'mlp_w2': nrm(ks[29], (L, MLP_HIDDEN, D_MODEL), MLP_HIDDEN ** -0.5),
    }

def first_block(x, norm_mix_pre, norm_mix_post, norm_mlp_pre, norm_mlp_post, w_in, w_out,
              attn_rel_bias, hgrn_lb_logits, hgrn_norm, rwkv_mu, rwkv_w0, rwkv_w2, rwkv_a0, rwkv_a2,
              rwkv_g2, rwkv_k_k, rwkv_k_a, rwkv_r_k, rwkv_ln_w, rwkv_ln_b, lru_conv_w, lru_conv_b,
              lru_wa, lru_ba, lru_wx, lru_bx, lru_lambda, mlp_w1, mlp_w2):
    dt = x.dtype
    f32 = jnp.float32
    lb_sm = jax.nn.softmax(hgrn_lb_logits.astype(f32), axis=0)
    lb_all = jnp.maximum(jnp.cumsum(lb_sm, axis=0) - lb_sm[0:1], 0.0)
    for l in range(DEPTH):
        h = rms_norm(x, norm_mix_pre[l])
        proj = (h @ w_in[l]).astype(f32)
        pa, pb, pc, pd = split_cols(proj, [ATTN_COLS, HGRN_COLS, RWKV_COLS, LRU_COLS])
        qa, ka, va = split_cols(pa, [GW, GW, GW])
        ya = chunk_attention(qa, ka, va, attn_rel_bias[l])
        qb, fb, ib, gb = split_cols(pb, [GW, GW, GW, GW])
        yb = hgrn2(qb, fb, ib, gb, lb_all[l], hgrn_norm[l].astype(f32))
        yc = rwkv7(pc, rwkv_mu[l].astype(f32), rwkv_w0[l].astype(f32), rwkv_w2[l].astype(f32),
                   rwkv_a0[l].astype(f32), rwkv_a2[l].astype(f32), rwkv_g2[l].astype(f32),
                   rwkv_k_k[l].astype(f32), rwkv_k_a[l].astype(f32), rwkv_r_k[l].astype(f32),
                   rwkv_ln_w[l].astype(f32), rwkv_ln_b[l].astype(f32))
        xd, gd = split_cols(pd, [GW, GW])
        yd = rglru(xd, gd, lru_conv_w[l].astype(f32), lru_conv_b[l].astype(f32), lru_wa[l].astype(f32),
                   lru_ba[l].astype(f32), lru_wx[l].astype(f32), lru_bx[l].astype(f32),
                   lru_lambda[l].astype(f32))
        mix = jnp.concatenate([ya, yb, yc, yd], axis=-1).astype(dt)
        x = x + rms_norm(mix @ w_out[l], norm_mix_post[l])
        h = rms_norm(x, norm_mlp_pre[l])
        ff = jnp.square(jax.nn.relu(h @ mlp_w1[l])) @ mlp_w2[l]
        x = x + rms_norm(ff, norm_mlp_post[l])
    return x


DEPTH_2 = 2

GRID_W = 64
CTX_LEN = 256
ROPE_THETA = 10000.0
NORM_EPS = 1e-6
NEG_INF_2 = -1e30
BLOCK = 128
WINDOW = 128

A_HEADS = 8
A_KV_HEADS = 2
A_HEAD_DIM = 64
B_HEADS = 4
B_QK_DIM = 64
B_V_DIM = 2 * B_QK_DIM
A_Q_W = A_HEADS * A_HEAD_DIM
A_KV_W = A_KV_HEADS * A_HEAD_DIM
B_QK_W = B_HEADS * 2 * B_QK_DIM
B_V_W = B_HEADS * B_V_DIM
AB_Q_W = A_Q_W + B_QK_W
AB_IN_W = AB_Q_W + 2 * A_KV_W + B_QK_W + B_V_W
AB_OUT_W = A_Q_W + B_V_W

C_HEADS = 16
C_Q_LORA = 384
C_KV_LORA = 256
C_NOPE = 64
C_ROPE = 32
C_V = 64
C_IN_W = C_Q_LORA + C_KV_LORA + C_ROPE
C_OUT_W = C_HEADS * C_V

FFN_HIDDEN = ((8 * D_MODEL + 3 * 256 - 1) // (3 * 256)) * 256

N_EVEN = (DEPTH_2 + 1) // 2
N_ODD = DEPTH_2 // 2

F32 = jnp.float32


def rmsnorm(x, g):
    xf = x.astype(F32)
    y = xf * lax.rsqrt(jnp.mean(xf * xf, axis=-1, keepdims=True) + NORM_EPS)
    return (y * g.astype(F32)).astype(x.dtype)

def modulate(xn, shift, scale):
    return xn * (1.0 + scale) + shift

def joint_softmax(*logits):
    m = functools.reduce(jnp.maximum, [s.max(axis=-1, keepdims=True) for s in logits])
    e = [jnp.exp(s - m) for s in logits]
    inv = 1.0 / functools.reduce(jnp.add, [t.sum(axis=-1, keepdims=True) for t in e])
    return [t * inv for t in e]

def axial_rope_tables(rows, rot_dim):
    row = jnp.repeat(jnp.arange(rows, dtype=F32), GRID_W)
    col = jnp.tile(jnp.arange(GRID_W, dtype=F32), rows)
    axis_dim = rot_dim // 2
    inv_freq = ROPE_THETA ** (-jnp.arange(0, axis_dim, 2, dtype=F32) / axis_dim)
    ang = jnp.concatenate([row[:, None] * inv_freq, col[:, None] * inv_freq], axis=-1)
    return jnp.cos(ang), jnp.sin(ang)

def apply_axial_rope(x, tab):
    cos, sin = tab
    quarter = x.shape[-1] // 4
    xr, xc = jnp.split(x.astype(F32), 2, axis=-1)

    def rot(u, cs, sn):
        u1, u2 = jnp.split(u, 2, axis=-1)
        return jnp.concatenate([u1 * cs - u2 * sn, u2 * cs + u1 * sn], axis=-1)

    out = jnp.concatenate([
        rot(xr, cos[:, None, :quarter], sin[:, None, :quarter]),
        rot(xc, cos[:, None, quarter:], sin[:, None, quarter:])], axis=-1)
    return out.astype(x.dtype)

def to_blocks(t):
    b, n = t.shape[:2]
    return jnp.moveaxis(t.reshape(b, n // BLOCK, BLOCK, *t.shape[2:]), 1, 0)

def from_blocks(t):
    t = jnp.moveaxis(t, 0, 1)
    return t.reshape(t.shape[0], -1, *t.shape[3:])

def swiglu(h, w13, w2):
    gate, up = jnp.split(h @ w13, 2, axis=-1)
    return (jax.nn.silu(gate) * up) @ w2

def lambda_init(layer_idx):
    return 0.8 - 0.6 * math.exp(-0.3 * layer_idx)

def window_gqa_latent(q, k, v, k_ctx, v_ctx, sink):
    bsz, n, _, dh = q.shape
    nb = n // BLOCK
    g = A_HEADS // A_KV_HEADS
    scale = dh ** -0.5
    qb = q.reshape(bsz, nb, BLOCK, A_KV_HEADS, g, dh)

    def band(t):
        tp = jnp.pad(t, ((0, 0), (BLOCK, BLOCK), (0, 0), (0, 0)))
        tp = tp.reshape(bsz, nb + 2, BLOCK, A_KV_HEADS, dh)
        return jnp.concatenate([tp[:, :-2], tp[:, 1:-1], tp[:, 2:]], axis=2)

    kb, vb = band(k), band(v)
    s_loc = jnp.einsum('bnqhgd,bnkhd->bhgnqk', qb, kb).astype(F32) * scale
    s_ctx = jnp.einsum('bnqhgd,bchd->bhgnqc', qb, k_ctx).astype(F32) * scale
    qi = jnp.arange(BLOCK)[:, None]
    kj = jnp.arange(3 * BLOCK)[None, :]
    key_pos = (jnp.arange(nb)[:, None, None] - 1) * BLOCK + kj[None]
    valid = (jnp.abs(kj - BLOCK - qi) <= WINDOW)[None] & (key_pos >= 0) & (key_pos < n)
    s_loc = jnp.where(valid, s_loc, NEG_INF_2)
    s_sink = sink.astype(F32).reshape(1, A_KV_HEADS, g, 1, 1, 1)
    p_loc, p_ctx, _ = joint_softmax(s_loc, s_ctx, s_sink)
    o = (jnp.einsum('bhgnqk,bnkhd->bnqhgd', p_loc.astype(v.dtype), vb)
         + jnp.einsum('bhgnqc,bchd->bnqhgd', p_ctx.astype(v.dtype), v_ctx))
    return o.reshape(bsz, n, A_HEADS * dh)

def gqa_ctx(q, k, v, sink):
    bsz, t, _, dh = q.shape
    g = A_HEADS // A_KV_HEADS
    qg = q.reshape(bsz, t, A_KV_HEADS, g, dh)
    s = jnp.einsum('bqhgd,bkhd->bhgqk', qg, k).astype(F32) * dh ** -0.5
    p, _ = joint_softmax(s, sink.astype(F32).reshape(1, A_KV_HEADS, g, 1, 1))
    o = jnp.einsum('bhgqk,bkhd->bqhgd', p.astype(v.dtype), v)
    return o.reshape(bsz, t, A_HEADS * dh)

def diff_attend(q, kv_parts, lam):
    scale = q.shape[-1] ** -0.5
    logits = [jnp.einsum('bqhmd,bkhmd->bmhqk', q, k).astype(F32) * scale for k, _ in kv_parts]
    probs = joint_softmax(*logits)
    outs = [jnp.einsum('bhqk,bkhd->bqhd', (p[:, 0] - lam * p[:, 1]).astype(v.dtype), v)
            for p, (_, v) in zip(probs, kv_parts)]
    return functools.reduce(jnp.add, outs)

def diff_out(o, subln_g, lam_init):
    b, t = o.shape[:2]
    return (rmsnorm(o, subln_g) * (1.0 - lam_init)).reshape(b, t, -1)

def ab_queries(p_q):
    b, t = p_q.shape[:2]
    qa = p_q[..., :A_Q_W].reshape(b, t, A_HEADS, A_HEAD_DIM)
    qb = p_q[..., A_Q_W:].reshape(b, t, B_HEADS, 2, B_QK_DIM)
    return qa, qb

def ab_keys_values(p_kv):
    b, t = p_kv.shape[:2]
    o1 = A_KV_W
    o2 = 2 * A_KV_W
    o3 = o2 + B_QK_W
    ka = p_kv[..., :o1].reshape(b, t, A_KV_HEADS, A_HEAD_DIM)
    va = p_kv[..., o1:o2].reshape(b, t, A_KV_HEADS, A_HEAD_DIM)
    kb = p_kv[..., o2:o3].reshape(b, t, B_HEADS, 2, B_QK_DIM)
    vb = p_kv[..., o3:].reshape(b, t, B_HEADS, B_V_DIM)
    return ka, va, kb, vb

def rope_diff(t, tab):
    b, n = t.shape[:2]
    return apply_axial_rope(t.reshape(b, n, B_HEADS * 2, B_QK_DIM), tab).reshape(t.shape)

def mixer_ab(hx, hc, w_in, w_out, sink, lam_vec, subln_g, lam_init, tab, ctx_queries):
    p = hx @ w_in
    qa, qb = ab_queries(p[..., :AB_Q_W])
    ka, va, kb, vb = ab_keys_values(p[..., AB_Q_W:])
    qa, ka = apply_axial_rope(qa, tab), apply_axial_rope(ka, tab)
    qb, kb = rope_diff(qb, tab), rope_diff(kb, tab)
    if ctx_queries:
        pc = hc @ w_in
        cqa, cqb = ab_queries(pc[..., :AB_Q_W])
        cka, cva, ckb, cvb = ab_keys_values(pc[..., AB_Q_W:])
    else:
        cka, cva, ckb, cvb = ab_keys_values(hc @ w_in[:, AB_Q_W:])
    lv = lam_vec.astype(F32)
    lam = jnp.exp(jnp.sum(lv[0] * lv[1])) - jnp.exp(jnp.sum(lv[2] * lv[3])) + lam_init

    oa = window_gqa_latent(qa, ka, va, cka, cva, sink)
    ob = from_blocks(lax.map(lambda qblk: diff_attend(qblk, [(kb, vb), (ckb, cvb)], lam),
                             to_blocks(qb)))
    yx = jnp.concatenate([oa, diff_out(ob, subln_g, lam_init)], axis=-1) @ w_out
    if not ctx_queries:
        return yx, None
    oca = gqa_ctx(cqa, cka, cva, sink)
    ocb = diff_out(diff_attend(cqb, [(ckb, cvb)], lam), subln_g, lam_init)
    yc = jnp.concatenate([oca, ocb], axis=-1) @ w_out
    return yx, yc

def mla_queries(p_q, q_norm_g, wq_b):
    b, t = p_q.shape[:2]
    q = (rmsnorm(p_q, q_norm_g) @ wq_b).reshape(b, t, C_HEADS, C_NOPE + C_ROPE)
    return q[..., :C_NOPE], q[..., C_NOPE:]

def mla_keys_values(p_kv, kv_norm_g, wkv_b):
    b, t = p_kv.shape[:2]
    kv_lat, k_rope = p_kv[..., :C_KV_LORA], p_kv[..., C_KV_LORA:]
    kv = (rmsnorm(kv_lat, kv_norm_g) @ wkv_b).reshape(b, t, C_HEADS, C_NOPE + C_V)
    return kv[..., :C_NOPE], k_rope, kv[..., C_NOPE:]

def mla_attend(q_nope, q_rope, kv_parts):
    scale = (C_NOPE + C_ROPE) ** -0.5
    logits = [(jnp.einsum('bqhd,bkhd->bhqk', q_nope, kn)
               + jnp.einsum('bqhr,bkr->bhqk', q_rope, kr)).astype(F32) * scale
              for kn, kr, _ in kv_parts]
    probs = joint_softmax(*logits)
    outs = [jnp.einsum('bhqk,bkhd->bqhd', p.astype(v.dtype), v) for p, (_, _, v) in zip(probs, kv_parts)]
    return functools.reduce(jnp.add, outs)

def mixer_mla(hx, hc, w_in, q_norm_g, kv_norm_g, wq_b, wkv_b, w_out, tab, ctx_queries):
    bsz, n, _ = hx.shape
    p = hx @ w_in
    qn, qr = mla_queries(p[..., :C_Q_LORA], q_norm_g, wq_b)
    kn, kr, v = mla_keys_values(p[..., C_Q_LORA:], kv_norm_g, wkv_b)
    qr = apply_axial_rope(qr, tab)
    kr = apply_axial_rope(kr[:, :, None, :], tab)[:, :, 0, :]
    if ctx_queries:
        pc = hc @ w_in
        cqn, cqr = mla_queries(pc[..., :C_Q_LORA], q_norm_g, wq_b)
        ckn, ckr, cv = mla_keys_values(pc[..., C_Q_LORA:], kv_norm_g, wkv_b)
    else:
        ckn, ckr, cv = mla_keys_values(hc @ w_in[:, C_Q_LORA:], kv_norm_g, wkv_b)
    o = from_blocks(lax.map(lambda qs: mla_attend(qs[0], qs[1], [(kn, kr, v), (ckn, ckr, cv)]),
                            (to_blocks(qn), to_blocks(qr))))
    yx = o.reshape(bsz, n, C_OUT_W) @ w_out
    if not ctx_queries:
        return yx, None
    oc = mla_attend(cqn, cqr, [(ckn, ckr, cv)])
    yc = oc.reshape(bsz, hc.shape[1], C_OUT_W) @ w_out
    return yx, yc

def second_inputs(seed: int = 0) -> dict:
    key = jax.random.key(seed)
    ks = jax.random.split(key, 20)

    def nrm(k, shape, scale):
        return jax.random.normal(k, shape, F32) * scale

    d = D_MODEL
    return {
        'x': nrm(ks[0], (BATCH, SEQ, d), 1.0),
        'c': nrm(ks[1], (BATCH, d), 1.0),
        'ctx': nrm(ks[2], (BATCH, CTX_LEN, d), 1.0),
        'c_ctx': nrm(ks[3], (d,), 1.0),
        'ada_w': nrm(ks[4], (DEPTH_2, d, 6 * d), 0.5 * d ** -0.5),
        'ada_b': nrm(ks[5], (DEPTH_2, 6 * d), 0.01),
        'norm_g': 1.0 + nrm(ks[6], (DEPTH_2, 4, d), 0.05),
        'ffn_w13': nrm(ks[7], (DEPTH_2, d, 2 * FFN_HIDDEN), d ** -0.5),
        'ffn_w2': nrm(ks[8], (DEPTH_2, FFN_HIDDEN, d), FFN_HIDDEN ** -0.5),
        'ab_w_in': nrm(ks[9], (N_EVEN, d, AB_IN_W), d ** -0.5),
        'ab_w_out': nrm(ks[10], (N_EVEN, AB_OUT_W, d), AB_OUT_W ** -0.5),
        'ab_sink': nrm(ks[11], (N_EVEN, A_HEADS), 0.5),
        'diff_lambda': nrm(ks[12], (N_EVEN, 4, B_QK_DIM), 0.1),
        'diff_subln_g': 1.0 + nrm(ks[13], (N_EVEN, B_V_DIM), 0.05),
        'mla_w_in': nrm(ks[14], (N_ODD, d, C_IN_W), d ** -0.5),
        'mla_q_norm_g': 1.0 + nrm(ks[15], (N_ODD, C_Q_LORA), 0.05),
        'mla_kv_norm_g': 1.0 + nrm(ks[16], (N_ODD, C_KV_LORA), 0.05),
        'mla_wq_b': nrm(ks[17], (N_ODD, C_Q_LORA, C_HEADS * (C_NOPE + C_ROPE)), C_Q_LORA ** -0.5),
        'mla_wkv_b': nrm(ks[18], (N_ODD, C_KV_LORA, C_HEADS * (C_NOPE + C_V)), C_KV_LORA ** -0.5),
        'mla_w_out': nrm(ks[19], (N_ODD, C_OUT_W, d), C_OUT_W ** -0.5),
    }

def second_block(x, c, ctx, c_ctx, ada_w, ada_b, norm_g, ffn_w13, ffn_w2,
              ab_w_in, ab_w_out, ab_sink, diff_lambda, diff_subln_g,
              mla_w_in, mla_q_norm_g, mla_kv_norm_g, mla_wq_b, mla_wkv_b, mla_w_out):
    bsz, n, d = x.shape
    ROWS = n // GRID_W
    tab_ab = axial_rope_tables(ROWS, A_HEAD_DIM)
    tab_c = axial_rope_tables(ROWS, C_ROPE)
    sc_x = jax.nn.silu(c)
    sc_c = jax.nn.silu(c_ctx)
    for l in range(DEPTH_2):
        ctx_out = l < DEPTH_2 - 1
        mx = (sc_x @ ada_w[l] + ada_b[l]).reshape(bsz, 6, 1, d)
        mc = (sc_c @ ada_w[l] + ada_b[l]).reshape(6, d)
        hx = modulate(rmsnorm(x, norm_g[l, 0]), mx[:, 0], mx[:, 1])
        hc = modulate(rmsnorm(ctx, norm_g[l, 0]), mc[0], mc[1])
        if l % 2 == 0:
            e = l // 2
            yx, yc = mixer_ab(hx, hc, ab_w_in[e], ab_w_out[e], ab_sink[e], diff_lambda[e],
                              diff_subln_g[e], lambda_init(l), tab_ab, ctx_out)
        else:
            o = l // 2
            yx, yc = mixer_mla(hx, hc, mla_w_in[o], mla_q_norm_g[o], mla_kv_norm_g[o],
                               mla_wq_b[o], mla_wkv_b[o], mla_w_out[o], tab_c, ctx_out)
        x = x + mx[:, 2] * rmsnorm(yx, norm_g[l, 1])
        hx = modulate(rmsnorm(x, norm_g[l, 2]), mx[:, 3], mx[:, 4])
        x = x + mx[:, 5] * rmsnorm(swiglu(hx, ffn_w13[l], ffn_w2[l]), norm_g[l, 3])
        if ctx_out:
            ctx = ctx + mc[2] * rmsnorm(yc, norm_g[l, 1])
            hc = modulate(rmsnorm(ctx, norm_g[l, 2]), mc[3], mc[4])
            ctx = ctx + mc[5] * rmsnorm(swiglu(hc, ffn_w13[l], ffn_w2[l]), norm_g[l, 3])
    return x


def setup_inputs(seed=0):
    out = dict(first_inputs(seed))
    for name, value in second_inputs(seed + 1).items():
        if name != "x":
            out[name + "_2"] = value
    return out


def reference(
    x, norm_mix_pre, norm_mix_post, norm_mlp_pre, norm_mlp_post, w_in, w_out, attn_rel_bias,
    hgrn_lb_logits, hgrn_norm, rwkv_mu, rwkv_w0, rwkv_w2, rwkv_a0, rwkv_a2, rwkv_g2, rwkv_k_k,
    rwkv_k_a, rwkv_r_k, rwkv_ln_w, rwkv_ln_b, lru_conv_w, lru_conv_b, lru_wa, lru_ba, lru_wx,
    lru_bx, lru_lambda, mlp_w1, mlp_w2, c_2, ctx_2, c_ctx_2, ada_w_2, ada_b_2, norm_g_2,
    ffn_w13_2, ffn_w2_2, ab_w_in_2, ab_w_out_2, ab_sink_2, diff_lambda_2, diff_subln_g_2,
    mla_w_in_2, mla_q_norm_g_2, mla_kv_norm_g_2, mla_wq_b_2, mla_wkv_b_2, mla_w_out_2,
):
    x = first_block(
        x, norm_mix_pre, norm_mix_post, norm_mlp_pre, norm_mlp_post, w_in, w_out, attn_rel_bias,
        hgrn_lb_logits, hgrn_norm, rwkv_mu, rwkv_w0, rwkv_w2, rwkv_a0, rwkv_a2, rwkv_g2,
        rwkv_k_k, rwkv_k_a, rwkv_r_k, rwkv_ln_w, rwkv_ln_b, lru_conv_w, lru_conv_b, lru_wa,
        lru_ba, lru_wx, lru_bx, lru_lambda, mlp_w1, mlp_w2,
    )
    return second_block(
        x, c_2, ctx_2, c_ctx_2, ada_w_2, ada_b_2, norm_g_2, ffn_w13_2, ffn_w2_2, ab_w_in_2,
        ab_w_out_2, ab_sink_2, diff_lambda_2, diff_subln_g_2, mla_w_in_2, mla_q_norm_g_2,
        mla_kv_norm_g_2, mla_wq_b_2, mla_wkv_b_2, mla_w_out_2,
    )


_drawn_inputs = setup_inputs


def setup_inputs(seed=0):
    import zlib

    import numpy as np

    out = dict(_drawn_inputs(seed))
    spreads = {}
    factors = {'attn_rel_bias': 2.755,
     'rwkv_w2': 4.484,
     'rwkv_a0': 2.77,
     'rwkv_ln_b': 5.811,
     'lru_ba': 43.018,
     'lru_bx': 26.759,
     'ada_b_2': 3.646,
     'ab_sink_2': 64.0,
     'diff_lambda_2': 6.521,
     'diff_subln_g_2': 24.265,
     'mla_q_norm_g_2': 8.0,
     'mla_kv_norm_g_2': 5.154}
    for name, (base, spread) in spreads.items():
        noise = np.random.default_rng([zlib.crc32(name.encode()), seed]).standard_normal(out[name].shape)
        drawn = base * np.exp(spread * noise) if base else spread * noise
        out[name] = jnp.asarray(drawn.astype(out[name].dtype))
    for name, factor in factors.items():
        out[name] = (out[name] * factor).astype(out[name].dtype)
    return out
```

```python
from contextlib import ExitStack, contextmanager

import numpy as np

import concourse.bass as bass
from concourse import mybir

F32 = mybir.dt.float32
ALU = mybir.AluOpType
ACT = mybir.ActivationFunctionType
AX = mybir.AxisListType

P = 128
BANK = 512
D = 1024
KD = D // P
SEQ = 512
CTX = 256
ALL = SEQ + CTX
NX = SEQ // P
NC_ = CTX // P
GW = 256
HD = 64
CH = 64
NCH = SEQ // CH
MLP = 4 * D
FFN = 2816
EPS = 1e-6
NEG = -1e30
REL = 256
THETA = 10000.0
GRID = 64

CONSTS = {}


def _columns():
    at = 0
    for name, n in [("ident", P), ("upper", P), ("lower", P), ("upper_eq", P), ("blk16", P),
                    ("lvl32", P), ("lvl64", P), ("stack", HD), ("anti", P), ("ones64", P),
                    ("keep_before", P), ("keep_after", P), ("rot64", P), ("rot32", P),
                    ("cos64", SEQ), ("sin64", SEQ), ("cos32", SEQ), ("sin32", SEQ),
                    ("restart", SEQ), ("diag", 2 * P)]:
        CONSTS[name] = (at, n)
        at += n
    return at


N_CONST = _columns()


def shape_constants():
    c = np.zeros((P, N_CONST), np.float32)

    def put(name, a):
        at, n = CONSTS[name]
        c[:a.shape[0], at:at + n] = a

    i, j = np.arange(P)[:, None], np.arange(P)[None, :]
    same = (i // HD) == (j // HD)
    put("ident", np.eye(P))
    put("upper", same & (i < j))
    put("lower", same & (i > j))
    put("upper_eq", same & (i <= j))
    put("blk16", i // 16 == j // 16)
    put("lvl32", (i // 32 == j // 32) & (i // 16 != j // 16))
    put("lvl64", (i // 64 == j // 64) & (i // 32 != j // 32))
    put("stack", np.eye(HD)[np.arange(P) % HD])
    put("anti", np.eye(P)[::-1])
    put("ones64", same)
    put("keep_before", np.where(j >= i, 0.0, NEG))
    put("keep_after", np.where(j <= i, 0.0, NEG))

    def rotation(dim, first, reps):
        q = dim // 4
        r = np.zeros((P, P), np.float32)
        cos, sin = np.zeros((P, SEQ)), np.zeros((P, SEQ))
        inv = THETA ** (-np.arange(0, dim // 2, 2, dtype=np.float32) / np.float32(dim // 2))
        inv = inv.astype(np.float32)
        t = np.arange(SEQ)
        for rep in range(reps):
            for axis, pos in enumerate((t // GRID, t % GRID)):
                for k in range(q):
                    a = first + rep * dim + axis * 2 * q + k
                    ang = (pos.astype(np.float32) * inv[k]).astype(np.float32)
                    r[a + q, a] = -1.0
                    r[a, a + q] = 1.0
                    for m in (a, a + q):
                        cos[m], sin[m] = np.cos(ang), np.sin(ang)
        return r, cos, sin

    r, cos, sin = rotation(64, 0, 2)
    put("rot64", r)
    put("cos64", cos)
    put("sin64", sin)
    r, cos, sin = rotation(32, 64, 1)
    put("rot32", r)
    put("cos32", cos)
    put("sin32", sin)
    put("restart", np.broadcast_to(np.arange(SEQ) % CH != 0, (P, SEQ)))
    z = np.zeros((P, 2 * P))
    z[:HD, HD] = 1.0
    z[HD:, 2 * HD] = 1.0
    put("diag", z)
    return c


VECTORS = [("norm_mix_pre", 8), ("norm_mlp_pre", 8), ("hgrn_norm", 2), ("rwkv_mu", 7), ("rwkv_w0", 2),
           ("rwkv_a0", 2), ("rwkv_k_k", 2), ("rwkv_k_a", 2), ("rwkv_r_k", 2), ("lru_conv_w", 8),
           ("lru_conv_b", 2), ("lru_ba", 2), ("lru_bx", 2), ("lru_lambda", 2), ("c_2", 8),
           ("c_ctx_2", 8), ("norm_g_2", 64), ("ada_b_2", 96), ("mla_q_norm_g_2", 3),
           ("mla_kv_norm_g_2", 2)]
VEC_AT = {}
_at = 0
for _n, _r in VECTORS:
    VEC_AT[_n] = _at
    _at += _r
N_VEC = _at


class Link:

    def __init__(self, sem):
        self.sem, self.n = sem, 0

    def on(self, eng):
        self.eng = eng
        return self

    def __call__(self, ins):
        self.n += 1
        ins.then_inc(self.sem, 1)
        self.eng.wait_ge(self.sem, self.n)


class Core:

    def __init__(self, nc, stack, dram):
        self.nc, self.dram = nc, dram
        self.act_link = Link(stack.enter_context(nc.semaphore("act_link")))
        self.dve_link = Link(stack.enter_context(nc.semaphore("dve_link")))
        self.ended = 0
        self.cleared = []

    @contextmanager
    def block(self):
        with self.nc.Block() as block:
            yield block
        self.ended += 1

    def reusable(self):
        for i, (number, when) in enumerate(self.cleared):
            if self.ended > when:
                return self.cleared.pop(i)[0]
        return None


class Stage:

    def __init__(self, core, name):
        self.core, self.nc, self.name, self.stack = core, core.nc, name, ExitStack()
        self.sems = []

    def __enter__(self):
        self.stack.__enter__()
        return self

    def __exit__(self, *a):
        for s in self.sems:
            self.nc.gpsimd.sem_clear(s)
            self.core.cleared.append((s.num, self.core.ended))
        return self.stack.__exit__(*a)

    def sb(self, name, shape, dt=F32):
        return self.stack.enter_context(self.nc.sbuf_tensor(f"{self.name}_{name}", shape, dt))

    def banks(self, n):
        return [self.stack.enter_context(self.nc.psum_tensor(f"{self.name}_bank{i}", [P, BANK], F32))
                for i in range(n)]

    def sem(self, name):
        num = self.core.reusable()
        s = self.stack.enter_context(self.nc.semaphore(f"{self.name}_{name}", num=num))
        self.sems.append(s)
        return s


def const(core, name):
    at, n = CONSTS[name]
    return core.dram["consts"][:, at:at + n]


def load(core, name, pairs):
    nc = core.nc
    with Stage(core, name) as st, core.block() as block:
        loaded = st.sem("loaded")

        @block.sync
        def _(sp):
            for dst, src in pairs:
                sp.dma_start(dst, src).then_inc(loaded, 16)
            sp.wait_ge(loaded, 16 * len(pairs))


def turn(core, name, groups, ident):
    nc = core.nc
    with Stage(core, name) as st:
        banks = st.banks(8)
        turned, written = st.sem("turned"), st.sem("written")
        with core.block() as block:
            @block.tensor
            def _(pe):
                for g, (blocks, out, scale) in enumerate(groups):
                    if g >= 8:
                        pe.wait_ge(written, g - 7)
                    for b, src in enumerate(blocks):
                        rows = src.shape[0]
                        cols = src.shape[1]
                        last = nc.tensor.transpose(banks[g % 8][0:cols, b * P:b * P + rows], src,
                                                   ident[0:rows, 0:rows])
                    last.then_inc(turned, 1)

            @block.vector
            def _(dve):
                for g, (blocks, out, scale) in enumerate(groups):
                    rows, n, cols = out.shape
                    dve.wait_ge(turned, g + 1)
                    src = banks[g % 8][:, 0:n * P].rearrange("p (b c) -> p b c", b=n)
                    src = src[out.start_partition():out.start_partition() + rows, :, 0:cols]
                    if scale is None:
                        nc.vector.tensor_copy(out, src).then_inc(written, 1)
                    else:
                        nc.vector.tensor_tensor(out, src, scale.to_broadcast([rows, n, cols]),
                                                ALU.mult).then_inc(written, 1)


def invert_mean(core, link, total, width, eps=EPS):
    link(core.nc.vector.tensor_scalar(total, total, 1.0 / width, eps, ALU.mult, ALU.add))
    return core.nc.vector.reciprocal(total, total)


def norm_to_features(core, name, jobs, ident):
    nc = core.nc
    with Stage(core, name) as st:
        width = jobs[0][0].shape[1]
        kt = width // P
        half = (kt + 1) // 2 if kt > 4 else kt
        banks = st.banks(8)
        squares = st.sb("squares", [P, 2, width])
        total = st.sb("total", [P, len(jobs)])
        rstd = st.sb("rstd", [P, len(jobs)])
        xn = st.sb("xn", [P, 2, width])
        summed, rooted, scaled = st.sem("summed"), st.sem("rooted"), st.sem("scaled")
        inverted = st.sem("inverted")
        turned, written = st.sem("turned"), st.sem("written")
        parts = [(k0, min(k0 + 4, kt)) for k0 in range(0, kt, 4)]
        with core.block() as block:
            @block.scalar
            def _(act):
                for t, (src, dst, gain, shift) in enumerate(jobs):
                    if t >= 2:
                        act.wait_ge(summed, t - 1)
                    nc.scalar.activation(squares[:, t % 2, :], src, ACT.Square,
                                         accum_out=total[:, t:t + 1]).then_inc(summed, 1)
                act.wait_ge(inverted, 1)
                nc.scalar.activation(rstd[:, :], total[:, :], ACT.Sqrt).then_inc(rooted, 1)

            def normalise(dve, t):
                if t >= 2:
                    dve.wait_ge(turned, len(parts) * (t - 1))
                nc.vector.tensor_scalar(xn[:, t % 2, :], jobs[t][0], rstd[:, t:t + 1],
                                        None, ALU.mult).then_inc(scaled, 1)

            @block.vector
            def _(dve):
                link = core.dve_link.on(dve)
                dve.wait_ge(summed, len(jobs))
                invert_mean(core, link, total[:, :], width).then_inc(inverted, 1)
                dve.wait_ge(rooted, 1)
                normalise(dve, 0)
                for t, (src, dst, gain, shift) in enumerate(jobs):
                    if t + 1 < len(jobs):
                        normalise(dve, t + 1)
                    for q, (k0, k1) in enumerate(parts):
                        n = len(parts) * t + q
                        dve.wait_ge(turned, n + 1)
                        ps = banks[n % 8][:, 0:(k1 - k0) * P].rearrange("p (b c) -> p b c", c=P)
                        out = dst[:, k0:k1, :]
                        ins = nc.vector.tensor_tensor(
                            out, ps, gain[:, k0:k1].unsqueeze(2).to_broadcast([P, k1 - k0, P]),
                            ALU.mult)
                        if shift is not None:
                            link(ins)
                            ins = nc.vector.tensor_tensor(
                                out, out, shift[:, k0:k1].unsqueeze(2).to_broadcast([P, k1 - k0, P]),
                                ALU.add)
                        ins.then_inc(written, 1)

            @block.tensor
            def _(pe):
                for t in range(len(jobs)):
                    pe.wait_ge(scaled, t + 1)
                    for q, (k0, k1) in enumerate(parts):
                        n = len(parts) * t + q
                        if n >= 8:
                            pe.wait_ge(written, n - 7)
                        for k in range(k0, k1):
                            last = nc.tensor.transpose(banks[n % 8][:, (k - k0) * P:(k - k0 + 1) * P],
                                                       xn[:, t % 2, k * P:(k + 1) * P], ident[:, :])
                        last.then_inc(turned, 1)


def add_normed(core, name, jobs):
    nc = core.nc
    with Stage(core, name) as st:
        squares = st.sb("squares", [P, 2, D])
        scaled_y = st.sb("scaled_y", [P, 2, D])
        total = st.sb("total", [P, len(jobs)])
        rstd = st.sb("rstd", [P, len(jobs)])
        summed, inverted, rooted = st.sem("summed"), st.sem("inverted"), st.sem("rooted")
        with core.block() as block:
            @block.scalar
            def _(act):
                for t, (y, x, row) in enumerate(jobs):
                    if t >= 2:
                        act.wait_ge(summed, t - 1)
                    nc.scalar.activation(squares[:, t % 2, :], y, ACT.Square,
                                         accum_out=total[:, t:t + 1]).then_inc(summed, 1)
                act.wait_ge(inverted, 1)
                nc.scalar.activation(rstd[:, :], total[:, :], ACT.Sqrt).then_inc(rooted, 1)

            @block.vector
            def _(dve):
                link = core.dve_link.on(dve)
                dve.wait_ge(summed, len(jobs))
                invert_mean(core, link, total[:, :], D).then_inc(inverted, 1)
                dve.wait_ge(rooted, 1)
                for t, (y, x, row) in enumerate(jobs):
                    link(nc.vector.scalar_tensor_tensor(scaled_y[:, t % 2, :], y, rstd[:, t:t + 1],
                                                        row, ALU.mult, ALU.mult))
                    link(nc.vector.tensor_tensor(x, x, scaled_y[:, t % 2, :], ALU.add))


W_SLOTS = 3


def linear(core, name, weight, srcs, form, finish, col0=0, cols=None, width=BANK, engine="act",
           out_tile=P):
    nc = core.nc
    K, N = weight.shape
    cols = N - col0 if cols is None else cols
    KT = K // P
    kchunk = 8
    chunks = []
    for n0 in range(0, cols, width):
        for k0 in range(0, KT, kchunk):
            chunks.append((n0, min(width, cols - n0), k0, min(k0 + kchunk, KT)))

    def tiles(n0, w):
        if form == "features":
            return [(s, n0 // out_tile + j, n0 + j * out_tile, min(out_tile, w - j * out_tile))
                    for j in range((w + out_tile - 1) // out_tile) for s in range(len(srcs))]
        return [(s, t, n0, w) for s, src in enumerate(srcs) for t in range(src.shape[2] // P)]

    wk = weight.rearrange("(k p) n -> p k n", p=P)
    with Stage(core, name) as st:
        banks = st.banks(8)
        ring = st.sb("ring", [P, W_SLOTS, min(kchunk, KT), width])
        loaded = [st.sem(f"loaded{i}") for i in range(W_SLOTS)]
        used, ready, free = st.sem("used"), st.sem("ready"), st.sem("free")
        after, n_ready, n_used = [], 0, 0
        for n0, w, k0, k1 in chunks:
            if k1 == KT:
                n_ready += len(tiles(n0, w))
                after.append((ready, n_ready))
            else:
                n_used += 1
                after.append((used, n_used))
        with core.block() as block:
            @block.sync
            def _(sp):
                for i, (n0, w, k0, k1) in enumerate(chunks):
                    if i >= W_SLOTS:
                        sp.wait_ge(*after[i - W_SLOTS])
                    sp.dma_start(ring[:, i % W_SLOTS, 0:k1 - k0, 0:w],
                                 wk[:, k0:k1, col0 + n0:col0 + n0 + w]).then_inc(loaded[i % W_SLOTS], 16)

            @block.tensor
            def _(pe):
                first = 0
                for i, (n0, w, k0, k1) in enumerate(chunks):
                    pe.wait_ge(loaded[i % W_SLOTS], 16 * (i // W_SLOTS + 1))
                    for j, (s, t, c, cw) in enumerate(tiles(n0, w)):
                        g = first + j
                        if k0 == 0 and g >= 8:
                            pe.wait_ge(free, g - 7)
                        for k in range(k0, k1):
                            wt = ring[:, i % W_SLOTS, k - k0, c - n0:c - n0 + cw]
                            if form == "features":
                                out, lhsT, rhs = (banks[g % 8][0:cw, 0:srcs[s].shape[2]], wt,
                                                  srcs[s][:, k, :])
                            else:
                                out, lhsT, rhs = (banks[g % 8][:, 0:cw],
                                                  srcs[s][:, k, t * P:(t + 1) * P], wt)
                            last = nc.tensor.matmul(out, lhsT=lhsT, rhs=rhs, start=(k == 0),
                                                    stop=(k == KT - 1))
                        if k1 == KT:
                            last.then_inc(ready, 1)
                    if k1 == KT:
                        first += len(tiles(n0, w))
                    else:
                        last.then_inc(used, 1)

            def write_out(eng):
                g = 0
                for n0, w, k0, k1 in chunks:
                    if k1 < KT:
                        continue
                    for s, t, c, cw in tiles(n0, w):
                        eng.wait_ge(ready, g + 1)
                        if form == "features":
                            ps = banks[g % 8][0:cw, 0:srcs[s].shape[2]]
                        else:
                            ps = banks[g % 8][:, 0:cw]
                        finish(eng, ps, s, t, c, cw).then_inc(free, 1)
                        g += 1

            if engine == "act":
                @block.scalar
                def _(act):
                    write_out(act)
            else:
                @block.vector
                def _(dve):
                    write_out(dve)


def gated_up(core, name, w13, srcs, dsts):
    nc = core.nc
    width = 256
    n_chunks = FFN // width
    wk = w13.rearrange("(k p) n -> p k n", p=P)
    ns = len(srcs)
    pairs = [(c, j, s) for c in range(n_chunks) for j in range(width // P) for s in range(ns)]
    per = width // P * ns
    with Stage(core, name) as st:
        banks = st.banks(8)
        ring = st.sb("ring", [P, W_SLOTS, 2, KD, width])
        gate = st.sb("gate", [P, 2, SEQ])
        loaded = [st.sem(f"loaded{i}") for i in range(W_SLOTS)]
        ready, silu_done, free = st.sem("ready"), st.sem("silu_done"), st.sem("free")
        with core.block() as block:
            @block.sync
            def _(sp):
                for c in range(n_chunks):
                    if c >= W_SLOTS:
                        sp.wait_ge(ready, per * (c - W_SLOTS + 1))
                    for h in range(2):
                        sp.dma_start(ring[:, c % W_SLOTS, h],
                                     wk[:, :, h * FFN + c * width:h * FFN + (c + 1) * width])\
                          .then_inc(loaded[c % W_SLOTS], 16)

            @block.tensor
            def _(pe):
                for p, (c, j, s) in enumerate(pairs):
                    if p % per == 0:
                        pe.wait_ge(loaded[c % W_SLOTS], 32 * (c // W_SLOTS + 1))
                    if p >= 4:
                        pe.wait_ge(free, p - 3)
                    for h in range(2):
                        for k in range(KD):
                            last = nc.tensor.matmul(banks[(2 * p + h) % 8][:, 0:srcs[s].shape[2]],
                                                    lhsT=ring[:, c % W_SLOTS, h, k, j * P:(j + 1) * P],
                                                    rhs=srcs[s][:, k, :], start=(k == 0),
                                                    stop=(k == KD - 1))
                    last.then_inc(ready, 1)

            @block.scalar
            def _(act):
                for p, (c, j, s) in enumerate(pairs):
                    act.wait_ge(ready, p + 1)
                    if p >= 2:
                        act.wait_ge(free, p - 1)
                    n = srcs[s].shape[2]
                    nc.scalar.activation(gate[:, p % 2, 0:n], banks[2 * p % 8][:, 0:n], ACT.Silu)\
                      .then_inc(silu_done, 1)

            @block.vector
            def _(dve):
                for p, (c, j, s) in enumerate(pairs):
                    dve.wait_ge(silu_done, p + 1)
                    n = srcs[s].shape[2]
                    nc.vector.tensor_tensor(dsts[s][:, c * (width // P) + j, :], gate[:, p % 2, 0:n],
                                            banks[(2 * p + 1) % 8][:, 0:n], ALU.mult).then_inc(free, 1)


def attend(core, name, jobs, ident):
    nc = core.nc
    NS = 4
    with Stage(core, name) as st:
        wide = [st.stack.enter_context(nc.psum_tensor(f"{name}_scores{b}", [P, 2 * BANK], F32))
                for b in range(2)]
        flip = st.stack.enter_context(nc.psum_tensor(f"{name}_flip", [P, 2 * BANK], F32))
        obank = [st.stack.enter_context(nc.psum_tensor(f"{name}_o{b}", [P, BANK], F32))
                 for b in range(2)]
        E = st.sb("E", [P, 2, ALL])
        ET = st.sb("ET", [P, 2, ALL])
        top = st.sb("top", [P, NS])
        ntop = st.sb("ntop", [P, NS])
        den = st.sb("den", [P, NS])
        esink = st.sb("esink", [P, NS])
        inv = st.sb("inv", [P, NS])
        scores_ready, max_ready, exp_done = st.sem("scores"), st.sem("max"), st.sem("exp")
        turned, copied, pv_done, out_done = (st.sem("turned"), st.sem("copied"), st.sem("pv"),
                                             st.sem("out"))
        N = len(jobs)

        def n_keys(i):
            return P * len(jobs[i]["values"])

        with core.block() as block:
            @block.tensor
            def _(pe):
                def scores(i):
                    job, S = jobs[i], wide[i % 2]
                    if i >= 2:
                        pe.wait_ge(exp_done, i - 1)
                    pieces, at = [], 0
                    for key in job["keys"]:
                        n, done = key.shape[1], 0
                        while done < n:
                            m = min(n - done, BANK - at % BANK)
                            pieces.append((at, m, job["q"], key[:, done:done + m]))
                            at, done = at + m, done + m
                    extra = [(c, r.shape[1], l, r) for c, l, r in job["bias"]]
                    for b in range(2):
                        mine = [x for x in pieces + extra if x[0] // BANK == b]
                        for x, (c, m, l, r) in enumerate(mine):
                            last = nc.tensor.matmul(S[:, c:c + m], lhsT=l, rhs=r, start=(x == 0),
                                                    stop=(x == len(mine) - 1), skip_group_check=True)
                    last.then_inc(scores_ready, 1)

                def turn_probs(i):
                    pe.wait_ge(exp_done, i + 1)
                    if i >= 1:
                        pe.wait_ge(copied, i)
                    for b in range(n_keys(i) // P):
                        last = nc.tensor.transpose(flip[:, b * P:(b + 1) * P],
                                                   E[:, i % 2, b * P:(b + 1) * P], ident[:, :])
                    last.then_inc(turned, 1)

                def weigh(i):
                    pe.wait_ge(copied, i + 1)
                    if i >= 2:
                        pe.wait_ge(out_done, i - 1)
                    values = jobs[i]["values"]
                    for b, v in enumerate(values):
                        last = nc.tensor.matmul(obank[i % 2][:, 0:v.shape[1]],
                                                lhsT=ET[:, i % 2, b * P:(b + 1) * P], rhs=v,
                                                start=(b == 0), stop=(b == len(values) - 1))
                    last.then_inc(pv_done, 1)

                for i in range(N + 2):
                    if i < N:
                        scores(i)
                    if 1 <= i <= N:
                        turn_probs(i - 1)
                    if i >= 2:
                        weigh(i - 2)

            @block.vector
            def _(dve):
                link = core.dve_link.on(dve)

                def maximum(i):
                    job, s = jobs[i], i % NS
                    dve.wait_ge(scores_ready, i + 1)
                    if job["hide"]:
                        rows, c0, c1 = job["hide"]
                        link(nc.vector.memset(wide[i % 2][rows[0]:rows[1], c0:c1], NEG))
                    link(nc.vector.reduce_max(top[:, s:s + 1], wide[i % 2][:, 0:n_keys(i)], AX.X))
                    if job["sink"] is None:
                        ins = nc.vector.tensor_scalar(ntop[:, s:s + 1], top[:, s:s + 1], -job["scale"],
                                                      None, ALU.mult)
                    else:
                        ins = nc.vector.tensor_scalar(ntop[:, s:s + 1], top[:, s:s + 1], -job["scale"],
                                                      job["sink"], ALU.mult, ALU.min)
                    ins.then_inc(max_ready, 1)

                def copy(i):
                    dve.wait_ge(turned, i + 1)
                    if i >= 2:
                        dve.wait_ge(pv_done, i - 1)
                    nc.vector.tensor_copy(ET[:, i % 2, 0:n_keys(i)], flip[:, 0:n_keys(i)])\
                      .then_inc(copied, 1)

                def result(i):
                    job, s = jobs[i], i % NS
                    o = obank[i % 2][:, 0:job["out"].shape[1]]
                    if job["sink"] is not None:
                        link(nc.vector.tensor_tensor(den[:, s:s + 1], den[:, s:s + 1],
                                                     esink[:, s:s + 1], ALU.add))
                    link(nc.vector.reciprocal(inv[:, s:s + 1], den[:, s:s + 1]))
                    dve.wait_ge(pv_done, i + 1)
                    if job["minus"] is None:
                        nc.vector.tensor_scalar(job["out"], o, inv[:, s:s + 1], None, ALU.mult)\
                          .then_inc(out_done, 1)
                    else:
                        lam, base = job["minus"]
                        link(nc.vector.tensor_scalar(inv[:, s:s + 1], inv[:, s:s + 1], lam, -1.0,
                                                     ALU.mult, ALU.mult))
                        dve.wait_ge(out_done, i)
                        nc.vector.scalar_tensor_tensor(job["out"], o, inv[:, s:s + 1], base, ALU.mult,
                                                       ALU.add).then_inc(out_done, 1)

                for i in range(N + 2):
                    if i < N:
                        maximum(i)
                    if 1 <= i <= N:
                        copy(i - 1)
                    if i >= 2:
                        result(i - 2)

            @block.scalar
            def _(act):
                for i, job in enumerate(jobs):
                    s = i % NS
                    act.wait_ge(max_ready, i + 1)
                    if i >= 2:
                        act.wait_ge(turned, i - 1)
                    if i >= NS:
                        act.wait_ge(out_done, i - NS + 1)
                    if job["sink"] is not None:
                        nc.scalar.activation(esink[:, s:s + 1], job["sink"], ACT.Exp,
                                             bias=ntop[:, s:s + 1], scale=-1.0)
                    nc.scalar.activation(E[:, i % 2, 0:n_keys(i)], wide[i % 2][:, 0:n_keys(i)], ACT.Exp,
                                         bias=ntop[:, s:s + 1], scale=job["scale"],
                                         accum_out=den[:, s:s + 1]).then_inc(exp_done, 1)


def copy_out(nc, dst):
    def finish(eng, ps, s, t, c, cw):
        return nc.scalar.activation(dst(s, t, c, cw), ps, ACT.Copy)
    return finish


T_QA, T_KA, T_VA = 0, 2, 4
T_QB, T_FB, T_IB, T_GB = 6, 8, 10, 12
T_RWKV = 14
T_XD, T_GD = 21, 23
N_PROJ = 25


def chunk_attention(core, proj, mix, ident):
    nc, dram = core.nc, core.dram
    heads = GW // HD
    EXT = 2 * SEQ
    NB = SEQ // P
    with Stage(core, "ca") as st:
        v_tok = st.sb("v_tok", [P, NX, GW])
        out_tok = st.sb("out_tok", [P, NX, GW])
        ext = st.sb("ext", [heads, EXT])
        hankel = st.sb("hankel", [P, heads, NB, P])
        anti = st.sb("anti", [P, P])
        q8 = st.sb("q8", [P, 2, SEQ])
        loaded, filled, stored = st.sem("loaded"), st.sem("filled"), st.sem("stored")
        with core.block() as block:
            @block.sync
            def _(sp):
                sp.dma_start(ext[:, SEQ - REL - 1:SEQ + REL],
                             dram["attn_rel_bias"][0]).then_inc(loaded, 16)
                sp.dma_start(anti[:, :], const(core, "anti")).then_inc(loaded, 16)
                sp.wait_ge(filled, 1)
                sp.dma_start(dram["bias_ext"][:, :], ext[:, :]).then_inc(stored, 16)
                sp.wait_ge(stored, 16)
                for h in range(heads):
                    for b in range(NB):
                        at = SEQ - P - P * b
                        src = bass.AP(dram["bias_ext"].tensor, h * EXT + at, [[1, P], [1, P]])
                        sp.dma_start(hankel[:, h, b, :], src).then_inc(loaded, 16)
                sp.wait_ge(loaded, 16 * (2 + heads * NB))

            @block.vector
            def _(dve):
                dve.wait_ge(loaded, 32)
                n = SEQ - REL - 1
                nc.vector.tensor_copy(ext[:, 0:n], ext[:, n:n + 1].to_broadcast([heads, n]))
                n = SEQ + REL
                nc.vector.tensor_copy(ext[:, n:EXT],
                                      ext[:, n - 1:n].to_broadcast([heads, EXT - n])).then_inc(filled, 1)
                nc.vector.tensor_scalar(q8[:, :, :], proj[:, T_QA:T_QA + 2, :], HD ** -0.5, None, ALU.mult)
        turn(core, "ca_v", [([proj[:, T_VA + a, t * P:(t + 1) * P] for a in range(2)],
                             v_tok[:, t, :].rearrange("p (a c) -> p a c", a=2), None)
                            for t in range(NX)], ident)
        jobs = []
        for h in range(heads):
            rows = slice(HD * (h % 2), HD * (h % 2) + HD)
            for t in range(NX):
                jobs.append(dict(
                    q=q8[rows, h // 2, t * P:(t + 1) * P],
                    keys=[proj[rows, T_KA + h // 2, 0:(t + 1) * P]],
                    bias=[(kb * P, anti[:, :], hankel[:, h, t - kb, :]) for kb in range(t + 1)],
                    hide=((0, CH), t * P + CH, (t + 1) * P),
                    values=[v_tok[:, kb, h * HD:(h + 1) * HD] for kb in range(t + 1)],
                    scale=1.0, sink=None, out=out_tok[:, t, h * HD:(h + 1) * HD], minus=None))
        attend(core, "ca_at", jobs, ident)
        turn(core, "ca_o", [([out_tok[:, t, a * P:(a + 1) * P] for a in range(2)],
                             mix[:, 0:2, t * P:(t + 1) * P], None) for t in range(NX)], ident)


def hgrn(core, proj, mix, vec, ident):
    nc = core.nc
    with Stage(core, "hg") as st:
        banks = st.banks(4)
        f = st.sb("f", [P, 2, SEQ])
        key = st.sb("key", [P, 2, SEQ])
        q = st.sb("q", [P, 2, SEQ])
        spread = st.sb("spread", [P, HD, P])
        window = st.sb("window", [P, 2 * P])
        kv = st.sb("kv", [P, 2, SEQ])
        state = st.sb("state", [P, 2, SEQ])
        read = st.sb("read", [P, 2, SEQ])
        o = st.sb("o", [P, 2, SEQ])
        rstd = st.sb("rstd", [P, 2, SEQ])
        ones = st.sb("ones", [P, P])
        load(core, "hg_c", [(window[:, :], const(core, "diag")), (ones[:, :], const(core, "ones64"))])
        gated, built, prepared = st.sem("gated"), st.sem("built"), st.sem("prepared")
        value_ready, kv_done, read_done = st.sem("value_ready"), st.sem("kv_done"), st.sem("read_done")
        state_done, added = st.sem("state_done"), st.sem("added")
        squared, meaned, inverted, rooted = (st.sem("squared"), st.sem("meaned"), st.sem("inverted"),
                                           st.sem("rooted"))
        N = 2 * HD
        with core.block() as block:
            @block.scalar
            def _(act):
                nc.scalar.activation(f[:, :, :], proj[:, T_FB:T_FB + 2, :], ACT.Sigmoid)
                nc.scalar.activation(key[:, :, :], proj[:, T_FB:T_FB + 2, :], ACT.Sigmoid, scale=-1.0)
                nc.scalar.activation(q[:, :, :], proj[:, T_QB:T_QB + 2, :], ACT.Silu).then_inc(gated, 1)
                nc.scalar.activation(proj[:, T_GB:T_GB + 2, :], proj[:, T_GB:T_GB + 2, :],
                                     ACT.Silu).then_inc(gated, 1)
                for a in range(2):
                    act.wait_ge(inverted, a + 1)
                    nc.scalar.activation(rstd[:, a, :], rstd[:, a, :], ACT.Sqrt).then_inc(rooted, 1)

            @block.vector
            def _(dve):
                link = core.dve_link.on(dve)
                nc.vector.tensor_copy(
                    spread[:, :, :].rearrange("p v (h m) -> p v h m", h=2),
                    ident[:, :].rearrange("p (h v) -> p v h", h=2).unsqueeze(3)
                    .to_broadcast([P, HD, 2, HD])).then_inc(built, 1)
                dve.wait_ge(gated, 2)
                for n in range(N):
                    a = n // HD
                    dve.wait_ge(value_ready, n + 1)
                    if n >= 2:
                        dve.wait_ge(state_done, n - 1)
                    nc.vector.tensor_tensor(kv[:, n % 2, :], key[:, a, :], banks[n % 2][:, :],
                                            ALU.mult).then_inc(kv_done, 1)
                    dve.wait_ge(kv_done, n + 1)
                    if n >= 2:
                        dve.wait_ge(read_done, n - 1)
                    nc.vector.tensor_tensor_scan(state[:, n % 2, :], f[:, a, :], kv[:, n % 2, :], 0.0,
                                                 ALU.mult, ALU.add).then_inc(state_done, 1)
                dve.wait_ge(added, N)
                for a in range(2):
                    link(nc.vector.tensor_copy(o[:, a, :], banks[2 + a][:, :]))
                    nc.vector.tensor_tensor(kv[:, a, :], o[:, a, :], o[:, a, :], ALU.mult)\
                      .then_inc(squared, 1)
                for a in range(2):
                    dve.wait_ge(meaned, a + 1)
                    link(nc.vector.tensor_scalar(rstd[:, a, :], banks[a][:, :], 1.0 / HD, EPS, ALU.mult,
                                                 ALU.add))
                    nc.vector.reciprocal(rstd[:, a, :], rstd[:, a, :]).then_inc(inverted, 1)
                for a in range(2):
                    dve.wait_ge(rooted, a + 1)
                    col = VEC_AT["hgrn_norm"] + a
                    link(nc.vector.scalar_tensor_tensor(o[:, a, :], o[:, a, :], vec[:, col:col + 1],
                                                        rstd[:, a, :], ALU.mult, ALU.mult))
                    nc.vector.tensor_tensor(mix[:, 2 + a, :], o[:, a, :], proj[:, T_GB + a, :], ALU.mult)

            @block.gpsimd
            def _(pool):
                pool.wait_ge(gated, 1)
                for n in range(N):
                    pool.wait_ge(state_done, n + 1)
                    if n >= 2:
                        pool.wait_ge(added, n - 1)
                    nc.gpsimd.tensor_tensor(read[:, n % 2, :], q[:, n // HD, :], state[:, n % 2, :],
                                            ALU.mult).then_inc(read_done, 1)

            @block.tensor
            def _(pe):
                pe.wait_ge(built, 1)

                def spread_value(n):
                    if n >= 2:
                        pe.wait_ge(kv_done, n - 1)
                    nc.tensor.matmul(banks[n % 2][:, :], lhsT=spread[:, n % HD, :],
                                     rhs=proj[:, T_IB + n // HD, :], start=True, stop=True)\
                      .then_inc(value_ready, 1)

                spread_value(0)
                for n in range(N):
                    if n + 1 < N:
                        spread_value(n + 1)
                    pe.wait_ge(read_done, n + 1)
                    v = n % HD
                    nc.tensor.matmul(banks[2 + n // HD][:, :], lhsT=window[:, HD - v:HD - v + P],
                                     rhs=read[:, n % 2, :], start=(v == 0), stop=(v == HD - 1),
                                     skip_group_check=True).then_inc(added, 1)
                for a in range(2):
                    pe.wait_ge(squared, a + 1)
                    nc.tensor.matmul(banks[a][:, :], lhsT=ones[:, :], rhs=kv[:, a, :], start=True,
                                     stop=True).then_inc(meaned, 1)


def rglru(core, proj, mix, vec):
    nc, dram = core.nc, core.dram
    with Stage(core, "lru") as st:
        banks = st.banks(4)
        w = st.sb("w", [P, 2, 2, P])
        conv = st.sb("conv", [P, 2, SEQ])
        gates = st.sb("gates", [P, 2, 2, SEQ])
        la = st.sb("la", [P, 2, SEQ])
        a = st.sb("a", [P, 2, SEQ])
        e2 = st.sb("e2", [P, 2, SEQ])
        th = st.sb("th", [P, 2, SEQ])
        u = st.sb("u", [P, 2, SEQ])
        g = st.sb("g", [P, 2, SEQ])
        g3 = st.sb("g3", [P, 2, SEQ])
        sm = st.sb("sm", [P, 8, 2])
        cleared, loaded = st.sem("cleared"), st.sem("loaded")
        conv_done, gated, sigm, decayed = st.sem("conv"), st.sem("gated"), st.sem("sigm"), st.sem("decay")
        exped, lam_done, lam_exp, cubed, tanhed = (st.sem("exped"), st.sem("lam"), st.sem("lam_exp"),
                                                   st.sem("cubed"), st.sem("tanhed"))
        rooted, prod = st.sem("rooted"), st.sem("prod")

        def v(name, i=0, n=2):
            return vec[:, VEC_AT[name] + i:VEC_AT[name] + i + n]

        with core.block() as block:
            @block.sync
            def _(sp):
                sp.wait_ge(cleared, 1)
                for m, name in enumerate(("lru_wa", "lru_wx")):
                    for b in range(4):
                        r = HD * (b % 2)
                        sp.dma_start(w[r:r + HD, m, b // 2, r:r + HD], dram[name][0, b])\
                          .then_inc(loaded, 16)
                sp.wait_ge(loaded, 128)

            @block.tensor
            def _(pe):
                pe.wait_ge(loaded, 128)
                pe.wait_ge(conv_done, 1)
                for m in range(2):
                    for i in range(2):
                        nc.tensor.matmul(banks[2 * m + i][:, :], lhsT=w[:, m, i, :], rhs=conv[:, i, :],
                                         start=True, stop=True).then_inc(gated, 1)

            @block.scalar
            def _(act):
                link = core.act_link.on(act)
                act.wait_ge(lam_done, 1)
                nc.scalar.activation(sm[:, 1, :], sm[:, 0, :], ACT.Exp, scale=-1.0).then_inc(lam_exp, 1)
                for m, b in enumerate(("lru_ba", "lru_bx")):
                    for i in range(2):
                        act.wait_ge(gated, 2 * m + i + 1)
                        nc.scalar.activation(gates[:, m, i, :], banks[2 * m + i][:, :], ACT.Sigmoid,
                                             bias=v(b, i, 1)).then_inc(sigm, 1)
                act.wait_ge(decayed, 1)
                nc.scalar.activation(a[:, :, :], la[:, :, :], ACT.Exp)
                nc.scalar.activation(e2[:, :, :], la[:, :, :], ACT.Exp, scale=2.0)
                nc.scalar.activation(th[:, :, :], la[:, :, :], ACT.Tanh, scale=-1.0).then_inc(exped, 1)
                act.wait_ge(cubed, 1)
                nc.scalar.activation(g3[:, :, :], g3[:, :, :], ACT.Tanh, scale=(2.0 / np.pi) ** 0.5)\
                  .then_inc(tanhed, 1)
                act.wait_ge(prod, 1)
                nc.scalar.activation(e2[:, :, :], e2[:, :, :], ACT.Sqrt).then_inc(rooted, 1)

            @block.vector
            def _(dve):
                link = core.dve_link.on(dve)
                V = nc.vector
                V.memset(w[:, :, :, :], 0.0).then_inc(cleared, 1)
                link(V.tensor_scalar(sm[:, 6, :], v("lru_lambda"), -1.0, None, ALU.mult))
                V.tensor_tensor(sm[:, 0, :], sm[:, 6, :], v("lru_lambda"), ALU.max).then_inc(lam_done, 1)
                x = proj[:, T_XD:T_XD + 2, :]
                for i in range(2):
                    cw = [VEC_AT["lru_conv_w"] + 2 * j + i for j in range(4)]
                    link(V.tensor_scalar(conv[:, i, :], x[:, i, :], vec[:, cw[3]:cw[3] + 1],
                                         v("lru_conv_b", i, 1), ALU.mult, ALU.add))
                    for j in range(3):
                        s = 3 - j
                        link(V.scalar_tensor_tensor(conv[:, i, s:], x[:, i, 0:SEQ - s],
                                                    vec[:, cw[j]:cw[j] + 1], conv[:, i, s:], ALU.mult,
                                                    ALU.add))
                V.sem_inc(conv_done, 1)
                dve.wait_ge(lam_exp, 1)
                link(V.tensor_scalar(sm[:, 2, :], sm[:, 1, :], 2.0, None, ALU.add))
                link(V.reciprocal(sm[:, 2, :], sm[:, 2, :]))
                link(V.tensor_tensor(sm[:, 2, :], sm[:, 2, :], sm[:, 1, :], ALU.mult))
                link(V.tensor_tensor(sm[:, 3, :], sm[:, 2, :], sm[:, 2, :], ALU.mult))
                link(V.tensor_scalar(sm[:, 4, :], sm[:, 3, :], 2.0 / 15, 2.0 / 13, ALU.mult, ALU.add))
                for k in (11, 9, 7, 5, 3, 1):
                    link(V.tensor_tensor(sm[:, 4, :], sm[:, 4, :], sm[:, 3, :], ALU.mult))
                    link(V.tensor_scalar(sm[:, 4, :], sm[:, 4, :], 2.0 / k, None, ALU.add))
                link(V.tensor_tensor(sm[:, 4, :], sm[:, 4, :], sm[:, 2, :], ALU.mult))
                link(V.tensor_scalar(sm[:, 5, :], v("lru_lambda"), -1.0, 0.0, ALU.mult, ALU.max))
                link(V.tensor_tensor(sm[:, 5, :], sm[:, 5, :], sm[:, 4, :], ALU.add))
                link(V.tensor_scalar(sm[:, 5, :], sm[:, 5, :], -8.0, None, ALU.mult))
                dve.wait_ge(sigm, 4)
                for i in range(2):
                    link(V.tensor_scalar(la[:, i, :], gates[:, 0, i, :], sm[:, 5, i:i + 1], None, ALU.mult))
                V.sem_inc(decayed, 1)
                link(V.tensor_tensor(u[:, :, :], gates[:, 1], conv[:, :, :], ALU.mult))
                gd = proj[:, T_GD:T_GD + 2, :]
                link(V.tensor_tensor(g[:, :, :], gd, gd, ALU.mult))
                link(V.tensor_scalar(g[:, :, :], g[:, :, :], 0.044715, 1.0, ALU.mult, ALU.add))
                V.tensor_tensor(g3[:, :, :], g[:, :, :], gd, ALU.mult).then_inc(cubed, 1)
                dve.wait_ge(exped, 1)
                V.scalar_tensor_tensor(e2[:, :, :], e2[:, :, :], 1.0, th[:, :, :], ALU.add, ALU.mult)\
                 .then_inc(prod, 1)
                dve.wait_ge(tanhed, 1)
                link(V.scalar_tensor_tensor(g3[:, :, :], g3[:, :, :], 1.0, gd, ALU.add, ALU.mult))
                dve.wait_ge(rooted, 1)
                link(V.tensor_tensor(u[:, :, :], u[:, :, :], e2[:, :, :], ALU.mult))
                for i in range(2):
                    link(V.tensor_tensor_scan(g[:, i, :], a[:, i, :], u[:, i, :], 0.0, ALU.mult, ALU.add))
                V.scalar_tensor_tensor(mix[:, 6:8, :], g[:, :, :], 0.5, g3[:, :, :], ALU.mult, ALU.mult)


def rwkv(core, proj, mix, vec, ident):
    nc, dram = core.nc, core.dram
    xs = proj[:, T_RWKV:T_RWKV + 7, :]
    free = list(range(0, T_RWKV)) + list(range(T_XD, N_PROJ))

    def two(i):
        at = free[2 * i]
        assert free[2 * i + 1] == at + 1
        return proj[:, at:at + 2, :]

    gate, av, lw, cum, kk, km, ex, ei, en = (two(i) for i in range(9))

    def v(name, i=0, n=2):
        return vec[:, VEC_AT[name] + i:VEC_AT[name] + i + n]

    with Stage(core, "rp") as st:
        banks = st.banks(8)
        diff = st.sb("diff", [P, 7, SEQ])
        lora = st.sb("lora", [P, GW])
        low = st.sb("low", [P, SEQ])
        ones = st.sb("ones", [P, P])
        restart = st.sb("restart", [P, SEQ])
        load(core, "rp_c", [(lora[0:32, :], dram["rwkv_w2"][0]), (lora[32:64, :], dram["rwkv_a2"][0]),
                            (lora[64:128, :], dram["rwkv_g2"][0]), (ones[:, :], const(core, "ones64")),
                            (restart[:, :], const(core, "restart"))])
        shifted, low_done, lora_done, sigm, ssq, summed = (st.sem("shifted"), st.sem("low"),
                                                           st.sem("lora"), st.sem("sigm"),
                                                           st.sem("ssq"), st.sem("summed"))
        inverted, rooted, cum_done, exped = (st.sem("inverted"), st.sem("rooted"), st.sem("cum"),
                                            st.sem("exped"))
        with core.block() as block:
            @block.vector
            def _(dve):
                link = core.dve_link.on(dve)
                V = nc.vector
                link(V.tensor_tensor(diff[:, :, 1:], xs[:, :, 0:SEQ - 1], xs[:, :, 1:], ALU.subtract))
                link(V.tensor_scalar(diff[:, :, 0:1], xs[:, :, 0:1], -1.0, None, ALU.mult))
                link(V.tensor_tensor(diff[:, :, :], diff[:, :, :],
                                     v("rwkv_mu", 0, 7).unsqueeze(2).to_broadcast([P, 7, SEQ]), ALU.mult))
                V.tensor_tensor(xs, xs, diff[:, :, :], ALU.add).then_inc(shifted, 1)
                dve.wait_ge(shifted, 1)
                for i in range(2):
                    link(V.tensor_scalar(kk[:, i, :], xs[:, 2 + i, :], v("rwkv_k_k", i, 1), None, ALU.mult))
                    V.tensor_tensor(diff[:, i, :], kk[:, i, :], kk[:, i, :], ALU.mult).then_inc(ssq, 1)
                dve.wait_ge(sigm, 4)
                for i in range(2):
                    link(V.tensor_scalar(lw[:, i, :], lw[:, i, :], -float(np.exp(-0.5)), None, ALU.mult))
                    V.tensor_tensor_scan(cum[:, i, :], restart[:, :], lw[:, i, :], 0.0, ALU.mult, ALU.add)\
                     .then_inc(cum_done, 1)
                dve.wait_ge(cum_done, 2)
                V.tensor_tensor(diff[:, 4:6, :], cum, lw, ALU.subtract).then_inc(cum_done, 1)
                for i in range(2):
                    dve.wait_ge(summed, i + 1)
                    link(V.tensor_scalar(diff[:, 2 + i, :], banks[6 + i][:, :], 1e-24, None, ALU.max))
                    V.reciprocal(diff[:, 2 + i, :], diff[:, 2 + i, :]).then_inc(inverted, 1)
                for i in range(2):
                    link(V.tensor_scalar(km[:, i, :], av[:, i, :], 1.0, v("rwkv_k_a", i, 1), ALU.subtract,
                                         ALU.mult))
                    link(V.scalar_tensor_tensor(km[:, i, :], km[:, i, :], 1.0, xs[:, 2 + i, :], ALU.add,
                                                ALU.mult))
                dve.wait_ge(rooted, 2)
                link(V.tensor_tensor(kk, kk, diff[:, 2:4, :], ALU.mult))
                for i in range(2):
                    V.scalar_tensor_tensor(xs[:, 2 + i, :], km[:, i, :], v("rwkv_r_k", i, 1),
                                           xs[:, i, :], ALU.mult, ALU.mult)
                dve.wait_ge(exped, 3)
                link(V.tensor_tensor(av, av, kk, ALU.mult))
                link(V.tensor_tensor(av, av, en, ALU.mult))
                link(V.tensor_tensor(km, km, en, ALU.mult))
                link(V.scalar_tensor_tensor(kk, kk, -1.0, ex, ALU.mult, ALU.mult))
                link(V.tensor_tensor(xs[:, 0:2, :], xs[:, 0:2, :], ei, ALU.mult))

            @block.scalar
            def _(act):
                act.wait_ge(shifted, 1)
                nc.scalar.activation(low[0:32, :], xs[0:32, 6, :], ACT.Tanh)
                nc.scalar.activation(low[32:64, :], xs[32:64, 6, :], ACT.Copy)
                nc.scalar.activation(low[64:128, :], xs[64:128, 6, :], ACT.Sigmoid).then_inc(low_done, 1)
                for i in range(2):
                    act.wait_ge(lora_done, 1)
                    nc.scalar.activation(lw[:, i, :], banks[i][:, :], ACT.Sigmoid,
                                         bias=v("rwkv_w0", i, 1)).then_inc(sigm, 1)
                    nc.scalar.activation(av[:, i, :], banks[2 + i][:, :], ACT.Sigmoid,
                                         bias=v("rwkv_a0", i, 1)).then_inc(sigm, 1)
                    nc.scalar.activation(gate[:, i, :], banks[4 + i][:, :], ACT.Copy)
                act.wait_ge(cum_done, 3)
                nc.scalar.activation(ex, diff[:, 4:6, :], ACT.Exp).then_inc(exped, 1)
                nc.scalar.activation(ei, cum, ACT.Exp).then_inc(exped, 1)
                nc.scalar.activation(en, cum, ACT.Exp, scale=-1.0).then_inc(exped, 1)
                for i in range(2):
                    act.wait_ge(inverted, i + 1)
                    nc.scalar.activation(diff[:, 2 + i, :], diff[:, 2 + i, :], ACT.Sqrt).then_inc(rooted, 1)

            @block.tensor
            def _(pe):
                for i in range(2):
                    pe.wait_ge(ssq, i + 1)
                    nc.tensor.matmul(banks[6 + i][:, :], lhsT=ones[:, :], rhs=diff[:, i, :], start=True,
                                     stop=True).then_inc(summed, 1)
                pe.wait_ge(low_done, 1)
                for r0, r1, b in ((0, 32, 0), (32, 64, 2), (64, 128, 4)):
                    for i in range(2):
                        last = nc.tensor.matmul(banks[b + i][:, :], lhsT=lora[r0:r1, i * P:(i + 1) * P],
                                                rhs=low[r0:r1, :], start=True, stop=True)
                last.then_inc(lora_done, 1)
    alpha, beta, kbar, rbar, prod = kk, av, km, xs[:, 0:2, :], xs[:, 2:4, :]
    vals = xs[:, 4:6, :]
    for pair in range(2):
        rwkv_pair(core, pair, dict(alpha=alpha[:, pair], beta=beta[:, pair], kbar=kbar[:, pair],
                                   rbar=rbar[:, pair], prod=prod[:, pair], vals=vals[:, pair],
                                   total=ei[:, pair], gate=gate[:, pair]), mix[:, 4 + pair, :], ident)


def rwkv_pair(core, pair, f, out, ident):
    nc, dram = core.nc, core.dram
    HALF = NCH // 2
    with Stage(core, f"rk{pair}") as st:
        def mats(name, n=P):
            return st.sb(name, [P, NCH, n])

        Ab, Bb, Kb, Rb, Vb, Qb = (mats(n) for n in ("alpha", "beta", "kbar", "rbar", "vals", "prod"))
        A, AT, AkT, RbT, RkT = (mats(n) for n in ("A", "AT", "AkT", "RbT", "RkT"))
        X, XT, Y2, Y2T, C2 = (mats(n) for n in ("X", "XT", "Y2", "Y2T", "C2"))
        V = mats("V", HD)
        AkV, U0 = mats("AkV", HD), mats("U0", HD)
        G = mats("G", HD)
        S = st.sb("S", [P, NCH + 1, HD])
        cons = {}
        for n in ("upper", "lower", "upper_eq", "blk16", "lvl32", "lvl64", "stack"):
            cons[n] = st.sb("c_" + n, [P, CONSTS[n][1]])
        lnw, lnb = st.sb("lnw", [P, HD]), st.sb("lnb", [P, HD])
        ones_col = st.sb("ones_col", [P, 1])
        bonus = st.sb("bonus", [P, NCH])
        stats = st.sb("stats", [P, NCH, 6])
        mv = st.sb("mv", [P, NCH, 2])
        rs = st.sb("rs", [P, NCH])
        ln_rows = [(t[h * HD:(h + 1) * HD, :],
                    bass.AP(dram[n].tensor, pair * P + h * HD, [[0, HD], [1, HD]]))
                   for t, n in ((lnw, "rwkv_ln_w"), (lnb, "rwkv_ln_b")) for h in range(2)]
        load(core, f"rk{pair}_c", [(cons[n][:, :], const(core, n)) for n in cons] + ln_rows)
        with core.block() as block:
            @block.gpsimd
            def _(pool):
                for t in (Ab, Bb, Kb):
                    nc.gpsimd.memset(t[:, :, :], 0.0)

            @block.vector
            def _(dve):
                for t in (Rb, Vb, Qb):
                    nc.vector.memset(t[:, :, :], 0.0)
                nc.vector.memset(S[:, 0, :], 0.0)
                nc.vector.memset(ones_col[:, :], 1.0)
        with core.block() as block:
            @block.vector
            def _(dve):
                for h in range(2):
                    r = slice(h * HD, (h + 1) * HD)
                    for t, n in ((Ab, "alpha"), (Bb, "beta"), (Kb, "kbar")):
                        nc.vector.tensor_copy(t[r, :, r], f[n][r, :].rearrange("p (c t) -> p c t", c=NCH))

            @block.scalar
            def _(act):
                for h in range(2):
                    r = slice(h * HD, (h + 1) * HD)
                    for t, n in ((Rb, "rbar"), (Vb, "vals"), (Qb, "prod")):
                        nc.scalar.activation(t[r, :, r], f[n][r, :].rearrange("p (c t) -> p c t", c=NCH),
                                             ACT.Copy)
        I = ident
        eye = ident[:, :].unsqueeze(1).to_broadcast([P, HALF, P])

        def mask(n):
            return cons[n][:, :].unsqueeze(1).to_broadcast([P, HALF, P])

        MASK, ADD, COPY = "mask", "add", "copy"
        steps = [
            (Bb, Ab, MASK, "upper", AT), (Ab, Bb, MASK, "lower", A),
            (Kb, Ab, MASK, "upper", AkT), (Bb, Rb, MASK, "upper_eq", RbT),
            (Kb, Rb, MASK, "upper_eq", RkT),
            (Vb, cons["stack"], COPY, None, V),
        ]
        products(core, f"rk{pair}_a", steps, mask)
        D1, D1T, C1, C1T = Y2, Y2T, A, AT
        with core.block() as block:
            @block.vector
            def _(dve):
                link = core.dve_link.on(dve)
                full = [P, NCH, P]

                def m(n):
                    return cons[n][:, :].unsqueeze(1).to_broadcast(full)

                E = ident[:, :].unsqueeze(1).to_broadcast(full)
                for src, d, x in ((A, D1, X), (AT, D1T, XT)):
                    link(nc.vector.tensor_tensor(d[:, :, :], src[:, :, :], m("blk16"), ALU.mult))
                    link(nc.vector.tensor_tensor(x[:, :, :], d[:, :, :], E, ALU.add))
                link(nc.vector.tensor_tensor(C2[:, :, :], A[:, :, :], m("lvl64"), ALU.mult))
                link(nc.vector.tensor_tensor(A[:, :, :], A[:, :, :], m("lvl32"), ALU.mult))
                link(nc.vector.tensor_tensor(AT[:, :, :], AT[:, :, :], m("lvl32"), ALU.mult))
        Z, ZT = mats("Z"), mats("ZT")
        W, WT = Ab, mats("WT")
        steps = []
        d, dT, e, eT = D1, D1T, Z, ZT
        for _ in range(3):
            steps += [(dT, d, COPY, None, e), (d, dT, COPY, None, eT),
                      (XT, e, ADD, X, X), (e, XT, ADD, XT, XT)]
            d, dT, e, eT = e, eT, d, dT
        steps += [(C1T, X, COPY, None, d), (C1, XT, COPY, None, dT),
                  (XT, d, ADD, X, e), (X, dT, ADD, XT, eT),
                  (C2, eT, COPY, None, d), (e, d, ADD, eT, X)]
        TT = X
        At, Bt, Kt = d, dT, e
        steps += [(Ab, I, COPY, None, XT), (Bb, I, COPY, None, Y2T), (Kb, I, COPY, None, AT)]
        At, Bt, Kt = XT, Y2T, AT
        steps += [(AkT, V, COPY, None, AkV), (TT, AkV, COPY, None, U0),
                  (TT, At, COPY, None, W), (At, TT, COPY, None, WT),
                  (W, Bt, ADD, eye, AkT)]
        M1T = AkT
        products(core, f"rk{pair}_b", steps, mask)
        total = f["total"].rearrange("p (c t) -> p c t", c=NCH)[:, :, CH - 1:CH]
        banks_needed = 8
        with Stage(core, f"rk{pair}_s") as ss:
            banks = ss.banks(banks_needed)
            g_ready, g_done, m_ready, s_done = (ss.sem("g_ready"), ss.sem("g_done"), ss.sem("m_ready"),
                                                ss.sem("s_done"))
            u_ready, u_done, y_ready, b_ready = (ss.sem("u_ready"), ss.sem("u_done"), ss.sem("y_ready"),
                                                 ss.sem("b_ready"))
            norm, root, gain_done, turned = (ss.sem("norm"), ss.sem("root"), ss.sem("gain"),
                                             ss.sem("turned"))
            U, Yt = G, U0
            with core.block() as block:
                @block.tensor
                def _(pe):
                    T = nc.tensor
                    for c in range(NCH):
                        g = banks[0][:, c * HD:(c + 1) * HD]
                        T.matmul(g, lhsT=Bt[:, c, :], rhs=U0[:, c, :], start=True, stop=False,
                                 skip_group_check=True)
                        last = T.matmul(g, lhsT=Kt[:, c, :], rhs=V[:, c, :], start=False, stop=True,
                                        skip_group_check=True)
                    last.then_inc(g_ready, 1)
                    for c in range(NCH):
                        last = T.matmul(banks[4][:, c:c + 1], lhsT=Qb[:, c, :], rhs=ones_col[:, 0:1],
                                        start=True, stop=True,
                                        skip_group_check=True)
                    last.then_inc(b_ready, 1)
                    for c in range(NCH):
                        if c >= 1:
                            pe.wait_ge(s_done, c)
                        else:
                            pe.wait_ge(g_done, 1)
                        T.matmul(banks[1 + c % 2][:, 0:HD], lhsT=M1T[:, c, :], rhs=S[:, c, :],
                                 start=True, stop=True).then_inc(m_ready, 1)
                    for c in range(NCH):
                        last = T.matmul(banks[3][:, c * HD:(c + 1) * HD], lhsT=WT[:, c, :],
                                        rhs=S[:, c, :], start=True, stop=True, skip_group_check=True)
                    last.then_inc(u_ready, 1)
                    pe.wait_ge(u_done, 1)
                    for c in range(NCH):
                        y = banks[5][:, c * HD:(c + 1) * HD]
                        T.matmul(y, lhsT=Rb[:, c, :], rhs=S[:, c, :], start=True, stop=False,
                                 skip_group_check=True)
                        T.matmul(y, lhsT=RbT[:, c, :], rhs=U[:, c, :], start=False, stop=False,
                                 skip_group_check=True)
                        last = T.matmul(y, lhsT=RkT[:, c, :], rhs=V[:, c, :], start=False, stop=True,
                                        skip_group_check=True)
                    last.then_inc(y_ready, 1)
                    pe.wait_ge(gain_done, 1)
                    for c in range(NCH):
                        last = T.matmul(banks[6][:, c * HD:(c + 1) * HD], lhsT=Vb[:, c, :],
                                        rhs=cons["stack"][:, :], start=True, stop=True,
                                        skip_group_check=True)
                    last.then_inc(turned, 1)

                @block.vector
                def _(dve):
                    link = core.dve_link.on(dve)
                    W_ = nc.vector
                    wide = [P, NCH, HD]

                    def bank(i):
                        return banks[i][:, :].rearrange("p (c v) -> p c v", c=NCH)

                    dve.wait_ge(g_ready, 1)
                    W_.tensor_tensor(G[:, :, :], bank(0), total.to_broadcast(wide), ALU.mult)\
                      .then_inc(g_done, 1)
                    dve.wait_ge(g_done, 1)
                    for c in range(NCH):
                        dve.wait_ge(m_ready, c + 1)
                        W_.scalar_tensor_tensor(S[:, c + 1, :], banks[1 + c % 2][:, 0:HD],
                                                total[:, c, :], G[:, c, :], ALU.mult, ALU.add)\
                          .then_inc(s_done, 1)
                    dve.wait_ge(s_done, NCH)
                    dve.wait_ge(u_ready, 1)
                    W_.tensor_tensor(U[:, :, :], bank(3), U0[:, :, :], ALU.add).then_inc(u_done, 1)
                    dve.wait_ge(b_ready, 1)
                    link(W_.tensor_copy(bonus[:, :], banks[4][:, 0:NCH]))
                    dve.wait_ge(y_ready, 1)
                    link(W_.tensor_copy(Yt[:, :, :], bank(5)))
                    for c in range(NCH):
                        link(W_.bn_stats(stats[:, c, :], Yt[:, c, :]))
                        link(W_.bn_aggr(mv[:, c, :], stats[:, c, :]))
                    link(W_.tensor_scalar(rs[:, :], mv[:, :, 1], HD * 1e-5, None, ALU.add))
                    W_.reciprocal(rs[:, :], rs[:, :]).then_inc(norm, 1)
                    link(W_.tensor_tensor(Yt[:, :, :], Yt[:, :, :], mv[:, :, 0:1].to_broadcast(wide),
                                          ALU.subtract))
                    dve.wait_ge(root, 1)
                    link(W_.tensor_tensor(Yt[:, :, :], Yt[:, :, :],
                                          rs[:, :].unsqueeze(2).to_broadcast(wide), ALU.mult))
                    link(W_.tensor_tensor(Yt[:, :, :], Yt[:, :, :],
                                          lnw[:, :].unsqueeze(1).to_broadcast(wide), ALU.mult))
                    link(W_.tensor_tensor(Yt[:, :, :], Yt[:, :, :],
                                          lnb[:, :].unsqueeze(1).to_broadcast(wide), ALU.add))
                    link(W_.tensor_tensor(V[:, :, :], V[:, :, :],
                                          bonus[:, :].unsqueeze(2).to_broadcast(wide), ALU.mult))
                    for h in range(2):
                        r = slice(h * HD, (h + 1) * HD)
                        ins = W_.tensor_tensor(Vb[r, :, r], Yt[r, :, :], V[r, :, :], ALU.add)
                        link(ins) if h == 0 else ins.then_inc(gain_done, 1)
                    dve.wait_ge(turned, 1)
                    W_.tensor_tensor(out, banks[6][:, :], f["gate"], ALU.mult)

                @block.scalar
                def _(act):
                    act.wait_ge(norm, 1)
                    nc.scalar.activation(rs[:, :], rs[:, :], ACT.Sqrt).then_inc(root, 1)


def products(core, name, steps, mask):
    nc = core.nc
    HALF = NCH // 2
    with Stage(core, name) as st:
        banks = st.banks(4)
        multiplied, written = st.sem("multiplied"), st.sem("written")
        turns = [(step, h) for step in steps for h in range(2)]
        with core.block() as block:
            @block.tensor
            def _(pe):
                for n, ((lhsT, rhs, how, arg, dst), h) in enumerate(turns):
                    if n >= 2:
                        pe.wait_ge(written, n - 1)
                    w = dst.shape[2]
                    for c in range(HALF):
                        cc = h * HALF + c
                        last = nc.tensor.matmul(
                            banks[n % 4][:, c * w:(c + 1) * w], lhsT=lhsT[:, cc, :],
                            rhs=rhs[:, cc, :] if len(rhs.shape) == 3 else rhs[:, :], start=True,
                            stop=True, skip_group_check=True)
                    last.then_inc(multiplied, 1)

            @block.vector
            def _(dve):
                for n, ((lhsT, rhs, how, arg, dst), h) in enumerate(turns):
                    dve.wait_ge(multiplied, n + 1)
                    w = dst.shape[2]
                    part = slice(h * HALF, (h + 1) * HALF)
                    ps = banks[n % 4][:, 0:HALF * w].rearrange("p (c v) -> p c v", c=HALF)
                    if how == "mask":
                        ins = nc.vector.tensor_tensor(dst[:, part, :], ps, mask(arg), ALU.mult)
                    elif how == "add":
                        other = arg if arg.shape[1] == HALF else arg[:, part, :]
                        ins = nc.vector.tensor_tensor(dst[:, part, :], ps, other, ALU.add)
                    else:
                        ins = nc.vector.tensor_copy(dst[:, part, :], ps)
                    ins.then_inc(written, 1)


def condition(core, name, layer, silu_c, vec, mod, ident, rows, row_specs):
    nc, dram = core.nc, core.dram
    W = 256
    NCK = 6 * D // W
    PER = W // P
    wk = dram["ada_w_2"][layer].rearrange("(k p) n -> p k n", p=P)
    with Stage(core, name) as st:
        banks = st.banks(3)
        ring = st.sb("ring", [P, W_SLOTS, KD, W])
        gated = st.sb("gated", [P, len(row_specs), KD])
        loaded = [st.sem(f"loaded{i}") for i in range(W_SLOTS)]
        done, free, added, rows_in, rows_out = (st.sem("done"), st.sem("free"), st.sem("added"),
                                                st.sem("rows_in"), st.sem("rows_out"))
        with core.block() as block:
            @block.sync
            def _(sp):
                for c in range(NCK):
                    if c >= W_SLOTS:
                        sp.wait_ge(done, c - W_SLOTS + 1)
                    sp.dma_start(ring[:, c % W_SLOTS], wk[:, :, c * W:(c + 1) * W])\
                      .then_inc(loaded[c % W_SLOTS], 16)

            @block.tensor
            def _(pe):
                for c in range(NCK):
                    pe.wait_ge(loaded[c % W_SLOTS], 16 * (c // W_SLOTS + 1))
                    for j in range(PER):
                        col = 2 * (PER * c + j)
                        for k in range(KD):
                            last = nc.tensor.matmul(banks[0][:, col:col + 2],
                                                    lhsT=ring[:, c % W_SLOTS, k, j * P:(j + 1) * P],
                                                    rhs=silu_c[:, k, :], start=(k == 0),
                                                    stop=(k == KD - 1), skip_group_check=True)
                    last.then_inc(done, 1)
                pe.wait_ge(added, 1)
                for r in range(len(row_specs)):
                    if r >= 1:
                        pe.wait_ge(rows_out, r)
                    for k in range(KD):
                        last = nc.tensor.matmul(banks[1 + k // 4][:, (k % 4) * P:(k % 4 + 1) * P],
                                                lhsT=gated[:, r, k:k + 1].to_broadcast([P, P]),
                                                rhs=ident[:, :], start=True, stop=True,
                                                skip_group_check=True)
                    last.then_inc(rows_in, 1)

            @block.vector
            def _(dve):
                link = core.dve_link.on(dve)
                at = VEC_AT["ada_b_2"] + 48 * layer

                def gain(i):
                    g = VEC_AT["norm_g_2"] + KD * (4 * layer + i)
                    return vec[:, g:g + KD]

                dve.wait_ge(done, NCK)
                link(nc.vector.tensor_tensor(mod[:, :, :], banks[0][:, 0:96].rearrange("p (j s) -> p s j", s=2),
                                             vec[:, at:at + 48].unsqueeze(1).to_broadcast([P, 2, 48]),
                                             ALU.add))
                for i, (which, g) in enumerate(((1, 0), (4, 2))):
                    for s in range(2):
                        m = mod[:, s, which * KD:(which + 1) * KD]
                        link(nc.vector.scalar_tensor_tensor(m, m, 1.0, gain(g), ALU.add, ALU.mult))
                for r, (row, which, s, g) in enumerate(row_specs):
                    last = nc.vector.tensor_tensor(gated[:, r, :], mod[:, s, which * KD:(which + 1) * KD],
                                                   gain(g), ALU.mult)
                last.then_inc(added, 1)
                for r, (row, which, s, g) in enumerate(row_specs):
                    dve.wait_ge(rows_in, r + 1)
                    nc.vector.tensor_copy(rows[:, row, 0:BANK], banks[1][:, :])
                    nc.vector.tensor_copy(rows[:, row, BANK:D], banks[2][:, :]).then_inc(rows_out, 1)


def rotate(core, name, tiles, rot, cos, sin):
    nc = core.nc
    with Stage(core, name) as st:
        banks = st.banks(4)
        r, c, s = st.sb("rot", [P, P]), st.sb("cos", [P, SEQ]), st.sb("sin", [P, SEQ])
        tmp = st.sb("tmp", [P, 2, SEQ])
        load(core, name + "_c", [(r[:, :], const(core, rot)), (c[:, :], const(core, cos)),
                                 (s[:, :], const(core, sin))])
        swapped, done = st.sem("swapped"), st.sem("done")
        with core.block() as block:
            @block.tensor
            def _(pe):
                for i, (whole, part) in enumerate(tiles):
                    if i >= 4:
                        pe.wait_ge(done, i - 3)
                    n = whole.shape[0]
                    nc.tensor.matmul(banks[i % 4][0:n, :], lhsT=r[0:n, 0:n], rhs=whole, start=True,
                                     stop=True).then_inc(swapped, 1)

            @block.vector
            def _(dve):
                link = core.dve_link.on(dve)
                for i, (whole, part) in enumerate(tiles):
                    a = part.start_partition()
                    q = slice(a, a + part.shape[0])
                    dve.wait_ge(swapped, i + 1)
                    nc.vector.tensor_tensor(tmp[q, i % 2, :], banks[i % 4][q, :], s[q, :], ALU.mult)
                    link(nc.vector.tensor_tensor(part, part, c[q, :], ALU.mult))
                    last = nc.vector.tensor_tensor(part, part, tmp[q, i % 2, :], ALU.add)
                    last.then_inc(done, 1)
                    dve.wait_ge(done, i + 1)


def window_and_diff(core, h_all, x, ctx, rows, o_tok, ident):
    nc, dram = core.nc, core.dram
    T_QAW, T_QD, T_KAW, T_VAW, T_KD, T_VD = 0, 4, 8, 9, 10, 14
    with Stage(core, "ab") as st:
        p = st.sb("p", [P, 18, ALL])
        v = st.sb("v", [P, NX + NC_, 5 * P])
        srcs = [h_all[:, :, 0:SEQ], h_all[:, :, SEQ:ALL]]
        linear(core, "ab_in", dram["ab_w_in_2"][0], srcs, "features",
               copy_out(nc, lambda s, t, c, cw: p[:, t, SEQ * s:SEQ * s + srcs[s].shape[2]]))
        turn(core, "ab_v", [g for t in range(NX + NC_) for g in (
            ([p[:, f, t * P:(t + 1) * P] for f in (T_VAW, T_VD, T_VD + 1, T_VD + 2)],
             v[:, t, 0:4 * P].rearrange("p (b c) -> p b c", b=4), None),
            ([p[:, T_VD + 3, t * P:(t + 1) * P]], v[:, t, 4 * P:5 * P].unsqueeze(1), None))], ident)
        rotate(core, "ab_r", [(p[:, f, 0:SEQ],) * 2 for f in (*range(T_QAW, T_KAW + 1),
                                                               *range(T_KD, T_VD))],
               "rot64", "cos64", "sin64")
        small = st.sb("small", [P, 8])
        keep = st.sb("keep", [P, 2, P])
        lv = st.sb("lv", [P, 4, HD])
        lam = st.sb("lam", [P, 4])
        gain = st.sb("gain", [P, P])
        load(core, "ab_c", [(small[:, :], bass.AP(dram["ab_sink_2"].tensor, 0, [[0, P], [1, 8]])),
                            (keep[:, 0, :], const(core, "keep_before")),
                            (keep[:, 1, :], const(core, "keep_after")),
                            (lv[:, :, :], bass.AP(dram["diff_lambda_2"].tensor, 0,
                                                  [[0, P], [HD, 4], [1, HD]])),
                            (gain[:, :], bass.AP(dram["diff_subln_g_2"].tensor, 0, [[0, P], [1, P]]))])
        dots, exps = st.sem("dots"), st.sem("exps")
        lam0 = 0.8 - 0.6
        with core.block() as block:
            @block.vector
            def _(dve):
                link = core.dve_link.on(dve)
                link(nc.vector.tensor_scalar(small[:, :], small[:, :], -1.0, None, ALU.mult))
                for i in range(2):
                    link(nc.vector.tensor_tensor(lv[:, 2 * i, :], lv[:, 2 * i, :], lv[:, 2 * i + 1, :],
                                                 ALU.mult))
                    link(nc.vector.reduce_sum(lam[:, i:i + 1], lv[:, 2 * i, :], AX.X))
                nc.vector.sem_inc(dots, 1)
                dve.wait_ge(exps, 1)
                link(nc.vector.tensor_tensor(lam[:, 2:3], lam[:, 0:1], lam[:, 1:2], ALU.subtract))
                link(nc.vector.tensor_scalar(lam[:, 2:3], lam[:, 2:3], lam0, None, ALU.add))

            @block.scalar
            def _(act):
                act.wait_ge(dots, 1)
                nc.scalar.activation(lam[:, 0:2], lam[:, 0:2], ACT.Exp).then_inc(exps, 1)
        jobs = []
        ctx_blocks = list(range(NX, NX + NC_))
        for h in range(8):
            rq = slice(HD * (h % 2), HD * (h % 2) + HD)
            kv = h // 4
            for t in range(NX + NC_):
                near = [b for b in (t - 1, t, t + 1) if 0 <= b < NX] if t < NX else []
                bias = []
                if t < NX:
                    if t >= 1:
                        bias.append((0, ident[:, :], keep[:, 0, :]))
                    if t + 1 < NX:
                        bias.append((P * (len(near) - 1), ident[:, :], keep[:, 1, :]))
                key = [p[rq, T_KAW, b * P:(b + 1) * P] for b in near] + [p[rq, T_KAW, SEQ:ALL]]
                if kv != h % 2:
                    key = [p[rq, T_VAW, b * P:(b + 1) * P] for b in near] + [p[rq, T_VAW, SEQ:ALL]]
                jobs.append(dict(q=p[rq, T_QAW + h // 2, t * P:(t + 1) * P], keys=key, bias=bias,
                                 hide=None,
                                 values=[v[:, b, kv * HD:(kv + 1) * HD] for b in near + ctx_blocks],
                                 scale=HD ** -0.5, sink=small[:, h:h + 1],
                                 out=o_tok[:, t, h * HD:(h + 1) * HD], minus=None))
        for h in range(4):
            for t in range(NX + NC_):
                blocks = list(range(NX + NC_)) if t < NX else ctx_blocks
                out = o_tok[:, t, BANK + h * P:BANK + (h + 1) * P]
                for m in range(2):
                    rq = slice(HD * m, HD * m + HD)
                    jobs.append(dict(q=p[rq, T_QD + h, t * P:(t + 1) * P],
                                     keys=[p[rq, T_KD + h, blocks[0] * P:ALL]], bias=[], hide=None,
                                     values=[v[:, b, (1 + h) * P:(2 + h) * P] for b in blocks],
                                     scale=HD ** -0.5, sink=None, out=out,
                                     minus=(lam[:, 2:3], out) if m else None))
        swapped_in, swapped_out = st.sem("swapped_in"), st.sem("swapped_out")
        with core.block() as block:
            @block.sync
            def _(sp):
                sp.dma_start(p[0:HD, T_VAW, :], p[HD:P, T_KAW, :]).then_inc(swapped_in, 16)
                sp.dma_start(p[HD:P, T_VAW, :], p[0:HD, T_KAW, :]).then_inc(swapped_in, 16)
                sp.wait_ge(swapped_in, 32)
        attend(core, "ab_at", jobs, ident)
        total = st.sb("total", [P, 24])
        sq = st.sb("sq", [P, P])
        summed, inverted, rooted = st.sem("summed"), st.sem("inverted"), st.sem("rooted")
        with core.block() as block:
            cells = [o_tok[:, t, BANK + h * P:BANK + (h + 1) * P] for t in range(NX + NC_)
                     for h in range(4)]

            @block.scalar
            def _(act):
                link = core.act_link.on(act)
                for i, o in enumerate(cells):
                    link(nc.scalar.activation(sq[:, :], o, ACT.Square, accum_out=total[:, i:i + 1]))
                nc.scalar.sem_inc(summed, 1)
                act.wait_ge(inverted, 1)
                nc.scalar.activation(total[:, :], total[:, :], ACT.Sqrt).then_inc(rooted, 1)

            @block.vector
            def _(dve):
                link = core.dve_link.on(dve)
                link(nc.vector.tensor_scalar(gain[:, :], gain[:, :], 1.0 - lam0, None, ALU.mult))
                dve.wait_ge(summed, 1)
                invert_mean(core, link, total[:, :], P).then_inc(inverted, 1)
                dve.wait_ge(rooted, 1)
                for i, o in enumerate(cells):
                    nc.vector.scalar_tensor_tensor(o, o, total[:, i:i + 1], gain[:, :], ALU.mult,
                                                   ALU.mult)


def latent(core, h_all, o_tok, vec, ident):
    nc, dram = core.nc, core.dram
    QL, KL, NH, NOPE, ROPE = 384, 256, 16, 64, 32
    DK = NOPE + ROPE
    NT = NX + NC_
    with Stage(core, "la") as st:
        pq = st.sb("pq", [P, 3, SEQ])
        pkv = st.sb("pkv", [P, 2, ALL])
        rope = st.sb("rope", [DK, ALL])
        if True:
            with Stage(core, "lc") as s3:
                ptok = s3.sb("ptok", [P, NT, QL + KL + ROPE])
                w = dram["mla_w_in_2"][0]
                linear(core, "la_q", w, [h_all[:, :, 0:SEQ]], "tokens",
                       copy_out(nc, lambda s, t, c, cw: ptok[:, t, 0:cw]), cols=QL)
                linear(core, "la_k", w, [h_all[:, :, 0:ALL]], "tokens",
                       copy_out(nc, lambda s, t, c, cw: ptok[:, t, QL:QL + cw]), col0=QL)
                turn(core, "la_r", [([ptok[:, t, QL + KL - NOPE:QL + KL + ROPE]],
                                     rope[NOPE:DK, t * P:(t + 1) * P].unsqueeze(1), None)
                                    for t in range(NT)], ident)
                gq, gk = VEC_AT["mla_q_norm_g_2"], VEC_AT["mla_kv_norm_g_2"]
                norm_to_features(core, "la_nq", [(ptok[:, t, 0:QL], pq[:, :, t * P:(t + 1) * P],
                                                  vec[:, gq:gq + 3], None) for t in range(NX)], ident)
                norm_to_features(core, "la_nk", [(ptok[:, t, QL:QL + KL], pkv[:, :, t * P:(t + 1) * P],
                                                  vec[:, gk:gk + 2], None) for t in range(NT)], ident)
            qT = st.sb("qT", [DK, NH, SEQ])
            kT = st.sb("kT", [DK, NH, ALL])
            linear(core, "la_wq", dram["mla_wq_b_2"][0], [pq[:, :, :]], "features",
                   copy_out(nc, lambda s, t, c, cw: qT[:, t, :]), width=4 * DK, out_tile=DK)
            wkv = dram["mla_wkv_b_2"][0]
            srcs = [pkv[:, :, 0:SEQ], pkv[:, :, SEQ:ALL]]

            def keys(eng, ps, s, t, c, cw):
                return nc.scalar.activation(kT[0:NOPE, t, SEQ * s:SEQ * s + srcs[s].shape[2]],
                                            ps[0:NOPE], ACT.Copy)

            linear(core, "la_wk", wkv, srcs, "features", keys)
            tiles = [(qT[:, h, :], qT[NOPE:DK, h, :]) for h in range(NH)]
            with core.block() as block:
                @block.vector
                def _(dve):
                    nc.vector.memset(rope[0:NOPE, :], 0.0)
            tiles.append((rope[:, 0:SEQ], rope[NOPE:DK, 0:SEQ]))
            rotate(core, "la_rot", tiles, "rot32", "cos32", "sin32")
            with core.block() as block:
                @block.vector
                def _(dve):
                    for h in range(0, NH, 2):
                        nc.vector.tensor_copy(kT[NOPE:DK, h, :], rope[NOPE:DK, :])

                @block.scalar
                def _(act):
                    for h in range(1, NH, 2):
                        nc.scalar.activation(kT[NOPE:DK, h, :], rope[NOPE:DK, :], ACT.Copy)
            v = core.values
            def vals(eng, ps, s, t, c, cw):
                src = ps.rearrange("p (h z) -> p h z", z=P)[:, :, NOPE:P]
                h0 = c // P
                return nc.scalar.activation(v[:, t, h0 * HD:(h0 + cw // P) * HD]
                                            .rearrange("p (h z) -> p h z", z=HD), src, ACT.Copy)
            linear(core, "la_wv", wkv, [pkv[:, :, :]], "tokens", vals)
        jobs = [dict(q=qT[:, h, t * P:(t + 1) * P], keys=[kT[:, h, :]], bias=[], hide=None,
                     values=[v[:, b, h * HD:(h + 1) * HD] for b in range(NT)],
                     scale=DK ** -0.5, sink=None, out=o_tok[:, t, h * HD:(h + 1) * HD], minus=None)
                for h in range(NH) for t in range(NX)]
        attend(core, "la_at", jobs, ident)


def program(nc, dram, out, upto=99):
    with ExitStack() as stack:
        core = Core(nc, stack, dram)

        def sb(name, shape):
            return stack.enter_context(nc.sbuf_tensor(name, shape, F32))

        ident = sb("ident", [P, P])
        vec = sb("vec", [P, N_VEC])
        x = sb("x", [P, NX, D])
        ctx = sb("ctx", [P, NC_, D])
        feat = sb("feat", [P, KD, ALL])
        tok = feat[:, :, :].rearrange("p k t -> p (k t)").rearrange("p (t d) -> p t d", d=D)

        n_rows = (N_VEC + P - 1) // P
        with Stage(core, "vec") as st:
            rows_sb = st.sb("rows", [P, n_rows, P])
            cleared, loaded = st.sem("cleared"), st.sem("loaded")
            with core.block() as block:
                @block.vector
                def _(dve):
                    nc.vector.memset(rows_sb[:, :, :], 0.0).then_inc(cleared, 1)

                @block.sync
                def _(sp):
                    n = 4
                    sp.dma_start(ident[:, :], const(core, "ident")).then_inc(loaded, 16)
                    sp.dma_start(x[:, :, :], dram["x"][0].rearrange("(t p) d -> p t d", p=P))\
                      .then_inc(loaded, 16)
                    sp.dma_start(ctx[:, :, :], dram["ctx_2"][0].rearrange("(t p) d -> p t d", p=P))\
                      .then_inc(loaded, 16)
                    sp.wait_ge(cleared, 1)
                    n = 3
                    for name, rows in VECTORS:
                        at, r = VEC_AT[name], 0
                        while r < rows:
                            m = min(rows - r, P - (at + r) % P)
                            src = bass.AP(dram[name].tensor, r * P, [[P, m], [1, P]])
                            p0 = (at + r) % P
                            sp.dma_start(rows_sb[p0:p0 + m, (at + r) // P, :], src).then_inc(loaded, 16)
                            r, n = r + m, n + 1
                    sp.wait_ge(loaded, 16 * n)
            turn(core, "vec_t", [([rows_sb[:, i, :]],
                                  vec[:, i * P:min(N_VEC, (i + 1) * P)].unsqueeze(1), None)
                                 for i in range(n_rows)], ident)

        def v(name, i=0, n=KD):
            return vec[:, VEC_AT[name] + i:VEC_AT[name] + i + n]

        def tok_tile(t):
            return tok[:, t, :]

        norm_to_features(core, "n1", [(x[:, t, :], feat[:, :, t * P:(t + 1) * P], v("norm_mix_pre"), None)
                                      for t in range(NX)], ident)
        with Stage(core, "m1") as st:
            proj = st.sb("proj", [P, N_PROJ, SEQ])
            linear(core, "w_in", dram["w_in"][0], [feat[:, :, 0:SEQ]], "features",
                   copy_out(nc, lambda s, t, c, cw: proj[:, t, :]))
            if upto == 1:
                return
            mix = feat
            chunk_attention(core, proj, mix[:, :, 0:SEQ], ident)
            rglru(core, proj, mix[:, :, 0:SEQ], vec)
            hgrn(core, proj, mix[:, :, 0:SEQ], vec, ident)
            rwkv(core, proj, mix[:, :, 0:SEQ], vec, ident)
            if upto == 2:
                return
        with Stage(core, "o1") as st:
            y = st.sb("y", [P, NX, D])
            row = st.sb("row", [P, 2, D])
            load(core, "o1_c", [(row[:, i, :], bass.AP(dram[n].tensor, 0, [[0, P], [1, D]]))
                                for i, n in enumerate(("norm_mix_post", "norm_mlp_post"))])
            linear(core, "w_out", dram["w_out"][0], [feat[:, :, 0:SEQ]], "tokens",
                   copy_out(nc, lambda s, t, c, cw: y[:, t, c:c + cw]))
            add_normed(core, "r1", [(y[:, t, :], x[:, t, :], row[:, 0, :]) for t in range(NX)])
            norm_to_features(core, "n2", [(x[:, t, :], feat[:, :, t * P:(t + 1) * P],
                                           v("norm_mlp_pre"), None) for t in range(NX)], ident)
            if upto == 3:
                return
            with Stage(core, "mlp") as s2:
                ff = s2.sb("ff", [P, MLP // P, SEQ])
                relu = s2.sb("relu", [P, 2, SEQ])

                def squared_relu(eng, ps, s, t, c, cw):
                    link = core.dve_link.on(eng)
                    link(nc.vector.tensor_scalar(relu[:, t % 2, :], ps, 0.0, None, ALU.max))
                    return nc.vector.tensor_tensor(ff[:, t, :], relu[:, t % 2, :], relu[:, t % 2, :],
                                                   ALU.mult)

                linear(core, "w1", dram["mlp_w1"][0], [feat[:, :, 0:SEQ]], "features", squared_relu,
                       engine="dve", width=256)
                linear(core, "w2", dram["mlp_w2"][0], [ff[:, :, :]], "tokens",
                       copy_out(nc, lambda s, t, c, cw: y[:, t, c:c + cw]))
            add_normed(core, "r2", [(y[:, t, :], x[:, t, :], row[:, 1, :]) for t in range(NX)])
        if upto == 4:
            return

        silu_c = sb("silu_c", [P, KD, 2])
        mod = sb("mod", [P, 2, 48])
        with core.block() as block:
            @block.scalar
            def _(act):
                for s, name in enumerate(("c_2", "c_ctx_2")):
                    nc.scalar.activation(silu_c[:, :, s], v(name), ACT.Silu)
        core.values = None
        for layer in range(2):
            last = layer == 1
            nt = NX if last else NX + NC_
            L = f"l{layer}"
            with Stage(core, L + "rows") as lr:
                rows = lr.sb("rows", [P, 2 if last else 4, D])
                specs = [(0, 2, 0, 1), (1, 5, 0, 3)] + ([] if last else [(2, 2, 1, 1), (3, 5, 1, 3)])
                condition(core, L + "ada", layer, silu_c, vec, mod, ident, rows, specs)

                def stream(t):
                    return x[:, t, :] if t < NX else ctx[:, t - NX, :]

                def normed(name, which, tiles):
                    norm_to_features(core, name, [
                        (stream(t), feat[:, :, t * P:(t + 1) * P],
                         mod[:, int(t >= NX), (which + 1) * KD:(which + 2) * KD],
                         mod[:, int(t >= NX), which * KD:(which + 1) * KD]) for t in range(tiles)], ident)

                normed(L + "n1", 0, NX + NC_)
                if upto == 5:
                    return
                if last:
                    with Stage(core, "lv") as sv:
                        core.values = sv.sb("values", [P, NX + NC_, D])
                        latent(core, feat[:, :, :], tok, vec, ident)
                    w_out = dram["mla_w_out_2"][0]
                else:
                    window_and_diff(core, feat[:, :, :], x, ctx, rows, tok, ident)
                    w_out = dram["ab_w_out_2"][0]
                if upto == 6:
                    return
                with Stage(core, L + "o") as so:
                    oT = so.sb("oT", [P, KD, nt * P])
                    turn(core, L + "t", [([tok[:, t, (4 * g + i) * P:(4 * g + i + 1) * P] for i in range(4)],
                                          oT[:, 4 * g:4 * g + 4, t * P:(t + 1) * P], None)
                                         for t in range(nt) for g in range(2)], ident)
                    linear(core, L + "wo", w_out, [oT[:, :, :]], "tokens",
                           copy_out(nc, lambda s, t, c, cw: tok[:, t, c:c + cw]))
                row_of = lambda t, i: rows[:, i + 2 * int(t >= NX), :]
                add_normed(core, L + "r1", [(tok_tile(t), stream(t), row_of(t, 0)) for t in range(nt)])
                normed(L + "n2", 3, nt)
                if upto == 7:
                    return
                with Stage(core, L + "f") as sf:
                    ff = sf.sb("ff", [P, FFN // P, nt * P])
                    parts = [slice(0, SEQ)] + ([] if last else [slice(SEQ, ALL)])
                    gated_up(core, L + "w13", dram["ffn_w13_2"][layer], [feat[:, :, s] for s in parts],
                             [ff[:, :, s] for s in parts])
                    linear(core, L + "w2", dram["ffn_w2_2"][layer], [ff[:, :, :]], "tokens",
                           copy_out(nc, lambda s, t, c, cw: tok[:, t, c:c + cw]))
                add_normed(core, L + "r2", [(tok_tile(t), stream(t), row_of(t, 1)) for t in range(nt)])
                if upto == 8:
                    return
        stored = stack.enter_context(nc.semaphore("stored"))
        with core.block() as block:
            @block.sync
            def _(sp):
                sp.dma_start(out[0].rearrange("(t p) d -> p t d", p=P), x[:, :, :]).then_inc(stored, 16)
                sp.wait_ge(stored, 16)


_INS = ["x", "norm_mix_pre", "norm_mix_post", "norm_mlp_pre", "norm_mlp_post", "w_in", "w_out",
        "attn_rel_bias", "hgrn_norm", "rwkv_mu", "rwkv_w0", "rwkv_w2", "rwkv_a0",
        "rwkv_a2", "rwkv_g2", "rwkv_k_k", "rwkv_k_a", "rwkv_r_k", "rwkv_ln_w", "rwkv_ln_b",
        "lru_conv_w", "lru_conv_b", "lru_wa", "lru_ba", "lru_wx", "lru_bx", "lru_lambda", "mlp_w1",
        "mlp_w2", "c_2", "ctx_2", "c_ctx_2", "ada_w_2", "ada_b_2", "norm_g_2", "ffn_w13_2", "ffn_w2_2",
        "ab_w_in_2", "ab_w_out_2", "ab_sink_2", "diff_lambda_2", "diff_subln_g_2", "mla_w_in_2",
        "mla_q_norm_g_2", "mla_kv_norm_g_2", "mla_wq_b_2", "mla_wkv_b_2", "mla_w_out_2"]


def kernel(**inputs):
    import concourse.bacc as bacc
    from concourse.bass_utils import run_bass_kernel_spmd

    nc = bacc.Bacc("TRN2", target_bir_lowering=False, num_devices=1)
    arrays, dram = {}, {}
    for name in _INS:
        a = np.ascontiguousarray(inputs[name])
        arrays[f"in_{name}"] = a
        dram[name] = nc.dram_tensor(f"in_{name}", a.shape, mybir.dt.from_np(a.dtype),
                                    kind="ExternalInput").ap()
    arrays["shape_constants"] = shape_constants()
    dram["consts"] = nc.dram_tensor("shape_constants", (P, N_CONST), F32, kind="ExternalInput").ap()
    dram["bias_ext"] = nc.dram_tensor("bias_ext", (GW // HD, 2 * SEQ), F32, kind="Internal").ap()
    out = nc.dram_tensor("out", (1, SEQ, D), F32, kind="ExternalOutput").ap()
    program(nc, dram, out)
    r = run_bass_kernel_spmd(nc, [arrays], core_ids=[0])
    return r.results[0]["out"]
```

```python
from contextlib import ExitStack, contextmanager

import numpy as np

import concourse.bass as bass
from concourse import mybir

F32 = mybir.dt.float32
F32R = mybir.dt.float32r
ALU = mybir.AluOpType
ACT = mybir.ActivationFunctionType
AX = mybir.AxisListType

P = 128
BANK = 512
D = 1024
KD = D // P
SEQ = 512
CTX = 256
ALL = SEQ + CTX
NX = SEQ // P
NC_ = CTX // P
GW = 256
HD = 64
CH = 64
NCH = SEQ // CH
MLP = 4 * D
FFN = 2816
EPS = 1e-6
NEG = -1e30
REL = 256
THETA = 10000.0
GRID = 64

CONSTS = {}


def _columns():
    at = 0
    for name, n in [("ident", P), ("upper", P), ("lower", P), ("upper_eq", P), ("blk16", P),
                    ("lvl32", P), ("lvl64", P), ("stack", HD), ("anti", P), ("ones64", P),
                    ("keep_before", P), ("keep_after", P), ("rot64", P), ("rot32", P),
                    ("cos64", SEQ), ("sin64", SEQ), ("cos32", SEQ), ("sin32", SEQ),
                    ("restart", SEQ), ("levels", 7 * P)]:
        CONSTS[name] = (at, n)
        at += n
    return at


N_CONST = _columns()


def shape_constants():
    c = np.zeros((P, N_CONST), np.float32)

    def put(name, a):
        at, n = CONSTS[name]
        c[:a.shape[0], at:at + n] = a

    i, j = np.arange(P)[:, None], np.arange(P)[None, :]
    same = (i // HD) == (j // HD)
    put("ident", np.eye(P))
    put("upper", same & (i < j))
    put("lower", same & (i > j))
    put("upper_eq", same & (i <= j))
    put("blk16", i // 16 == j // 16)
    put("lvl32", (i // 32 == j // 32) & (i // 16 != j // 16))
    put("lvl64", (i // 64 == j // 64) & (i // 32 != j // 32))
    put("stack", np.eye(HD)[np.arange(P) % HD])
    put("anti", np.eye(P)[::-1])
    put("ones64", same)
    put("keep_before", np.where(j >= i, 0.0, NEG))
    put("keep_after", np.where(j <= i, 0.0, NEG))

    def rotation(dim, first, reps):
        q = dim // 4
        r = np.zeros((P, P), np.float32)
        cos, sin = np.zeros((P, SEQ)), np.zeros((P, SEQ))
        inv = THETA ** (-np.arange(0, dim // 2, 2, dtype=np.float32) / np.float32(dim // 2))
        inv = inv.astype(np.float32)
        t = np.arange(SEQ)
        for rep in range(reps):
            for axis, pos in enumerate((t // GRID, t % GRID)):
                for k in range(q):
                    a = first + rep * dim + axis * 2 * q + k
                    ang = (pos.astype(np.float32) * inv[k]).astype(np.float32)
                    r[a + q, a] = -1.0
                    r[a, a + q] = 1.0
                    for m in (a, a + q):
                        cos[m], sin[m] = np.cos(ang), np.sin(ang)
        return r, cos, sin

    r, cos, sin = rotation(64, 0, 2)
    put("rot64", r)
    put("cos64", cos)
    put("sin64", sin)
    r, cos, sin = rotation(32, 64, 1)
    put("rot32", r)
    put("cos32", cos)
    put("sin32", sin)
    put("restart", np.broadcast_to(np.arange(SEQ) % CH != 0, (P, SEQ)))
    put("levels", np.concatenate(
        [i == j] + [(i // b == j // b) & (i % b < b // 2) & (j % b >= b // 2)
                    for b in (2, 4, 8, 16, 32, 64)], axis=1))
    return c


VECTORS = [("norm_mix_pre", 8), ("norm_mlp_pre", 8), ("hgrn_norm", 2), ("rwkv_mu", 7), ("rwkv_w0", 2),
           ("rwkv_a0", 2), ("rwkv_k_k", 2), ("rwkv_k_a", 2), ("rwkv_r_k", 2), ("lru_conv_w", 8),
           ("lru_conv_b", 2), ("lru_ba", 2), ("lru_bx", 2), ("lru_lambda", 2), ("c_2", 8),
           ("c_ctx_2", 8), ("norm_g_2", 64), ("ada_b_2", 96), ("mla_q_norm_g_2", 3),
           ("mla_kv_norm_g_2", 2)]
VEC_AT = {}
_at = 0
for _n, _r in VECTORS:
    VEC_AT[_n] = _at
    _at += _r
N_VEC = _at


class Link:

    def __init__(self, sem):
        self.sem, self.n = sem, 0

    def on(self, eng):
        self.eng = eng
        return self

    def __call__(self, ins):
        self.n += 1
        ins.then_inc(self.sem, 1)
        self.eng.wait_ge(self.sem, self.n)


class Core:

    def __init__(self, nc, stack, dram):
        self.nc, self.dram = nc, dram
        self.act_link = Link(stack.enter_context(nc.semaphore("act_link")))
        self.dve_link = Link(stack.enter_context(nc.semaphore("dve_link")))
        self.ended = 0
        self.cleared = []

    @contextmanager
    def block(self):
        with self.nc.Block() as block:
            yield block
        self.ended += 1

    def reusable(self):
        for i, (number, when) in enumerate(self.cleared):
            if self.ended > when:
                return self.cleared.pop(i)[0]
        return None


class Stage:

    def __init__(self, core, name):
        self.core, self.nc, self.name, self.stack = core, core.nc, name, ExitStack()
        self.sems = []

    def __enter__(self):
        self.stack.__enter__()
        return self

    def __exit__(self, *a):
        for s in self.sems:
            self.nc.gpsimd.sem_clear(s)
            self.core.cleared.append((s.num, self.core.ended))
        return self.stack.__exit__(*a)

    def sb(self, name, shape, dt=F32):
        return self.stack.enter_context(self.nc.sbuf_tensor(f"{self.name}_{name}", shape, dt))

    def banks(self, n):
        return [self.stack.enter_context(self.nc.psum_tensor(f"{self.name}_bank{i}", [P, BANK], F32))
                for i in range(n)]

    def sem(self, name):
        num = self.core.reusable()
        s = self.stack.enter_context(self.nc.semaphore(f"{self.name}_{name}", num=num))
        self.sems.append(s)
        return s


def const(core, name):
    at, n = CONSTS[name]
    return core.dram["consts"][:, at:at + n]


def load(core, name, pairs):
    nc = core.nc
    with Stage(core, name) as st, core.block() as block:
        loaded = st.sem("loaded")

        @block.sync
        def _(sp):
            for dst, src in pairs:
                sp.dma_start(dst, src).then_inc(loaded, 16)
            sp.wait_ge(loaded, 16 * len(pairs))


def turn(core, name, groups, ident):
    nc = core.nc
    with Stage(core, name) as st:
        banks = st.banks(4)
        turned, written = st.sem("turned"), st.sem("written")
        with core.block() as block:
            @block.tensor
            def _(pe):
                for g, (blocks, out, scale) in enumerate(groups):
                    if g >= 4:
                        pe.wait_ge(written, g - 3)
                    for b, src in enumerate(blocks):
                        rows = src.shape[0]
                        cols = src.shape[1]
                        last = nc.tensor.transpose(banks[g % 4][0:cols, b * P:b * P + rows], src,
                                                   ident[0:rows, 0:rows])
                    last.then_inc(turned, 1)

            @block.vector
            def _(dve):
                for g, (blocks, out, scale) in enumerate(groups):
                    rows, n, cols = out.shape
                    dve.wait_ge(turned, g + 1)
                    src = banks[g % 4][:, 0:n * P].rearrange("p (b c) -> p b c", b=n)
                    src = src[out.start_partition():out.start_partition() + rows, :, 0:cols]
                    if scale is None:
                        nc.vector.tensor_copy(out, src).then_inc(written, 1)
                    else:
                        nc.vector.tensor_tensor(out, src, scale.to_broadcast([rows, n, cols]),
                                                ALU.mult).then_inc(written, 1)


def invert_mean(core, link, total, width, eps=EPS):
    link(core.nc.vector.tensor_scalar(total, total, 1.0 / width, eps, ALU.mult, ALU.add))
    return core.nc.vector.reciprocal(total, total)


def norm_to_features(core, name, jobs, ident):
    nc = core.nc
    with Stage(core, name) as st:
        width = jobs[0][0].shape[1]
        kt = width // P
        half = (kt + 1) // 2 if kt > 4 else kt
        banks = st.banks(8)
        squares = st.sb("squares", [P, 2, width])
        total = st.sb("total", [P, len(jobs)])
        rstd = st.sb("rstd", [P, len(jobs)])
        xn = st.sb("xn", [P, 2, width])
        summed, rooted, scaled = st.sem("summed"), st.sem("rooted"), st.sem("scaled")
        inverted, valued, hi_done = st.sem("inverted"), st.sem("valued"), st.sem("hi_done")
        full = st.sb("full", [P, 2, 4, P])
        turned, written = st.sem("turned"), st.sem("written")
        parts = [(k0, min(k0 + 4, kt)) for k0 in range(0, kt, 4)]
        with core.block() as block:
            @block.scalar
            def _(act):
                for t, (src, dst, gain, shift) in enumerate(jobs):
                    if t >= 2:
                        act.wait_ge(summed, t - 1)
                    nc.scalar.activation(squares[:, t % 2, :], src, ACT.Square,
                                         accum_out=total[:, t:t + 1]).then_inc(summed, 1)
                act.wait_ge(inverted, 1)
                nc.scalar.activation(rstd[:, :], total[:, :], ACT.Sqrt).then_inc(rooted, 1)
                for t, (src, dst, gain, shift) in enumerate(jobs):
                    for q, (k0, k1) in enumerate(parts):
                        n = len(parts) * t + q
                        act.wait_ge(valued, n + 1)
                        hi_of(nc, dst[0][:, k0:k1, :], full[:, n % 2, 0:k1 - k0, :]).then_inc(hi_done, 1)

            def low_part(dve, n):
                t, (k0, k1) = n // len(parts), parts[n % len(parts)]
                hi, lo = jobs[t][1]
                dve.wait_ge(hi_done, n + 1)
                lo_of(nc, lo[:, k0:k1, :], full[:, n % 2, 0:k1 - k0, :], hi[:, k0:k1, :])\
                    .then_inc(written, 1)

            def normalise(dve, t):
                if t >= 2:
                    dve.wait_ge(turned, len(parts) * (t - 1))
                nc.vector.tensor_scalar(xn[:, t % 2, :], jobs[t][0], rstd[:, t:t + 1],
                                        None, ALU.mult).then_inc(scaled, 1)

            @block.vector
            def _(dve):
                link = core.dve_link.on(dve)
                dve.wait_ge(summed, len(jobs))
                invert_mean(core, link, total[:, :], width).then_inc(inverted, 1)
                dve.wait_ge(rooted, 1)
                normalise(dve, 0)
                for t, (src, dst, gain, shift) in enumerate(jobs):
                    if t + 1 < len(jobs):
                        normalise(dve, t + 1)
                    for q, (k0, k1) in enumerate(parts):
                        n = len(parts) * t + q
                        dve.wait_ge(turned, n + 1)
                        ps = banks[n % 8][:, 0:(k1 - k0) * P].rearrange("p (b c) -> p b c", c=P)
                        out = full[:, n % 2, 0:k1 - k0, :]
                        if n >= 2:
                            dve.wait_ge(written, n - 1)
                        ins = nc.vector.tensor_tensor(
                            out, ps, gain[:, k0:k1].unsqueeze(2).to_broadcast([P, k1 - k0, P]),
                            ALU.mult)
                        if shift is not None:
                            link(ins)
                            ins = nc.vector.tensor_tensor(
                                out, out, shift[:, k0:k1].unsqueeze(2).to_broadcast([P, k1 - k0, P]),
                                ALU.add)
                        ins.then_inc(valued, 1)
                        if n >= 1:
                            low_part(dve, n - 1)
                low_part(dve, len(parts) * len(jobs) - 1)

            @block.tensor
            def _(pe):
                for t in range(len(jobs)):
                    pe.wait_ge(scaled, t + 1)
                    for q, (k0, k1) in enumerate(parts):
                        n = len(parts) * t + q
                        if n >= 8:
                            pe.wait_ge(written, n - 7)
                        for k in range(k0, k1):
                            last = nc.tensor.transpose(banks[n % 8][:, (k - k0) * P:(k - k0 + 1) * P],
                                                       xn[:, t % 2, k * P:(k + 1) * P], ident[:, :])
                        last.then_inc(turned, 1)


def add_normed(core, name, jobs):
    nc = core.nc
    with Stage(core, name) as st:
        squares = st.sb("squares", [P, 2, D])
        scaled_y = st.sb("scaled_y", [P, 2, D])
        total = st.sb("total", [P, len(jobs)])
        rstd = st.sb("rstd", [P, len(jobs)])
        summed, inverted, rooted = st.sem("summed"), st.sem("inverted"), st.sem("rooted")
        with core.block() as block:
            @block.scalar
            def _(act):
                for t, (y, x, row) in enumerate(jobs):
                    if t >= 2:
                        act.wait_ge(summed, t - 1)
                    nc.scalar.activation(squares[:, t % 2, :], y, ACT.Square,
                                         accum_out=total[:, t:t + 1]).then_inc(summed, 1)
                act.wait_ge(inverted, 1)
                nc.scalar.activation(rstd[:, :], total[:, :], ACT.Sqrt).then_inc(rooted, 1)

            @block.vector
            def _(dve):
                link = core.dve_link.on(dve)
                dve.wait_ge(summed, len(jobs))
                invert_mean(core, link, total[:, :], D).then_inc(inverted, 1)
                dve.wait_ge(rooted, 1)
                for t, (y, x, row) in enumerate(jobs):
                    link(nc.vector.scalar_tensor_tensor(scaled_y[:, t % 2, :], y, rstd[:, t:t + 1],
                                                        row, ALU.mult, ALU.mult))
                    link(nc.vector.tensor_tensor(x, x, scaled_y[:, t % 2, :], ALU.add))


W_SLOTS = 3


def hi_of(nc, out, src):
    return nc.scalar.activation(out, src, ACT.Copy)


def lo_of(nc, out, src, hi):
    return nc.vector.tensor_tensor(out, src, hi.bitcast(F32), ALU.subtract)


def three_products(nc, out, lhsT, rhs, k, first, last_):
    for n, (i, j) in enumerate(((0, 0), (0, 1), (1, 0))):
        last = nc.tensor.matmul(out, lhsT=lhsT(i, k), rhs=rhs(j, k), start=first and n == 0,
                                stop=last_ and n == 2)
    return last


def linear(core, name, weight, srcs, form, finish, col0=0, cols=None, width=None, kchunk=None,
           engine="act", out_tile=P, ring=None):
    nc = core.nc
    K, N = weight.shape
    cols = N - col0 if cols is None else cols
    KT = K // P
    pre = isinstance(srcs[0], tuple)
    kchunk = min(KT, kchunk or (8 if pre else 2))
    width = width or (256 if pre else BANK)
    lens = [(s[0] if pre else s).shape[2] for s in srcs]
    chunks = []
    for n0 in range(0, cols, width):
        for k0 in range(0, KT, kchunk):
            chunks.append((n0, min(width, cols - n0), k0, min(k0 + kchunk, KT)))
    NCHK = len(chunks)

    def tiles(n0, w):
        if form == "features":
            return [(s, n0 // out_tile + j, n0 + j * out_tile, min(out_tile, w - j * out_tile))
                    for j in range((w + out_tile - 1) // out_tile) for s in range(len(srcs))]
        return [(s, t, n0, w) for s in range(len(srcs)) for t in range(lens[s] // P)]

    wk = weight.rearrange("(k p) n -> p k n", p=P)
    with Stage(core, name) as st:
        banks = st.banks(8)
        raw = st.sb("raw", [P, W_SLOTS, kchunk, width]) if ring is None else ring
        whi = st.sb("whi", [P, 2, kchunk, width], F32R)
        wlo = st.sb("wlo", [P, 2, kchunk, width], F32R)
        if not pre:
            shi = [st.sb(f"shi{s}", [P, 2, kchunk, n], F32R) for s, n in enumerate(lens)]
            slo = [st.sb(f"slo{s}", [P, 2, kchunk, n], F32R) for s, n in enumerate(lens)]
        loaded = [st.sem(f"loaded{i}") for i in range(W_SLOTS)]
        used, ready, free = st.sem("used"), st.sem("ready"), st.sem("free")
        hi_done, lo_done = st.sem("hi_done"), st.sem("lo_done")
        after, first, n_ready, n_used = [], [], 0, 0
        for n0, w, k0, k1 in chunks:
            first.append(n_ready)
            if k1 == KT:
                n_ready += len(tiles(n0, w))
                after.append((ready, n_ready))
            else:
                n_used += 1
                after.append((used, n_used))

        def parts(i):
            n0, w, k0, k1 = chunks[i]
            n = k1 - k0
            yield raw[:, i % W_SLOTS, 0:n, 0:w], whi[:, i % 2, 0:n, 0:w], wlo[:, i % 2, 0:n, 0:w]
            if not pre:
                for s, src in enumerate(srcs):
                    yield src[:, k0:k1, :], shi[s][:, i % 2, 0:n, :], slo[s][:, i % 2, 0:n, :]

        def write_out(eng, i):
            n0, w, k0, k1 = chunks[i]
            if k1 == KT:
                for j, (s, t, c, cw) in enumerate(tiles(n0, w)):
                    g = first[i] + j
                    eng.wait_ge(ready, g + 1)
                    ps = (banks[g % 8][0:cw, 0:lens[s]] if form == "features"
                          else banks[g % 8][:, 0:cw])
                    finish(eng, ps, s, t, c, cw).then_inc(free, 1)

        with core.block() as block:
            @block.sync
            def _(sp):
                for i, (n0, w, k0, k1) in enumerate(chunks):
                    if i >= W_SLOTS:
                        sp.wait_ge(lo_done, i - W_SLOTS + 1)
                    sp.dma_start(raw[:, i % W_SLOTS, 0:k1 - k0, 0:w],
                                 wk[:, k0:k1, col0 + n0:col0 + n0 + w]).then_inc(loaded[i % W_SLOTS], 16)

            @block.scalar
            def _(act):
                for i in range(NCHK + 1):
                    if i < NCHK:
                        act.wait_ge(loaded[i % W_SLOTS], 16 * (i // W_SLOTS + 1))
                        if i >= 2:
                            act.wait_ge(*after[i - 2])
                        for src, hi, lo in parts(i):
                            last = hi_of(nc, hi, src)
                        last.then_inc(hi_done, 1)
                    if i >= 1 and engine == "act":
                        write_out(act, i - 1)

            @block.vector
            def _(dve):
                for i in range(NCHK + 1):
                    if i < NCHK:
                        dve.wait_ge(hi_done, i + 1)
                        for src, hi, lo in parts(i):
                            last = lo_of(nc, lo, src, hi)
                        last.then_inc(lo_done, 1)
                    if i >= 1 and engine == "dve":
                        write_out(dve, i - 1)

            @block.tensor
            def _(pe):
                for i, (n0, w, k0, k1) in enumerate(chunks):
                    pe.wait_ge(lo_done, i + 1)
                    for j, (s, t, c, cw) in enumerate(tiles(n0, w)):
                        g = first[i] + j
                        if k0 == 0 and g >= 8:
                            pe.wait_ge(free, g - 7)

                        def wt(part, k):
                            return (whi, wlo)[part][:, i % 2, k - k0, c - n0:c - n0 + cw]

                        def xt(part, k):
                            x = (srcs[s][part][:, k, :] if pre
                                 else (shi, slo)[part][s][:, i % 2, k - k0, :])
                            return x if form == "features" else x[:, t * P:(t + 1) * P]

                        out = (banks[g % 8][0:cw, 0:lens[s]] if form == "features"
                               else banks[g % 8][:, 0:cw])
                        lhsT, rhs = (wt, xt) if form == "features" else (xt, wt)
                        for k in range(k0, k1):
                            last = three_products(nc, out, lhsT, rhs, k, k == 0, k == KT - 1)
                        if k1 == KT:
                            last.then_inc(ready, 1)
                    if k1 < KT:
                        last.then_inc(used, 1)


def gated_up(core, name, w13, srcs, dsts, raw):
    nc = core.nc
    n_chunks = FFN // P
    slots = raw.shape[1]
    wk = w13.rearrange("(k p) n -> p k n", p=P)
    ns = len(srcs)
    lens = [s[0].shape[2] for s in srcs]
    pairs = [(c, s) for c in range(n_chunks) for s in range(ns)]
    with Stage(core, name) as st:
        banks = st.banks(8)
        whi = st.sb("whi", [P, 2, 2, KD, P], F32R)
        wlo = st.sb("wlo", [P, 2, 2, KD, P], F32R)
        gate = st.sb("gate", [P, 2, SEQ])
        loaded = [st.sem(f"loaded{i}") for i in range(slots)]
        ready, silu_done, free = st.sem("ready"), st.sem("silu_done"), st.sem("free")
        hi_done, lo_done = st.sem("hi_done"), st.sem("lo_done")
        with core.block() as block:
            @block.sync
            def _(sp):
                for c in range(n_chunks):
                    if c >= slots:
                        sp.wait_ge(lo_done, c - slots + 1)
                    for h in range(2):
                        sp.dma_start(raw[:, c % slots, h],
                                     wk[:, :, h * FFN + c * P:h * FFN + (c + 1) * P])\
                          .then_inc(loaded[c % slots], 16)

            @block.tensor
            def _(pe):
                for p, (c, s) in enumerate(pairs):
                    if s == 0:
                        pe.wait_ge(lo_done, c + 1)
                    if p >= 4:
                        pe.wait_ge(free, p - 3)
                    for h in range(2):
                        for k in range(KD):
                            last = three_products(
                                nc, banks[(2 * p + h) % 8][:, 0:lens[s]],
                                lambda part, k: (whi, wlo)[part][:, c % 2, h, k, :],
                                lambda part, k: srcs[s][part][:, k, :], k, k == 0, k == KD - 1)
                    last.then_inc(ready, 1)

            @block.scalar
            def _(act):
                def split(c):
                    act.wait_ge(loaded[c % slots], 32 * (c // slots + 1))
                    if c >= 2:
                        act.wait_ge(ready, ns * (c - 1))
                    hi_of(nc, whi[:, c % 2], raw[:, c % slots]).then_inc(hi_done, 1)

                split(0)
                for p, (c, s) in enumerate(pairs):
                    if s == 0 and c + 1 < n_chunks:
                        split(c + 1)
                    act.wait_ge(ready, p + 1)
                    if p >= 2:
                        act.wait_ge(free, p - 1)
                    n = lens[s]
                    nc.scalar.activation(gate[:, p % 2, 0:n], banks[2 * p % 8][:, 0:n], ACT.Silu)\
                      .then_inc(silu_done, 1)

            @block.vector
            def _(dve):
                def split(c):
                    dve.wait_ge(hi_done, c + 1)
                    lo_of(nc, wlo[:, c % 2], raw[:, c % slots], whi[:, c % 2]).then_inc(lo_done, 1)

                split(0)
                for p, (c, s) in enumerate(pairs):
                    if s == 0 and c + 1 < n_chunks:
                        split(c + 1)
                    dve.wait_ge(silu_done, p + 1)
                    n = lens[s]
                    nc.vector.tensor_tensor(dsts[s][:, c, :], gate[:, p % 2, 0:n],
                                            banks[(2 * p + 1) % 8][:, 0:n], ALU.mult).then_inc(free, 1)


def attend(core, name, jobs, ident):
    nc = core.nc
    NS = 4
    with Stage(core, name) as st:
        wide = [st.stack.enter_context(nc.psum_tensor(f"{name}_scores{b}", [P, 2 * BANK], F32))
                for b in range(2)]
        flip = st.stack.enter_context(nc.psum_tensor(f"{name}_flip", [P, 2 * BANK], F32))
        obank = [st.stack.enter_context(nc.psum_tensor(f"{name}_o{b}", [P, BANK], F32))
                 for b in range(2)]
        E = st.sb("E", [P, 2, ALL])
        ET = st.sb("ET", [P, 2, ALL])
        top = st.sb("top", [P, NS])
        ntop = st.sb("ntop", [P, NS])
        den = st.sb("den", [P, NS])
        esink = st.sb("esink", [P, NS])
        inv = st.sb("inv", [P, NS])
        scores_ready, max_ready, exp_done = st.sem("scores"), st.sem("max"), st.sem("exp")
        turned, copied, pv_done, out_done = (st.sem("turned"), st.sem("copied"), st.sem("pv"),
                                             st.sem("out"))
        N = len(jobs)

        def n_keys(i):
            return P * len(jobs[i]["values"])

        with core.block() as block:
            @block.tensor
            def _(pe):
                def scores(i):
                    job, S = jobs[i], wide[i % 2]
                    if i >= 2:
                        pe.wait_ge(exp_done, i - 1)
                    pieces, at = [], 0
                    for key in job["keys"]:
                        n, done = key.shape[1], 0
                        while done < n:
                            m = min(n - done, BANK - at % BANK)
                            pieces.append((at, m, job["q"], key[:, done:done + m]))
                            at, done = at + m, done + m
                    extra = [(c, r.shape[1], l, r) for c, l, r in job["bias"]]
                    for b in range(2):
                        mine = [x for x in pieces + extra if x[0] // BANK == b]
                        for x, (c, m, l, r) in enumerate(mine):
                            last = nc.tensor.matmul(S[:, c:c + m], lhsT=l, rhs=r, start=(x == 0),
                                                    stop=(x == len(mine) - 1), skip_group_check=True)
                    last.then_inc(scores_ready, 1)

                def turn_probs(i):
                    pe.wait_ge(exp_done, i + 1)
                    if i >= 1:
                        pe.wait_ge(copied, i)
                    for b in range(n_keys(i) // P):
                        last = nc.tensor.transpose(flip[:, b * P:(b + 1) * P],
                                                   E[:, i % 2, b * P:(b + 1) * P], ident[:, :])
                    last.then_inc(turned, 1)

                def weigh(i):
                    pe.wait_ge(copied, i + 1)
                    if i >= 2:
                        pe.wait_ge(out_done, i - 1)
                    values = jobs[i]["values"]
                    for b, v in enumerate(values):
                        last = nc.tensor.matmul(obank[i % 2][:, 0:v.shape[1]],
                                                lhsT=ET[:, i % 2, b * P:(b + 1) * P], rhs=v,
                                                start=(b == 0), stop=(b == len(values) - 1))
                    last.then_inc(pv_done, 1)

                for i in range(N + 2):
                    if i < N:
                        scores(i)
                    if 1 <= i <= N:
                        turn_probs(i - 1)
                    if i >= 2:
                        weigh(i - 2)

            @block.vector
            def _(dve):
                link = core.dve_link.on(dve)

                def maximum(i):
                    job, s = jobs[i], i % NS
                    dve.wait_ge(scores_ready, i + 1)
                    if job["hide"]:
                        rows, c0, c1 = job["hide"]
                        link(nc.vector.memset(wide[i % 2][rows[0]:rows[1], c0:c1], NEG))
                    link(nc.vector.reduce_max(top[:, s:s + 1], wide[i % 2][:, 0:n_keys(i)], AX.X))
                    if job["sink"] is None:
                        ins = nc.vector.tensor_scalar(ntop[:, s:s + 1], top[:, s:s + 1], -job["scale"],
                                                      None, ALU.mult)
                    else:
                        ins = nc.vector.tensor_scalar(ntop[:, s:s + 1], top[:, s:s + 1], -job["scale"],
                                                      job["sink"], ALU.mult, ALU.min)
                    ins.then_inc(max_ready, 1)

                def copy(i):
                    dve.wait_ge(turned, i + 1)
                    if i >= 2:
                        dve.wait_ge(pv_done, i - 1)
                    nc.vector.tensor_copy(ET[:, i % 2, 0:n_keys(i)], flip[:, 0:n_keys(i)])\
                      .then_inc(copied, 1)

                def result(i):
                    job, s = jobs[i], i % NS
                    o = obank[i % 2][:, 0:job["out"].shape[1]]
                    if job["sink"] is not None:
                        link(nc.vector.tensor_tensor(den[:, s:s + 1], den[:, s:s + 1],
                                                     esink[:, s:s + 1], ALU.add))
                    link(nc.vector.reciprocal(inv[:, s:s + 1], den[:, s:s + 1]))
                    dve.wait_ge(pv_done, i + 1)
                    if job["minus"] is None:
                        nc.vector.tensor_scalar(job["out"], o, inv[:, s:s + 1], None, ALU.mult)\
                          .then_inc(out_done, 1)
                    else:
                        lam, base = job["minus"]
                        link(nc.vector.tensor_scalar(inv[:, s:s + 1], inv[:, s:s + 1], lam, -1.0,
                                                     ALU.mult, ALU.mult))
                        dve.wait_ge(out_done, i)
                        nc.vector.scalar_tensor_tensor(job["out"], o, inv[:, s:s + 1], base, ALU.mult,
                                                       ALU.add).then_inc(out_done, 1)

                for i in range(N + 2):
                    if i < N:
                        maximum(i)
                    if 1 <= i <= N:
                        copy(i - 1)
                    if i >= 2:
                        result(i - 2)

            @block.scalar
            def _(act):
                for i, job in enumerate(jobs):
                    s = i % NS
                    act.wait_ge(max_ready, i + 1)
                    if i >= 2:
                        act.wait_ge(turned, i - 1)
                    if i >= NS:
                        act.wait_ge(out_done, i - NS + 1)
                    if job["sink"] is not None:
                        nc.scalar.activation(esink[:, s:s + 1], job["sink"], ACT.Exp,
                                             bias=ntop[:, s:s + 1], scale=-1.0)
                    nc.scalar.activation(E[:, i % 2, 0:n_keys(i)], wide[i % 2][:, 0:n_keys(i)], ACT.Exp,
                                         bias=ntop[:, s:s + 1], scale=job["scale"],
                                         accum_out=den[:, s:s + 1]).then_inc(exp_done, 1)


def copy_out(nc, dst):
    def finish(eng, ps, s, t, c, cw):
        return nc.scalar.activation(dst(s, t, c, cw), ps, ACT.Copy)
    return finish


T_QA, T_KA, T_VA = 0, 2, 4
T_QB, T_FB, T_IB, T_GB = 6, 8, 10, 12
T_RWKV = 14
T_XD, T_GD = 21, 23
N_PROJ = 25


def chunk_attention(core, proj, mix, ident):
    nc, dram = core.nc, core.dram
    heads = GW // HD
    EXT = 2 * SEQ
    NB = SEQ // P
    with Stage(core, "ca") as st:
        v_tok = st.sb("v_tok", [P, NX, GW])
        out_tok = st.sb("out_tok", [P, NX, GW])
        ext = st.sb("ext", [heads, EXT])
        hankel = st.sb("hankel", [P, heads, NB, P])
        anti = st.sb("anti", [P, P])
        q8 = st.sb("q8", [P, 2, SEQ])
        loaded, filled, stored = st.sem("loaded"), st.sem("filled"), st.sem("stored")
        with core.block() as block:
            @block.sync
            def _(sp):
                sp.dma_start(ext[:, SEQ - REL - 1:SEQ + REL],
                             dram["attn_rel_bias"][0]).then_inc(loaded, 16)
                sp.dma_start(anti[:, :], const(core, "anti")).then_inc(loaded, 16)
                sp.wait_ge(filled, 1)
                sp.dma_start(dram["bias_ext"][:, :], ext[:, :]).then_inc(stored, 16)
                sp.wait_ge(stored, 16)
                for h in range(heads):
                    for b in range(NB):
                        at = SEQ - P - P * b
                        src = bass.AP(dram["bias_ext"].tensor, h * EXT + at, [[1, P], [1, P]])
                        sp.dma_start(hankel[:, h, b, :], src).then_inc(loaded, 16)
                sp.wait_ge(loaded, 16 * (2 + heads * NB))

            @block.vector
            def _(dve):
                dve.wait_ge(loaded, 32)
                n = SEQ - REL - 1
                nc.vector.tensor_copy(ext[:, 0:n], ext[:, n:n + 1].to_broadcast([heads, n]))
                n = SEQ + REL
                nc.vector.tensor_copy(ext[:, n:EXT],
                                      ext[:, n - 1:n].to_broadcast([heads, EXT - n])).then_inc(filled, 1)
                nc.vector.tensor_scalar(q8[:, :, :], proj[:, T_QA:T_QA + 2, :], HD ** -0.5, None, ALU.mult)
        turn(core, "ca_v", [([proj[:, T_VA + a, t * P:(t + 1) * P] for a in range(2)],
                             v_tok[:, t, :].rearrange("p (a c) -> p a c", a=2), None)
                            for t in range(NX)], ident)
        jobs = []
        for h in range(heads):
            rows = slice(HD * (h % 2), HD * (h % 2) + HD)
            for t in range(NX):
                jobs.append(dict(
                    q=q8[rows, h // 2, t * P:(t + 1) * P],
                    keys=[proj[rows, T_KA + h // 2, 0:(t + 1) * P]],
                    bias=[(kb * P, anti[:, :], hankel[:, h, t - kb, :]) for kb in range(t + 1)],
                    hide=((0, CH), t * P + CH, (t + 1) * P),
                    values=[v_tok[:, kb, h * HD:(h + 1) * HD] for kb in range(t + 1)],
                    scale=1.0, sink=None, out=out_tok[:, t, h * HD:(h + 1) * HD], minus=None))
        attend(core, "ca_at", jobs, ident)
        turn(core, "ca_o", [([out_tok[:, t, a * P:(a + 1) * P] for a in range(2)],
                             mix[:, 0:2, t * P:(t + 1) * P], None) for t in range(NX)], ident)


class Conditioning:

    SLOTS = 4

    def __init__(self, core, stage, silu_c):
        self.core, self.silu_c = core, silu_c
        self.ring = stage.sb("ring", [P, self.SLOTS, KD, P])
        self.bank = stage.banks(1)[0]
        self.loaded = [stage.sem(f"loaded{i}") for i in range(self.SLOTS)]
        self.done = stage.sem("done")
        self.chunks = [(layer, j) for layer in range(2) for j in range(6 * D // P)]
        self.sent = self.taken = 0

    def send(self, sp, n):
        end = min(self.taken + n + self.SLOTS, len(self.chunks))
        for i in range(self.sent, end):
            layer, j = self.chunks[i]
            if i >= self.SLOTS:
                sp.wait_ge(self.done, i - self.SLOTS + 1)
            wk = self.core.dram["ada_w_2"][layer].rearrange("(k p) n -> p k n", p=P)
            sp.dma_start(self.ring[:, i % self.SLOTS], wk[:, :, j * P:(j + 1) * P])\
              .then_inc(self.loaded[i % self.SLOTS], 16)
        self.sent = max(self.sent, end)

    def left(self):
        return len(self.chunks) - self.taken

    def take(self, pe):
        i = self.taken
        if i == len(self.chunks):
            return
        self.taken += 1
        pe.wait_ge(self.loaded[i % self.SLOTS], 16 * (i // self.SLOTS + 1))
        for k in range(KD):
            last = self.core.nc.tensor.matmul(self.bank[:, 2 * i:2 * i + 2],
                                              lhsT=self.ring[:, i % self.SLOTS, k, :],
                                              rhs=self.silu_c[:, k, :], start=(k == 0),
                                              stop=(k == KD - 1), skip_group_check=True)
        last.then_inc(self.done, 1)


def hgrn(core, proj, mix, vec, ident, cond):
    nc = core.nc
    NT = SEQ // P
    LEVELS = 7
    with Stage(core, "hg") as st:
        def pairs(name):
            return st.sb(name, [P, 2, SEQ])

        key, q, cum, qe, kl, o, gate = (pairs(n) for n in ("key", "q", "cum", "qe", "kl", "o", "gate"))
        decay = st.sb("decay", [P, 2, 2, SEQ])
        qd = st.sb("qd", [P, 2, 2, SEQ])
        kd = st.sb("kd", [P, 2, 2, SEQ])
        att = st.sb("att", [P, 4, SEQ])
        i_tok = st.sb("i_tok", [P, 2, NT, P])
        k_tok = st.sb("k_tok", [P, 2, NT, P])
        G = st.sb("G", [P, 2, NCH, P])
        S = st.sb("S", [P, 2, NCH + 1, P])
        total = st.sb("total", [P, 2, NCH])
        levels = st.sb("levels", [P, LEVELS, P])
        restart = st.sb("restart", [P, SEQ])
        ones = st.sb("ones", [P, P])
        f = proj[:, T_FB:T_FB + 2, :]
        load(core, "hg_c", [(levels[:, :, :], const(core, "levels").rearrange("p (l c) -> p l c", c=P)),
                            (ones[:, :], const(core, "ones64")), (restart[:, :], const(core, "restart"))])

        def by_chunk(t):
            return t[:, :, :].rearrange("p a (c t) -> p (a c) t", t=CH)

        logged, gated, cum_done, exped = (st.sem("logged"), st.sem("gated"), st.sem("cum"),
                                          st.sem("exped"))
        with core.block() as block:
            @block.scalar
            def _(act):
                link = core.act_link.on(act)
                link(nc.scalar.activation(o[:, :, :], f, ACT.Abs))
                link(nc.scalar.activation(o[:, :, :], o[:, :, :], ACT.Exp, scale=-1.0))
                nc.scalar.activation(o[:, :, :], o[:, :, :], ACT.Ln, bias=1.0).then_inc(logged, 1)
                nc.scalar.activation(key[:, :, :], f, ACT.Sigmoid, scale=-1.0)
                nc.scalar.activation(q[:, :, :], proj[:, T_QB:T_QB + 2, :], ACT.Silu)
                nc.scalar.activation(gate[:, :, :], proj[:, T_GB:T_GB + 2, :], ACT.Silu).then_inc(gated, 1)
                act.wait_ge(cum_done, 1)
                nc.scalar.activation(qe[:, :, :], cum[:, :, :], ACT.Exp)
                nc.scalar.activation(total[:, :, :].rearrange("p a c -> p (a c)").unsqueeze(2),
                                     by_chunk(cum)[:, :, CH - 1:CH], ACT.Exp)
                act.wait_ge(cum_done, 2)
                nc.scalar.activation(kl[:, :, :], kl[:, :, :], ACT.Exp).then_inc(exped, 1)

            @block.vector
            def _(dve):
                link = core.dve_link.on(dve)
                V = nc.vector
                V.memset(att[:, :, :], 0.0)
                V.memset(S[:, :, 0, :], 0.0)
                dve.wait_ge(logged, 1)
                link(V.scalar_tensor_tensor(cum[:, :, :], f, 0.0, o[:, :, :], ALU.min, ALU.subtract))
                for a in range(2):
                    ins = V.tensor_tensor_scan(cum[:, a, :], restart[:, :], cum[:, a, :], 0.0, ALU.mult,
                                               ALU.add)
                    link(ins) if a == 0 else ins.then_inc(cum_done, 1)
                dve.wait_ge(cum_done, 1)
                V.tensor_tensor(by_chunk(kl), by_chunk(cum)[:, :, CH - 1:CH].to_broadcast([P, 2 * NCH, CH]),
                                by_chunk(cum), ALU.subtract).then_inc(cum_done, 1)
                dve.wait_ge(gated, 1)
                dve.wait_ge(exped, 1)
                link(V.tensor_tensor(qe[:, :, :], qe[:, :, :], q[:, :, :], ALU.mult))
                link(V.tensor_tensor(kl[:, :, :], kl[:, :, :], key[:, :, :], ALU.mult))
        turn(core, "hg_t", [([src[:, a, t * P:(t + 1) * P] for t in range(NT)], dst[:, a, :, :], None)
                            for a in range(2)
                            for src, dst in ((proj[:, T_IB:T_IB + 2, :], i_tok), (kl, k_tok))], ident)
        differed, decayed, weighted, scored, copied = (st.sem("differed"), st.sem("decayed"),
                                                       st.sem("weighted"), st.sem("scored"),
                                                       st.sem("copied"))
        g_ready, g_done = st.sem("g_ready"), st.sem("g_done")
        with Stage(core, "hgl") as ss:
            banks = ss.banks(6)
            with core.block() as block:
                @block.sync
                def _(sp):
                    cond.send(sp, LEVELS * 4)

                @block.vector
                def _(dve):
                    V = nc.vector

                    def differ(n):
                        b = 1 << n
                        h = b // 2
                        if n >= 3:
                            dve.wait_ge(weighted, 2 * (n - 2))
                        src = cum[:, :, :].rearrange("p a t -> p (a t)").rearrange("p (n b) -> p n b", b=b)
                        dst = decay[:, n % 2].rearrange("p a t -> p (a t)").rearrange("p (n b) -> p n b", b=b)
                        mid = src[:, :, h - 1:h].to_broadcast([P, 2 * SEQ // b, h])
                        V.tensor_tensor(dst[:, :, 0:h], mid, src[:, :, 0:h], ALU.subtract)
                        V.tensor_tensor(dst[:, :, h:b], src[:, :, h:b], mid, ALU.subtract)\
                         .then_inc(differed, 1)

                    def weight(n):
                        dve.wait_ge(decayed, n)
                        if n >= 3:
                            dve.wait_ge(scored, 4 * (n - 1))
                        V.tensor_tensor(qd[:, n % 2], q[:, :, :], decay[:, n % 2], ALU.mult)\
                         .then_inc(weighted, 1)

                    differ(1)
                    for n in range(LEVELS):
                        if n >= 1:
                            weight(n)
                        if n + 1 < LEVELS and n >= 1:
                            differ(n + 1)
                        for b in range(4):
                            dve.wait_ge(scored, 4 * n + b + 1)
                            V.copy_predicated(
                                att[:, b, :].rearrange("p (t c) -> p t c", c=P),
                                levels[:, n:n + 1, :].bitcast(mybir.dt.uint32).to_broadcast([P, NT, P]),
                                banks[b][:, :].rearrange("p (t c) -> p t c", c=P)).then_inc(copied, 1)
                        if n < 2:
                            dve.wait_ge(g_ready, n + 1)
                            for par in range(2):
                                last = V.tensor_tensor(
                                    G[:, n, par::2, :],
                                    banks[4 + par][:, :].rearrange("p (t c) -> p t c", c=P),
                                    ones[:, :].unsqueeze(1).to_broadcast([P, NT, P]), ALU.mult)
                            last.then_inc(g_done, 1)

                @block.gpsimd
                def _(pool):
                    for n in range(1, LEVELS):
                        pool.wait_ge(decayed, n)
                        if n >= 3:
                            pool.wait_ge(scored, 4 * (n - 1))
                        nc.gpsimd.tensor_tensor(kd[:, n % 2], key[:, :, :], decay[:, n % 2], ALU.mult)\
                          .then_inc(weighted, 1)

                @block.scalar
                def _(act):
                    for n in range(1, LEVELS):
                        act.wait_ge(differed, n)
                        nc.scalar.activation(decay[:, n % 2], decay[:, n % 2], ACT.Exp)\
                          .then_inc(decayed, 1)

                @block.tensor
                def _(pe):
                    for n in range(LEVELS):
                        if n >= 1:
                            pe.wait_ge(weighted, 2 * n)
                        qs, ks = (q[:, :, :], key[:, :, :]) if n == 0 else (qd[:, n % 2], kd[:, n % 2])
                        for b in range(4):
                            if n >= 1:
                                pe.wait_ge(copied, 4 * (n - 1) + b + 1)
                            a, r = b // 2, slice((b % 2) * HD, (b % 2 + 1) * HD)
                            for t in range(NT):
                                c = slice(t * P, (t + 1) * P)
                                last = nc.tensor.matmul(banks[b][:, c], lhsT=ks[r, a, c], rhs=qs[r, a, c],
                                                        start=True, stop=True, skip_group_check=True)
                            last.then_inc(scored, 1)
                            cond.take(pe)
                        if n < 2:
                            if n == 1:
                                pe.wait_ge(g_done, 1)
                            for t in range(NT):
                                for par in range(2):
                                    r = slice(par * CH, (par + 1) * CH)
                                    last = nc.tensor.matmul(banks[4 + par][:, t * P:(t + 1) * P],
                                                            lhsT=k_tok[r, n, t, :], rhs=i_tok[r, n, t, :],
                                                            start=True, stop=True, skip_group_check=True)
                            last.then_inc(g_ready, 1)
        within, stated, across, moved = (st.sem("within"), st.sem("stated"), st.sem("across"),
                                         st.sem("moved"))
        squared, meaned, inverted, rooted = (st.sem("squared"), st.sem("meaned"), st.sem("inverted"),
                                             st.sem("rooted"))
        sq, rstd, inter = qd[:, 0], qd[:, 1], kd[:, 0]
        with Stage(core, "hgo") as ss:
            banks = ss.banks(6)
            with core.block() as block:
                @block.sync
                def _(sp):
                    cond.send(sp, 4)

                @block.tensor
                def _(pe):
                    for a in range(2):
                        for h in range(2):
                            for t in range(NT):
                                c = slice(t * P, (t + 1) * P)
                                last = nc.tensor.matmul(banks[a][h * HD:(h + 1) * HD, c],
                                                        lhsT=i_tok[:, a, t, h * HD:(h + 1) * HD],
                                                        rhs=att[:, 2 * a + h, c], start=True, stop=True,
                                                        skip_group_check=True)
                        last.then_inc(within, 1)
                    for _ in range(4):
                        cond.take(pe)
                    for a in range(2):
                        pe.wait_ge(stated, a + 1)
                        for c in range(NCH):
                            last = nc.tensor.matmul(banks[2 + a][:, c * CH:(c + 1) * CH],
                                                    lhsT=S[:, a, c, :], rhs=qe[:, a, c * CH:(c + 1) * CH],
                                                    start=True, stop=True, skip_group_check=True)
                        last.then_inc(across, 1)
                    for a in range(2):
                        pe.wait_ge(squared, a + 1)
                        nc.tensor.matmul(banks[4 + a][:, :], lhsT=ones[:, :], rhs=sq[:, a, :], start=True,
                                         stop=True).then_inc(meaned, 1)

                @block.scalar
                def _(act):
                    for a in range(2):
                        act.wait_ge(across, a + 1)
                        nc.scalar.activation(inter[:, a, :], banks[2 + a][:, :], ACT.Copy)\
                          .then_inc(moved, 1)
                    for a in range(2):
                        act.wait_ge(inverted, a + 1)
                        nc.scalar.activation(rstd[:, a, :], rstd[:, a, :], ACT.Sqrt).then_inc(rooted, 1)

                @block.vector
                def _(dve):
                    link = core.dve_link.on(dve)
                    V = nc.vector
                    for a in range(2):
                        for c in range(NCH - 1):
                            ins = V.scalar_tensor_tensor(S[:, a, c + 1, :], S[:, a, c, :],
                                                         total[:, a, c:c + 1], G[:, a, c, :], ALU.mult,
                                                         ALU.add)
                            link(ins) if c < NCH - 2 else ins.then_inc(stated, 1)
                    for a in range(2):
                        dve.wait_ge(within, a + 1)
                        dve.wait_ge(moved, a + 1)
                        link(V.tensor_tensor(o[:, a, :], banks[a][:, :], inter[:, a, :], ALU.add))
                        V.tensor_tensor(sq[:, a, :], o[:, a, :], o[:, a, :], ALU.mult).then_inc(squared, 1)
                    for a in range(2):
                        dve.wait_ge(meaned, a + 1)
                        link(V.tensor_scalar(rstd[:, a, :], banks[4 + a][:, :], 1.0 / HD, EPS, ALU.mult,
                                             ALU.add))
                        V.reciprocal(rstd[:, a, :], rstd[:, a, :]).then_inc(inverted, 1)
                    for a in range(2):
                        dve.wait_ge(rooted, a + 1)
                        col = VEC_AT["hgrn_norm"] + a
                        link(V.scalar_tensor_tensor(o[:, a, :], o[:, a, :], vec[:, col:col + 1],
                                                    rstd[:, a, :], ALU.mult, ALU.mult))
                        V.tensor_tensor(mix[:, 2 + a, :], o[:, a, :], gate[:, a, :], ALU.mult)


def rglru(core, proj, mix, vec):
    nc, dram = core.nc, core.dram
    with Stage(core, "lru") as st:
        banks = st.banks(4)
        w = st.sb("w", [P, 2, 2, P])
        conv = st.sb("conv", [P, 2, SEQ])
        gates = st.sb("gates", [P, 2, 2, SEQ])
        la = st.sb("la", [P, 2, SEQ])
        a = st.sb("a", [P, 2, SEQ])
        e2 = st.sb("e2", [P, 2, SEQ])
        th = st.sb("th", [P, 2, SEQ])
        u = st.sb("u", [P, 2, SEQ])
        g = st.sb("g", [P, 2, SEQ])
        g3 = st.sb("g3", [P, 2, SEQ])
        sm = st.sb("sm", [P, 8, 2])
        cleared, loaded = st.sem("cleared"), st.sem("loaded")
        conv_done, gated, sigm, decayed = st.sem("conv"), st.sem("gated"), st.sem("sigm"), st.sem("decay")
        exped, lam_done, lam_exp, cubed, tanhed = (st.sem("exped"), st.sem("lam"), st.sem("lam_exp"),
                                                   st.sem("cubed"), st.sem("tanhed"))
        rooted, prod = st.sem("rooted"), st.sem("prod")

        def v(name, i=0, n=2):
            return vec[:, VEC_AT[name] + i:VEC_AT[name] + i + n]

        with core.block() as block:
            @block.sync
            def _(sp):
                sp.wait_ge(cleared, 1)
                for m, name in enumerate(("lru_wa", "lru_wx")):
                    for b in range(4):
                        r = HD * (b % 2)
                        sp.dma_start(w[r:r + HD, m, b // 2, r:r + HD], dram[name][0, b])\
                          .then_inc(loaded, 16)
                sp.wait_ge(loaded, 128)

            @block.tensor
            def _(pe):
                pe.wait_ge(loaded, 128)
                pe.wait_ge(conv_done, 1)
                for m in range(2):
                    for i in range(2):
                        nc.tensor.matmul(banks[2 * m + i][:, :], lhsT=w[:, m, i, :], rhs=conv[:, i, :],
                                         start=True, stop=True).then_inc(gated, 1)

            @block.scalar
            def _(act):
                link = core.act_link.on(act)
                act.wait_ge(lam_done, 1)
                nc.scalar.activation(sm[:, 1, :], sm[:, 0, :], ACT.Exp, scale=-1.0).then_inc(lam_exp, 1)
                for m, b in enumerate(("lru_ba", "lru_bx")):
                    for i in range(2):
                        act.wait_ge(gated, 2 * m + i + 1)
                        nc.scalar.activation(gates[:, m, i, :], banks[2 * m + i][:, :], ACT.Sigmoid,
                                             bias=v(b, i, 1)).then_inc(sigm, 1)
                act.wait_ge(decayed, 1)
                nc.scalar.activation(a[:, :, :], la[:, :, :], ACT.Exp)
                nc.scalar.activation(e2[:, :, :], la[:, :, :], ACT.Exp, scale=2.0)
                nc.scalar.activation(th[:, :, :], la[:, :, :], ACT.Tanh, scale=-1.0).then_inc(exped, 1)
                act.wait_ge(cubed, 1)
                nc.scalar.activation(g3[:, :, :], g3[:, :, :], ACT.Tanh, scale=(2.0 / np.pi) ** 0.5)\
                  .then_inc(tanhed, 1)
                act.wait_ge(prod, 1)
                nc.scalar.activation(e2[:, :, :], e2[:, :, :], ACT.Sqrt).then_inc(rooted, 1)

            @block.vector
            def _(dve):
                link = core.dve_link.on(dve)
                V = nc.vector
                V.memset(w[:, :, :, :], 0.0).then_inc(cleared, 1)
                link(V.tensor_scalar(sm[:, 6, :], v("lru_lambda"), -1.0, None, ALU.mult))
                V.tensor_tensor(sm[:, 0, :], sm[:, 6, :], v("lru_lambda"), ALU.max).then_inc(lam_done, 1)
                x = proj[:, T_XD:T_XD + 2, :]
                for i in range(2):
                    cw = [VEC_AT["lru_conv_w"] + 2 * j + i for j in range(4)]
                    link(V.tensor_scalar(conv[:, i, :], x[:, i, :], vec[:, cw[3]:cw[3] + 1],
                                         v("lru_conv_b", i, 1), ALU.mult, ALU.add))
                    for j in range(3):
                        s = 3 - j
                        link(V.scalar_tensor_tensor(conv[:, i, s:], x[:, i, 0:SEQ - s],
                                                    vec[:, cw[j]:cw[j] + 1], conv[:, i, s:], ALU.mult,
                                                    ALU.add))
                V.sem_inc(conv_done, 1)
                dve.wait_ge(lam_exp, 1)
                link(V.tensor_scalar(sm[:, 2, :], sm[:, 1, :], 2.0, None, ALU.add))
                link(V.reciprocal(sm[:, 2, :], sm[:, 2, :]))
                link(V.tensor_tensor(sm[:, 2, :], sm[:, 2, :], sm[:, 1, :], ALU.mult))
                link(V.tensor_tensor(sm[:, 3, :], sm[:, 2, :], sm[:, 2, :], ALU.mult))
                link(V.tensor_scalar(sm[:, 4, :], sm[:, 3, :], 2.0 / 15, 2.0 / 13, ALU.mult, ALU.add))
                for k in (11, 9, 7, 5, 3, 1):
                    link(V.tensor_tensor(sm[:, 4, :], sm[:, 4, :], sm[:, 3, :], ALU.mult))
                    link(V.tensor_scalar(sm[:, 4, :], sm[:, 4, :], 2.0 / k, None, ALU.add))
                link(V.tensor_tensor(sm[:, 4, :], sm[:, 4, :], sm[:, 2, :], ALU.mult))
                link(V.tensor_scalar(sm[:, 5, :], v("lru_lambda"), -1.0, 0.0, ALU.mult, ALU.max))
                link(V.tensor_tensor(sm[:, 5, :], sm[:, 5, :], sm[:, 4, :], ALU.add))
                link(V.tensor_scalar(sm[:, 5, :], sm[:, 5, :], -8.0, None, ALU.mult))
                dve.wait_ge(sigm, 4)
                for i in range(2):
                    link(V.tensor_scalar(la[:, i, :], gates[:, 0, i, :], sm[:, 5, i:i + 1], None, ALU.mult))
                V.sem_inc(decayed, 1)
                link(V.tensor_tensor(u[:, :, :], gates[:, 1], conv[:, :, :], ALU.mult))
                gd = proj[:, T_GD:T_GD + 2, :]
                link(V.tensor_tensor(g[:, :, :], gd, gd, ALU.mult))
                link(V.tensor_scalar(g[:, :, :], g[:, :, :], 0.044715, 1.0, ALU.mult, ALU.add))
                V.tensor_tensor(g3[:, :, :], g[:, :, :], gd, ALU.mult).then_inc(cubed, 1)
                dve.wait_ge(exped, 1)
                V.scalar_tensor_tensor(e2[:, :, :], e2[:, :, :], 1.0, th[:, :, :], ALU.add, ALU.mult)\
                 .then_inc(prod, 1)
                dve.wait_ge(tanhed, 1)
                link(V.scalar_tensor_tensor(g3[:, :, :], g3[:, :, :], 1.0, gd, ALU.add, ALU.mult))
                dve.wait_ge(rooted, 1)
                link(V.tensor_tensor(u[:, :, :], u[:, :, :], e2[:, :, :], ALU.mult))
                for i in range(2):
                    link(V.tensor_tensor_scan(g[:, i, :], a[:, i, :], u[:, i, :], 0.0, ALU.mult, ALU.add))
                V.scalar_tensor_tensor(mix[:, 6:8, :], g[:, :, :], 0.5, g3[:, :, :], ALU.mult, ALU.mult)


def rwkv(core, proj, mix, vec, ident, cond):
    nc, dram = core.nc, core.dram
    xs = proj[:, T_RWKV:T_RWKV + 7, :]
    free = list(range(0, T_RWKV)) + list(range(T_XD, N_PROJ))

    def two(i):
        at = free[2 * i]
        assert free[2 * i + 1] == at + 1
        return proj[:, at:at + 2, :]

    gate, av, lw, cum, kk, km, ex, ei, en = (two(i) for i in range(9))

    def v(name, i=0, n=2):
        return vec[:, VEC_AT[name] + i:VEC_AT[name] + i + n]

    with Stage(core, "rp") as st:
        banks = st.banks(6)
        diff = st.sb("diff", [P, 7, SEQ])
        lora = st.sb("lora", [P, GW])
        low = st.sb("low", [P, SEQ])
        ones = st.sb("ones", [P, P])
        restart = st.sb("restart", [P, SEQ])
        load(core, "rp_c", [(lora[0:32, :], dram["rwkv_w2"][0]), (lora[32:64, :], dram["rwkv_a2"][0]),
                            (lora[64:128, :], dram["rwkv_g2"][0]), (ones[:, :], const(core, "ones64")),
                            (restart[:, :], const(core, "restart"))])
        shifted, low_done, lora_done, sigm, ssq, summed = (st.sem("shifted"), st.sem("low"),
                                                           st.sem("lora"), st.sem("sigm"),
                                                           st.sem("ssq"), st.sem("summed"))
        inverted, rooted, cum_done, exped = (st.sem("inverted"), st.sem("rooted"), st.sem("cum"),
                                            st.sem("exped"))
        with core.block() as block:
            @block.vector
            def _(dve):
                link = core.dve_link.on(dve)
                V = nc.vector
                link(V.tensor_tensor(diff[:, :, 1:], xs[:, :, 0:SEQ - 1], xs[:, :, 1:], ALU.subtract))
                link(V.tensor_scalar(diff[:, :, 0:1], xs[:, :, 0:1], -1.0, None, ALU.mult))
                link(V.tensor_tensor(diff[:, :, :], diff[:, :, :],
                                     v("rwkv_mu", 0, 7).unsqueeze(2).to_broadcast([P, 7, SEQ]), ALU.mult))
                V.tensor_tensor(xs, xs, diff[:, :, :], ALU.add).then_inc(shifted, 1)
                dve.wait_ge(shifted, 1)
                for i in range(2):
                    link(V.tensor_scalar(kk[:, i, :], xs[:, 2 + i, :], v("rwkv_k_k", i, 1), None, ALU.mult))
                    V.tensor_tensor(diff[:, i, :], kk[:, i, :], kk[:, i, :], ALU.mult).then_inc(ssq, 1)
                for i in range(2):
                    dve.wait_ge(summed, i + 1)
                    link(V.tensor_scalar(diff[:, 2 + i, :], banks[4 + i][:, :], 1e-24, None, ALU.max))
                    V.reciprocal(diff[:, 2 + i, :], diff[:, 2 + i, :]).then_inc(inverted, 1)
                dve.wait_ge(sigm, 4)
                for i in range(2):
                    link(V.tensor_scalar(lw[:, i, :], lw[:, i, :], -float(np.exp(-0.5)), None, ALU.mult))
                    V.tensor_tensor_scan(cum[:, i, :], restart[:, :], lw[:, i, :], 0.0, ALU.mult, ALU.add)\
                     .then_inc(cum_done, 1)
                dve.wait_ge(cum_done, 2)
                V.tensor_tensor(diff[:, 4:6, :], cum, lw, ALU.subtract).then_inc(cum_done, 1)
                for i in range(2):
                    link(V.tensor_scalar(km[:, i, :], av[:, i, :], 1.0, v("rwkv_k_a", i, 1), ALU.subtract,
                                         ALU.mult))
                    link(V.scalar_tensor_tensor(km[:, i, :], km[:, i, :], 1.0, xs[:, 2 + i, :], ALU.add,
                                                ALU.mult))
                dve.wait_ge(rooted, 2)
                link(V.tensor_tensor(kk, kk, diff[:, 2:4, :], ALU.mult))
                for i in range(2):
                    V.scalar_tensor_tensor(xs[:, 2 + i, :], km[:, i, :], v("rwkv_r_k", i, 1),
                                           xs[:, i, :], ALU.mult, ALU.mult)
                dve.wait_ge(exped, 3)
                link(V.tensor_tensor(av, av, kk, ALU.mult))
                link(V.tensor_tensor(av, av, en, ALU.mult))
                link(V.tensor_tensor(km, km, en, ALU.mult))
                link(V.scalar_tensor_tensor(kk, kk, -1.0, ex, ALU.mult, ALU.mult))
                link(V.tensor_tensor(xs[:, 0:2, :], xs[:, 0:2, :], ei, ALU.mult))

            @block.scalar
            def _(act):
                act.wait_ge(shifted, 1)
                nc.scalar.activation(low[0:32, :], xs[0:32, 6, :], ACT.Tanh)
                nc.scalar.activation(low[32:64, :], xs[32:64, 6, :], ACT.Copy)
                nc.scalar.activation(low[64:128, :], xs[64:128, 6, :], ACT.Sigmoid).then_inc(low_done, 1)
                for i in range(2):
                    act.wait_ge(lora_done, 1)
                    nc.scalar.activation(lw[:, i, :], banks[i][:, :], ACT.Sigmoid,
                                         bias=v("rwkv_w0", i, 1)).then_inc(sigm, 1)
                    nc.scalar.activation(av[:, i, :], banks[2 + i][:, :], ACT.Sigmoid,
                                         bias=v("rwkv_a0", i, 1)).then_inc(sigm, 1)
                    nc.scalar.activation(gate[:, i, :], banks[4 + i][:, :], ACT.Copy)
                act.wait_ge(cum_done, 3)
                nc.scalar.activation(ex, diff[:, 4:6, :], ACT.Exp).then_inc(exped, 1)
                nc.scalar.activation(ei, cum, ACT.Exp).then_inc(exped, 1)
                nc.scalar.activation(en, cum, ACT.Exp, scale=-1.0).then_inc(exped, 1)
                for i in range(2):
                    act.wait_ge(inverted, i + 1)
                    nc.scalar.activation(diff[:, 2 + i, :], diff[:, 2 + i, :], ACT.Sqrt).then_inc(rooted, 1)

            @block.tensor
            def _(pe):
                for i in range(2):
                    pe.wait_ge(ssq, i + 1)
                    nc.tensor.matmul(banks[4 + i][:, :], lhsT=ones[:, :], rhs=diff[:, i, :], start=True,
                                     stop=True).then_inc(summed, 1)
                pe.wait_ge(low_done, 1)
                pe.wait_ge(inverted, 2)
                for r0, r1, b in ((0, 32, 0), (32, 64, 2), (64, 128, 4)):
                    for i in range(2):
                        last = nc.tensor.matmul(banks[b + i][:, :], lhsT=lora[r0:r1, i * P:(i + 1) * P],
                                                rhs=low[r0:r1, :], start=True, stop=True)
                last.then_inc(lora_done, 1)
    alpha, beta, kbar, rbar, prod = kk, av, km, xs[:, 0:2, :], xs[:, 2:4, :]
    vals = xs[:, 4:6, :]
    for pair in range(2):
        rwkv_pair(core, pair, dict(alpha=alpha[:, pair], beta=beta[:, pair], kbar=kbar[:, pair],
                                   rbar=rbar[:, pair], prod=prod[:, pair], vals=vals[:, pair],
                                   total=ei[:, pair], gate=gate[:, pair]), mix[:, 4 + pair, :], ident, cond)


def rwkv_pair(core, pair, f, out, ident, cond):
    nc, dram = core.nc, core.dram
    HALF = NCH // 2
    with Stage(core, f"rk{pair}") as st:
        def mats(name, n=P):
            return st.sb(name, [P, NCH, n])

        Ab, Bb, Kb, Rb, Vb, Qb = (mats(n) for n in ("alpha", "beta", "kbar", "rbar", "vals", "prod"))
        A, AT, AkT, RbT, RkT = (mats(n) for n in ("A", "AT", "AkT", "RbT", "RkT"))
        X, XT, Y2, Y2T, C2 = (mats(n) for n in ("X", "XT", "Y2", "Y2T", "C2"))
        V = mats("V", HD)
        AkV, U0 = mats("AkV", HD), mats("U0", HD)
        G = mats("G", HD)
        S = st.sb("S", [P, NCH + 1, HD])
        cons = {}
        for n in ("upper", "lower", "upper_eq", "blk16", "lvl32", "lvl64", "stack"):
            cons[n] = st.sb("c_" + n, [P, CONSTS[n][1]])
        lnw, lnb = st.sb("lnw", [P, HD]), st.sb("lnb", [P, HD])
        ones_col = st.sb("ones_col", [P, 1])
        bonus = st.sb("bonus", [P, NCH])
        stats = st.sb("stats", [P, NCH, 6])
        mv = st.sb("mv", [P, NCH, 2])
        rs = st.sb("rs", [P, NCH])
        ln_rows = [(t[h * HD:(h + 1) * HD, :],
                    bass.AP(dram[n].tensor, pair * P + h * HD, [[0, HD], [1, HD]]))
                   for t, n in ((lnw, "rwkv_ln_w"), (lnb, "rwkv_ln_b")) for h in range(2)]
        load(core, f"rk{pair}_c", [(cons[n][:, :], const(core, n)) for n in cons] + ln_rows)
        with core.block() as block:
            @block.gpsimd
            def _(pool):
                for t in (Ab, Bb, Kb):
                    nc.gpsimd.memset(t[:, :, :], 0.0)

            @block.vector
            def _(dve):
                for t in (Rb, Vb, Qb):
                    nc.vector.memset(t[:, :, :], 0.0)
                nc.vector.memset(S[:, 0, :], 0.0)
                nc.vector.memset(ones_col[:, :], 1.0)
        with core.block() as block:
            @block.vector
            def _(dve):
                for h in range(2):
                    r = slice(h * HD, (h + 1) * HD)
                    for t, n in ((Ab, "alpha"), (Bb, "beta"), (Kb, "kbar")):
                        nc.vector.tensor_copy(t[r, :, r], f[n][r, :].rearrange("p (c t) -> p c t", c=NCH))

            @block.scalar
            def _(act):
                for h in range(2):
                    r = slice(h * HD, (h + 1) * HD)
                    for t, n in ((Rb, "rbar"), (Vb, "vals"), (Qb, "prod")):
                        nc.scalar.activation(t[r, :, r], f[n][r, :].rearrange("p (c t) -> p c t", c=NCH),
                                             ACT.Copy)
        I = ident
        eye = ident[:, :].unsqueeze(1).to_broadcast([P, HALF, P])

        def mask(n):
            return cons[n][:, :].unsqueeze(1).to_broadcast([P, HALF, P])

        MASK, ADD, COPY = "mask", "add", "copy"
        steps = [
            (Bb, Ab, MASK, "upper", AT), (Ab, Bb, MASK, "lower", A),
            (Kb, Ab, MASK, "upper", AkT), (Bb, Rb, MASK, "upper_eq", RbT),
            (Kb, Rb, MASK, "upper_eq", RkT),
            (Vb, cons["stack"], COPY, None, V),
        ]
        products(core, f"rk{pair}_a", steps, mask, cond)
        D1, D1T, C1, C1T = Y2, Y2T, A, AT
        with core.block() as block:
            @block.vector
            def _(dve):
                link = core.dve_link.on(dve)
                full = [P, NCH, P]

                def m(n):
                    return cons[n][:, :].unsqueeze(1).to_broadcast(full)

                E = ident[:, :].unsqueeze(1).to_broadcast(full)
                for src, d, x in ((A, D1, X), (AT, D1T, XT)):
                    link(nc.vector.tensor_tensor(d[:, :, :], src[:, :, :], m("blk16"), ALU.mult))
                    link(nc.vector.tensor_tensor(x[:, :, :], d[:, :, :], E, ALU.add))
                link(nc.vector.tensor_tensor(C2[:, :, :], A[:, :, :], m("lvl64"), ALU.mult))
                link(nc.vector.tensor_tensor(A[:, :, :], A[:, :, :], m("lvl32"), ALU.mult))
                link(nc.vector.tensor_tensor(AT[:, :, :], AT[:, :, :], m("lvl32"), ALU.mult))
        Z, ZT = mats("Z"), mats("ZT")
        W, WT = Ab, mats("WT")
        steps = []
        d, dT, e, eT = D1, D1T, Z, ZT
        for _ in range(3):
            steps += [(dT, d, COPY, None, e), (d, dT, COPY, None, eT),
                      (XT, e, ADD, X, X), (e, XT, ADD, XT, XT)]
            d, dT, e, eT = e, eT, d, dT
        steps += [(C1T, X, COPY, None, d), (C1, XT, COPY, None, dT),
                  (XT, d, ADD, X, e), (X, dT, ADD, XT, eT),
                  (C2, eT, COPY, None, d), (e, d, ADD, eT, X)]
        TT = X
        At, Bt, Kt = d, dT, e
        steps += [(Ab, I, COPY, None, XT), (Bb, I, COPY, None, Y2T), (Kb, I, COPY, None, AT)]
        At, Bt, Kt = XT, Y2T, AT
        steps += [(AkT, V, COPY, None, AkV), (TT, AkV, COPY, None, U0),
                  (TT, At, COPY, None, W), (At, TT, COPY, None, WT),
                  (W, Bt, ADD, eye, AkT)]
        M1T = AkT
        products(core, f"rk{pair}_b", steps, mask, cond)
        total = f["total"].rearrange("p (c t) -> p c t", c=NCH)[:, :, CH - 1:CH]
        banks_needed = 7
        with Stage(core, f"rk{pair}_s") as ss:
            banks = ss.banks(banks_needed)
            g_ready, g_done, m_ready, s_done = (ss.sem("g_ready"), ss.sem("g_done"), ss.sem("m_ready"),
                                                ss.sem("s_done"))
            u_ready, u_done, y_ready, b_ready = (ss.sem("u_ready"), ss.sem("u_done"), ss.sem("y_ready"),
                                                 ss.sem("b_ready"))
            norm, root, gain_done, turned = (ss.sem("norm"), ss.sem("root"), ss.sem("gain"),
                                             ss.sem("turned"))
            U, Yt = G, U0
            with core.block() as block:
                @block.tensor
                def _(pe):
                    T = nc.tensor
                    for c in range(NCH):
                        g = banks[0][:, c * HD:(c + 1) * HD]
                        T.matmul(g, lhsT=Bt[:, c, :], rhs=U0[:, c, :], start=True, stop=False,
                                 skip_group_check=True)
                        last = T.matmul(g, lhsT=Kt[:, c, :], rhs=V[:, c, :], start=False, stop=True,
                                        skip_group_check=True)
                    last.then_inc(g_ready, 1)
                    for c in range(NCH):
                        last = T.matmul(banks[4][:, c:c + 1], lhsT=Qb[:, c, :], rhs=ones_col[:, 0:1],
                                        start=True, stop=True,
                                        skip_group_check=True)
                    last.then_inc(b_ready, 1)
                    for c in range(NCH):
                        if c >= 1:
                            pe.wait_ge(s_done, c)
                        else:
                            pe.wait_ge(g_done, 1)
                        T.matmul(banks[1 + c % 2][:, 0:HD], lhsT=M1T[:, c, :], rhs=S[:, c, :],
                                 start=True, stop=True).then_inc(m_ready, 1)
                    for c in range(NCH):
                        last = T.matmul(banks[3][:, c * HD:(c + 1) * HD], lhsT=WT[:, c, :],
                                        rhs=S[:, c, :], start=True, stop=True, skip_group_check=True)
                    last.then_inc(u_ready, 1)
                    pe.wait_ge(u_done, 1)
                    for c in range(NCH):
                        y = banks[5][:, c * HD:(c + 1) * HD]
                        T.matmul(y, lhsT=Rb[:, c, :], rhs=S[:, c, :], start=True, stop=False,
                                 skip_group_check=True)
                        T.matmul(y, lhsT=RbT[:, c, :], rhs=U[:, c, :], start=False, stop=False,
                                 skip_group_check=True)
                        last = T.matmul(y, lhsT=RkT[:, c, :], rhs=V[:, c, :], start=False, stop=True,
                                        skip_group_check=True)
                    last.then_inc(y_ready, 1)
                    pe.wait_ge(gain_done, 1)
                    for c in range(NCH):
                        last = T.matmul(banks[6][:, c * HD:(c + 1) * HD], lhsT=Vb[:, c, :],
                                        rhs=cons["stack"][:, :], start=True, stop=True,
                                        skip_group_check=True)
                    last.then_inc(turned, 1)

                @block.vector
                def _(dve):
                    link = core.dve_link.on(dve)
                    W_ = nc.vector
                    wide = [P, NCH, HD]

                    def bank(i):
                        return banks[i][:, :].rearrange("p (c v) -> p c v", c=NCH)

                    dve.wait_ge(g_ready, 1)
                    W_.tensor_tensor(G[:, :, :], bank(0), total.to_broadcast(wide), ALU.mult)\
                      .then_inc(g_done, 1)
                    dve.wait_ge(g_done, 1)
                    for c in range(NCH):
                        dve.wait_ge(m_ready, c + 1)
                        W_.scalar_tensor_tensor(S[:, c + 1, :], banks[1 + c % 2][:, 0:HD],
                                                total[:, c, :], G[:, c, :], ALU.mult, ALU.add)\
                          .then_inc(s_done, 1)
                    dve.wait_ge(s_done, NCH)
                    dve.wait_ge(u_ready, 1)
                    W_.tensor_tensor(U[:, :, :], bank(3), U0[:, :, :], ALU.add).then_inc(u_done, 1)
                    dve.wait_ge(b_ready, 1)
                    link(W_.tensor_copy(bonus[:, :], banks[4][:, 0:NCH]))
                    dve.wait_ge(y_ready, 1)
                    link(W_.tensor_copy(Yt[:, :, :], bank(5)))
                    for c in range(NCH):
                        link(W_.bn_stats(stats[:, c, :], Yt[:, c, :]))
                        link(W_.bn_aggr(mv[:, c, :], stats[:, c, :]))
                    link(W_.tensor_scalar(rs[:, :], mv[:, :, 1], HD * 1e-5, None, ALU.add))
                    W_.reciprocal(rs[:, :], rs[:, :]).then_inc(norm, 1)
                    link(W_.tensor_tensor(Yt[:, :, :], Yt[:, :, :], mv[:, :, 0:1].to_broadcast(wide),
                                          ALU.subtract))
                    dve.wait_ge(root, 1)
                    link(W_.tensor_tensor(Yt[:, :, :], Yt[:, :, :],
                                          rs[:, :].unsqueeze(2).to_broadcast(wide), ALU.mult))
                    link(W_.tensor_tensor(Yt[:, :, :], Yt[:, :, :],
                                          lnw[:, :].unsqueeze(1).to_broadcast(wide), ALU.mult))
                    link(W_.tensor_tensor(Yt[:, :, :], Yt[:, :, :],
                                          lnb[:, :].unsqueeze(1).to_broadcast(wide), ALU.add))
                    link(W_.tensor_tensor(V[:, :, :], V[:, :, :],
                                          bonus[:, :].unsqueeze(2).to_broadcast(wide), ALU.mult))
                    for h in range(2):
                        r = slice(h * HD, (h + 1) * HD)
                        ins = W_.tensor_tensor(Vb[r, :, r], Yt[r, :, :], V[r, :, :], ALU.add)
                        link(ins) if h == 0 else ins.then_inc(gain_done, 1)
                    dve.wait_ge(turned, 1)
                    W_.tensor_tensor(out, banks[6][:, :], f["gate"], ALU.mult)

                @block.scalar
                def _(act):
                    act.wait_ge(norm, 1)
                    nc.scalar.activation(rs[:, :], rs[:, :], ACT.Sqrt).then_inc(root, 1)


def products(core, name, steps, mask, cond):
    nc = core.nc
    HALF = NCH // 2
    with Stage(core, name) as st:
        banks = st.banks(4)
        multiplied, written = st.sem("multiplied"), st.sem("written")
        turns = [(step, h) for step in steps for h in range(2)]
        with core.block() as block:
            @block.sync
            def _(sp):
                cond.send(sp, len(turns) // 2)

            @block.tensor
            def _(pe):
                for n, ((lhsT, rhs, how, arg, dst), h) in enumerate(turns):
                    if n >= 2:
                        pe.wait_ge(written, n - 1)
                    w = dst.shape[2]
                    for c in range(HALF):
                        cc = h * HALF + c
                        last = nc.tensor.matmul(
                            banks[n % 4][:, c * w:(c + 1) * w], lhsT=lhsT[:, cc, :],
                            rhs=rhs[:, cc, :] if len(rhs.shape) == 3 else rhs[:, :], start=True,
                            stop=True, skip_group_check=True)
                    last.then_inc(multiplied, 1)
                    if n % 2:
                        cond.take(pe)

            @block.vector
            def _(dve):
                for n, ((lhsT, rhs, how, arg, dst), h) in enumerate(turns):
                    dve.wait_ge(multiplied, n + 1)
                    w = dst.shape[2]
                    part = slice(h * HALF, (h + 1) * HALF)
                    ps = banks[n % 4][:, 0:HALF * w].rearrange("p (c v) -> p c v", c=HALF)
                    if how == "mask":
                        ins = nc.vector.tensor_tensor(dst[:, part, :], ps, mask(arg), ALU.mult)
                    elif how == "add":
                        other = arg if arg.shape[1] == HALF else arg[:, part, :]
                        ins = nc.vector.tensor_tensor(dst[:, part, :], ps, other, ALU.add)
                    else:
                        ins = nc.vector.tensor_copy(dst[:, part, :], ps)
                    ins.then_inc(written, 1)


def modulation(core, cond, vec, mods):
    nc = core.nc
    with core.block() as block:
        @block.sync
        def _(sp):
            cond.send(sp, cond.left())

        @block.tensor
        def _(pe):
            while cond.left():
                cond.take(pe)

        @block.vector
        def _(dve):
            link = core.dve_link.on(dve)
            dve.wait_ge(cond.done, len(cond.chunks))
            for layer, mod in enumerate(mods):
                at = VEC_AT["ada_b_2"] + 48 * layer
                link(nc.vector.tensor_tensor(
                    mod[:, :, :], cond.bank[:, 96 * layer:96 * (layer + 1)].rearrange("p (j s) -> p s j", s=2),
                    vec[:, at:at + 48].unsqueeze(1).to_broadcast([P, 2, 48]), ALU.add))
                for which, g in ((1, 0), (4, 2)):
                    for s in range(2):
                        m = mod[:, s, which * KD:(which + 1) * KD]
                        nc.vector.scalar_tensor_tensor(m, m, 1.0, gain_of(vec, layer, g), ALU.add,
                                                       ALU.mult)


def gain_of(vec, layer, i):
    g = VEC_AT["norm_g_2"] + KD * (4 * layer + i)
    return vec[:, g:g + KD]


def gate_rows(core, name, layer, which, i, vec, mod, rows, ident):
    nc = core.nc
    n = rows.shape[1]
    with Stage(core, name) as st:
        banks = st.banks(2 * n)
        gated = st.sb("gated", [P, n, KD])
        gates, spread = st.sem("gates"), st.sem("spread")
        with core.block() as block:
            @block.vector
            def _(dve):
                nc.vector.tensor_tensor(gated[:, :, :], mod[:, 0:n, which * KD:(which + 1) * KD],
                                        gain_of(vec, layer, i).unsqueeze(1).to_broadcast([P, n, KD]),
                                        ALU.mult).then_inc(gates, 1)
                for b in range(2 * n):
                    dve.wait_ge(spread, b + 1)
                    nc.vector.tensor_copy(rows[:, b // 2, (b % 2) * BANK:(b % 2 + 1) * BANK], banks[b][:, :])

            @block.tensor
            def _(pe):
                pe.wait_ge(gates, 1)
                for b in range(2 * n):
                    for k in range(4):
                        kk = (b % 2) * 4 + k
                        last = nc.tensor.matmul(banks[b][:, k * P:(k + 1) * P],
                                                lhsT=gated[:, b // 2, kk:kk + 1].to_broadcast([P, P]),
                                                rhs=ident[:, :], start=True, stop=True,
                                                skip_group_check=True)
                    last.then_inc(spread, 1)


def rotate(core, name, tiles, rot, cos, sin):
    nc = core.nc
    with Stage(core, name) as st:
        banks = st.banks(4)
        r, c, s = st.sb("rot", [P, P]), st.sb("cos", [P, SEQ]), st.sb("sin", [P, SEQ])
        tmp = st.sb("tmp", [P, 2, SEQ])
        load(core, name + "_c", [(r[:, :], const(core, rot)), (c[:, :], const(core, cos)),
                                 (s[:, :], const(core, sin))])
        swapped, done = st.sem("swapped"), st.sem("done")
        with core.block() as block:
            @block.tensor
            def _(pe):
                for i, (whole, part) in enumerate(tiles):
                    if i >= 4:
                        pe.wait_ge(done, i - 3)
                    n = whole.shape[0]
                    nc.tensor.matmul(banks[i % 4][0:n, :], lhsT=r[0:n, 0:n], rhs=whole, start=True,
                                     stop=True).then_inc(swapped, 1)

            @block.vector
            def _(dve):
                link = core.dve_link.on(dve)
                for i, (whole, part) in enumerate(tiles):
                    a = part.start_partition()
                    q = slice(a, a + part.shape[0])
                    dve.wait_ge(swapped, i + 1)
                    nc.vector.tensor_tensor(tmp[q, i % 2, :], banks[i % 4][q, :], s[q, :], ALU.mult)
                    link(nc.vector.tensor_tensor(part, part, c[q, :], ALU.mult))
                    last = nc.vector.tensor_tensor(part, part, tmp[q, i % 2, :], ALU.add)
                    last.then_inc(done, 1)
                    dve.wait_ge(done, i + 1)


def window_and_diff(core, get_input, o_tok, ident):
    nc, dram = core.nc, core.dram
    T_QAW, T_QD, T_KAW, T_VAW, T_KD, T_VD = 0, 4, 8, 9, 10, 14
    with Stage(core, "ab") as st:
        p = st.sb("p", [P, 18, ALL])
        with Stage(core, "ab_h") as sh:
            ring = o_tok.rearrange("p t d -> p (t d)").rearrange("p (s k c) -> p s k c", s=W_SLOTS,
                                                                 k=KD)
            h = get_input(sh)
            linear(core, "ab_in", dram["ab_w_in_2"][0], [h[0:SEQ], h[SEQ:ALL]], "features",
                   copy_out(nc, lambda s, t, c, cw: p[:, t, SEQ * s:(SEQ, ALL)[s]]), ring=ring)
        v = st.sb("v", [P, NX + NC_, 5 * P])
        turn(core, "ab_v", [g for t in range(NX + NC_) for g in (
            ([p[:, f, t * P:(t + 1) * P] for f in (T_VAW, T_VD, T_VD + 1, T_VD + 2)],
             v[:, t, 0:4 * P].rearrange("p (b c) -> p b c", b=4), None),
            ([p[:, T_VD + 3, t * P:(t + 1) * P]], v[:, t, 4 * P:5 * P].unsqueeze(1), None))], ident)
        rotate(core, "ab_r", [(p[:, f, 0:SEQ],) * 2 for f in (*range(T_QAW, T_KAW + 1),
                                                               *range(T_KD, T_VD))],
               "rot64", "cos64", "sin64")
        small = st.sb("small", [P, 8])
        keep = st.sb("keep", [P, 2, P])
        lv = st.sb("lv", [P, 4, HD])
        lam = st.sb("lam", [P, 4])
        gain = st.sb("gain", [P, P])
        load(core, "ab_c", [(small[:, :], bass.AP(dram["ab_sink_2"].tensor, 0, [[0, P], [1, 8]])),
                            (keep[:, 0, :], const(core, "keep_before")),
                            (keep[:, 1, :], const(core, "keep_after")),
                            (lv[:, :, :], bass.AP(dram["diff_lambda_2"].tensor, 0,
                                                  [[0, P], [HD, 4], [1, HD]])),
                            (gain[:, :], bass.AP(dram["diff_subln_g_2"].tensor, 0, [[0, P], [1, P]]))])
        dots, exps = st.sem("dots"), st.sem("exps")
        lam0 = 0.8 - 0.6
        with core.block() as block:
            @block.vector
            def _(dve):
                link = core.dve_link.on(dve)
                link(nc.vector.tensor_scalar(small[:, :], small[:, :], -1.0, None, ALU.mult))
                for i in range(2):
                    link(nc.vector.tensor_tensor(lv[:, 2 * i, :], lv[:, 2 * i, :], lv[:, 2 * i + 1, :],
                                                 ALU.mult))
                    link(nc.vector.reduce_sum(lam[:, i:i + 1], lv[:, 2 * i, :], AX.X))
                nc.vector.sem_inc(dots, 1)
                dve.wait_ge(exps, 1)
                link(nc.vector.tensor_tensor(lam[:, 2:3], lam[:, 0:1], lam[:, 1:2], ALU.subtract))
                link(nc.vector.tensor_scalar(lam[:, 2:3], lam[:, 2:3], lam0, None, ALU.add))

            @block.scalar
            def _(act):
                act.wait_ge(dots, 1)
                nc.scalar.activation(lam[:, 0:2], lam[:, 0:2], ACT.Exp).then_inc(exps, 1)
        jobs = []
        ctx_blocks = list(range(NX, NX + NC_))
        for h in range(8):
            rq = slice(HD * (h % 2), HD * (h % 2) + HD)
            kv = h // 4
            for t in range(NX + NC_):
                near = [b for b in (t - 1, t, t + 1) if 0 <= b < NX] if t < NX else []
                bias = []
                if t < NX:
                    if t >= 1:
                        bias.append((0, ident[:, :], keep[:, 0, :]))
                    if t + 1 < NX:
                        bias.append((P * (len(near) - 1), ident[:, :], keep[:, 1, :]))
                key = [p[rq, T_KAW, b * P:(b + 1) * P] for b in near] + [p[rq, T_KAW, SEQ:ALL]]
                if kv != h % 2:
                    key = [p[rq, T_VAW, b * P:(b + 1) * P] for b in near] + [p[rq, T_VAW, SEQ:ALL]]
                jobs.append(dict(q=p[rq, T_QAW + h // 2, t * P:(t + 1) * P], keys=key, bias=bias,
                                 hide=None,
                                 values=[v[:, b, kv * HD:(kv + 1) * HD] for b in near + ctx_blocks],
                                 scale=HD ** -0.5, sink=small[:, h:h + 1],
                                 out=o_tok[:, t, h * HD:(h + 1) * HD], minus=None))
        for h in range(4):
            for t in range(NX + NC_):
                blocks = list(range(NX + NC_)) if t < NX else ctx_blocks
                out = o_tok[:, t, BANK + h * P:BANK + (h + 1) * P]
                for m in range(2):
                    rq = slice(HD * m, HD * m + HD)
                    jobs.append(dict(q=p[rq, T_QD + h, t * P:(t + 1) * P],
                                     keys=[p[rq, T_KD + h, blocks[0] * P:ALL]], bias=[], hide=None,
                                     values=[v[:, b, (1 + h) * P:(2 + h) * P] for b in blocks],
                                     scale=HD ** -0.5, sink=None, out=out,
                                     minus=(lam[:, 2:3], out) if m else None))
        swapped_in, swapped_out = st.sem("swapped_in"), st.sem("swapped_out")
        with core.block() as block:
            @block.sync
            def _(sp):
                sp.dma_start(p[0:HD, T_VAW, :], p[HD:P, T_KAW, :]).then_inc(swapped_in, 16)
                sp.dma_start(p[HD:P, T_VAW, :], p[0:HD, T_KAW, :]).then_inc(swapped_in, 16)
                sp.wait_ge(swapped_in, 32)
        attend(core, "ab_at", jobs, ident)
        total = st.sb("total", [P, 24])
        sq = st.sb("sq", [P, P])
        summed, inverted, rooted = st.sem("summed"), st.sem("inverted"), st.sem("rooted")
        with core.block() as block:
            cells = [o_tok[:, t, BANK + h * P:BANK + (h + 1) * P] for t in range(NX + NC_)
                     for h in range(4)]

            @block.scalar
            def _(act):
                link = core.act_link.on(act)
                for i, o in enumerate(cells):
                    link(nc.scalar.activation(sq[:, :], o, ACT.Square, accum_out=total[:, i:i + 1]))
                nc.scalar.sem_inc(summed, 1)
                act.wait_ge(inverted, 1)
                nc.scalar.activation(total[:, :], total[:, :], ACT.Sqrt).then_inc(rooted, 1)

            @block.vector
            def _(dve):
                link = core.dve_link.on(dve)
                link(nc.vector.tensor_scalar(gain[:, :], gain[:, :], 1.0 - lam0, None, ALU.mult))
                dve.wait_ge(summed, 1)
                invert_mean(core, link, total[:, :], P).then_inc(inverted, 1)
                dve.wait_ge(rooted, 1)
                for i, o in enumerate(cells):
                    nc.vector.scalar_tensor_tensor(o, o, total[:, i:i + 1], gain[:, :], ALU.mult,
                                                   ALU.mult)


def latent(core, get_input, o_tok, vec, ident):
    nc, dram = core.nc, core.dram
    QL, KL, NH, NOPE, ROPE = 384, 256, 16, 64, 32
    DK = NOPE + ROPE
    NT = NX + NC_
    with Stage(core, "la") as st:
        pq = core.pair(st.stack.enter_context(Stage(core, "la_pq")), 3, SEQ)
        pkv = core.pair(st.stack.enter_context(Stage(core, "la_pkv")), 2, ALL)
        rope = st.sb("rope", [DK, ALL])
        if True:
            with Stage(core, "lc") as s3:
                ptok = s3.sb("ptok", [P, NT, QL + KL + ROPE])
                w = dram["mla_w_in_2"][0]
                with Stage(core, "la_h") as sh:
                    h = get_input(sh)
                    linear(core, "la_q", w, [h[0:SEQ]], "tokens",
                           copy_out(nc, lambda s, t, c, cw: ptok[:, t, 0:cw]), cols=QL, width=QL,
                           kchunk=4)
                    linear(core, "la_k", w, [h[0:ALL]], "tokens",
                           copy_out(nc, lambda s, t, c, cw: ptok[:, t, QL:QL + cw]), col0=QL,
                           width=KL + ROPE, kchunk=4)
                turn(core, "la_r", [([ptok[:, t, QL + KL - NOPE:QL + KL + ROPE]],
                                     rope[NOPE:DK, t * P:(t + 1) * P].unsqueeze(1), None)
                                    for t in range(NT)], ident)
                gq, gk = VEC_AT["mla_q_norm_g_2"], VEC_AT["mla_kv_norm_g_2"]
                norm_to_features(core, "la_nq", [(ptok[:, t, 0:QL], pq[t * P:(t + 1) * P],
                                                  vec[:, gq:gq + 3], None) for t in range(NX)], ident)
                norm_to_features(core, "la_nk", [(ptok[:, t, QL:QL + KL], pkv[t * P:(t + 1) * P],
                                                  vec[:, gk:gk + 2], None) for t in range(NT)], ident)
            qT = st.sb("qT", [DK, NH, SEQ])
            kT = st.sb("kT", [DK, NH, ALL])
            linear(core, "la_wq", dram["mla_wq_b_2"][0], [pq[0:SEQ]], "features",
                   copy_out(nc, lambda s, t, c, cw: qT[:, t, :]), width=2 * DK, out_tile=DK)
            wkv = dram["mla_wkv_b_2"][0]
            srcs = [pkv[0:SEQ], pkv[SEQ:ALL]]

            def keys(eng, ps, s, t, c, cw):
                return nc.scalar.activation(kT[0:NOPE, t, SEQ * s:(SEQ, ALL)[s]],
                                            ps[0:NOPE], ACT.Copy)

            linear(core, "la_wk", wkv, srcs, "features", keys)
            tiles = [(qT[:, h, :], qT[NOPE:DK, h, :]) for h in range(NH)]
            with core.block() as block:
                @block.vector
                def _(dve):
                    nc.vector.memset(rope[0:NOPE, :], 0.0)
            tiles.append((rope[:, 0:SEQ], rope[NOPE:DK, 0:SEQ]))
            rotate(core, "la_rot", tiles, "rot32", "cos32", "sin32")
            with core.block() as block:
                @block.vector
                def _(dve):
                    for h in range(0, NH, 2):
                        nc.vector.tensor_copy(kT[NOPE:DK, h, :], rope[NOPE:DK, :])

                @block.scalar
                def _(act):
                    for h in range(1, NH, 2):
                        nc.scalar.activation(kT[NOPE:DK, h, :], rope[NOPE:DK, :], ACT.Copy)
            v = core.values
            def vals(eng, ps, s, t, c, cw):
                src = ps.rearrange("p (h z) -> p h z", z=P)[:, :, NOPE:P]
                h0 = c // P
                return nc.scalar.activation(v[:, t, h0 * HD:(h0 + cw // P) * HD]
                                            .rearrange("p (h z) -> p h z", z=HD), src, ACT.Copy)
            linear(core, "la_wv", wkv, [pkv[0:ALL]], "tokens", vals)
        jobs = [dict(q=qT[:, h, t * P:(t + 1) * P], keys=[kT[:, h, :]], bias=[], hide=None,
                     values=[v[:, b, h * HD:(h + 1) * HD] for b in range(NT)],
                     scale=DK ** -0.5, sink=None, out=o_tok[:, t, h * HD:(h + 1) * HD], minus=None)
                for h in range(NH) for t in range(NX)]
        attend(core, "la_at", jobs, ident)


def program(nc, dram, out, upto=99):
    with ExitStack() as stack:
        core = Core(nc, stack, dram)

        def sb(name, shape):
            return stack.enter_context(nc.sbuf_tensor(name, shape, F32))

        ident = sb("ident", [P, P])
        vec = sb("vec", [P, N_VEC])
        x = sb("x", [P, NX, D])
        feat = sb("feat", [P, KD, ALL])

        class Pair:

            def __init__(self, stage, kt, n):
                self.hi, self.lo = (stage.sb(m, [P, kt, n], F32R) for m in ("hi", "lo"))

            def __getitem__(self, cols):
                return self.hi[:, :, cols], self.lo[:, :, cols]

        core.pair = Pair
        tok = feat[:, :, :].rearrange("p k t -> p (k t)").rearrange("p (t d) -> p t d", d=D)

        n_rows = (N_VEC + P - 1) // P
        with Stage(core, "vec") as st:
            rows_sb = st.sb("rows", [P, n_rows, P])
            cleared, loaded = st.sem("cleared"), st.sem("loaded")
            with core.block() as block:
                @block.vector
                def _(dve):
                    nc.vector.memset(rows_sb[:, :, :], 0.0).then_inc(cleared, 1)

                @block.sync
                def _(sp):
                    sp.dma_start(ident[:, :], const(core, "ident")).then_inc(loaded, 16)
                    sp.dma_start(x[:, :, :], dram["x"][0].rearrange("(t p) d -> p t d", p=P))\
                      .then_inc(loaded, 16)
                    sp.wait_ge(cleared, 1)
                    n = 2
                    for name, rows in VECTORS:
                        at, r = VEC_AT[name], 0
                        while r < rows:
                            m = min(rows - r, P - (at + r) % P)
                            src = bass.AP(dram[name].tensor, r * P, [[P, m], [1, P]])
                            p0 = (at + r) % P
                            sp.dma_start(rows_sb[p0:p0 + m, (at + r) // P, :], src).then_inc(loaded, 16)
                            r, n = r + m, n + 1
                    sp.wait_ge(loaded, 16 * n)
            turn(core, "vec_t", [([rows_sb[:, i, :]],
                                  vec[:, i * P:min(N_VEC, (i + 1) * P)].unsqueeze(1), None)
                                 for i in range(n_rows)], ident)

        def v(name, i=0, n=KD):
            return vec[:, VEC_AT[name] + i:VEC_AT[name] + i + n]

        def tok_tile(t):
            return tok[:, t, :]

        silu_c = sb("silu_c", [P, KD, 2])
        mods = [sb(f"mod{i}", [P, 2, 48]) for i in range(2)]
        with core.block() as block:
            @block.scalar
            def _(act):
                for s, name in enumerate(("c_2", "c_ctx_2")):
                    nc.scalar.activation(silu_c[:, :, s], v(name), ACT.Silu)

        with Stage(core, "m1") as st:
            proj = st.sb("proj", [P, N_PROJ, SEQ])
            with Stage(core, "m0") as s0:
                h = Pair(s0, KD, SEQ)
                norm_to_features(core, "n1", [(x[:, t, :], h[t * P:(t + 1) * P], v("norm_mix_pre"), None)
                                              for t in range(NX)], ident)
                linear(core, "w_in", dram["w_in"][0], [h[0:SEQ]], "features",
                       copy_out(nc, lambda s, t, c, cw: proj[:, t, :]))
            if upto == 1:
                return
            mix = feat
            chunk_attention(core, proj, mix[:, :, 0:SEQ], ident)
            rglru(core, proj, mix[:, :, 0:SEQ], vec)
            with Stage(core, "ada") as sa:
                cond = Conditioning(core, sa, silu_c)
                hgrn(core, proj, mix[:, :, 0:SEQ], vec, ident, cond)
                rwkv(core, proj, mix[:, :, 0:SEQ], vec, ident, cond)
                modulation(core, cond, vec, mods)
            if upto == 2:
                return
        with Stage(core, "o1") as st:
            row = st.sb("row", [P, 2, D])
            load(core, "o1_c", [(row[:, i, :], bass.AP(dram[n].tensor, 0, [[0, P], [1, D]]))
                                for i, n in enumerate(("norm_mix_post", "norm_mlp_post"))])
            with Stage(core, "o0") as s2:
                y = s2.sb("y", [P, NX, D])
                linear(core, "w_out", dram["w_out"][0], [feat[:, :, 0:SEQ]], "tokens",
                       copy_out(nc, lambda s, t, c, cw: y[:, t, c:c + cw]))
                add_normed(core, "r1", [(y[:, t, :], x[:, t, :], row[:, 0, :]) for t in range(NX)])
            if upto == 3:
                return
            with Stage(core, "mlp") as s2:
                ff = s2.sb("ff", [P, MLP // P, SEQ])
                relu = s2.sb("relu", [P, 2, SEQ])
                def squared_relu(eng, ps, s, t, c, cw):
                    link = core.dve_link.on(eng)
                    link(nc.vector.tensor_scalar(relu[:, t % 2, :], ps, 0.0, None, ALU.max))
                    return nc.vector.tensor_tensor(ff[:, t, :], relu[:, t % 2, :], relu[:, t % 2, :],
                                                   ALU.mult)

                with Stage(core, "mlph") as s3:
                    h = Pair(s3, KD, SEQ)
                    norm_to_features(core, "n2", [(x[:, t, :], h[t * P:(t + 1) * P],
                                                   v("norm_mlp_pre"), None) for t in range(NX)], ident)
                    linear(core, "w1", dram["mlp_w1"][0], [h[0:SEQ]], "features", squared_relu,
                           engine="dve", kchunk=4)
                linear(core, "w2", dram["mlp_w2"][0], [ff[:, :, :]], "tokens",
                       copy_out(nc, lambda s, t, c, cw: tok[:, t, c:c + cw]))
            add_normed(core, "r2", [(tok[:, t, :], x[:, t, :], row[:, 1, :]) for t in range(NX)])
        if upto == 4:
            return

        ctx = sb("ctx", [P, NC_, D])
        load(core, "ctx", [(ctx[:, :, :], dram["ctx_2"][0].rearrange("(t p) d -> p t d", p=P))])
        core.values = None
        for layer in range(2):
            last = layer == 1
            nt = NX if last else NX + NC_
            L = f"l{layer}"
            mod = mods[layer]

            def stream(t):
                return x[:, t, :] if t < NX else ctx[:, t - NX, :]

            def normed(name, which, tiles, h):
                norm_to_features(core, name, [
                    (stream(t), h[t * P:(t + 1) * P],
                     mod[:, int(t >= NX), (which + 1) * KD:(which + 2) * KD],
                     mod[:, int(t >= NX), which * KD:(which + 1) * KD]) for t in range(tiles)], ident)

            def attention_input(stage):
                h = Pair(stage, KD, ALL)
                normed(L + "n1", 0, NX + NC_, h)
                return h

            if last:
                with Stage(core, "lv") as sv:
                    core.values = sv.sb("values", [P, NX + NC_, D])
                    latent(core, attention_input, tok, vec, ident)
                w_out = dram["mla_w_out_2"][0]
            else:
                window_and_diff(core, attention_input, tok, ident)
                w_out = dram["ab_w_out_2"][0]
            if upto == 6:
                return
            with Stage(core, L + "o") as so:
                oT = so.sb("oT", [P, KD, nt * P])
                turn(core, L + "t", [([tok[:, t, (4 * g + i) * P:(4 * g + i + 1) * P] for i in range(4)],
                                      oT[:, 4 * g:4 * g + 4, t * P:(t + 1) * P], None)
                                     for t in range(nt) for g in range(2)], ident)
                linear(core, L + "wo", w_out, [oT[:, :, :]], "tokens",
                       copy_out(nc, lambda s, t, c, cw: tok[:, t, c:c + cw]))
            with Stage(core, L + "g1") as sg:
                rows = sg.sb("rows", [P, 1 if last else 2, D])
                gate_rows(core, L + "s1", layer, 2, 1, vec, mod, rows, ident)
                add_normed(core, L + "r1", [(tok_tile(t), stream(t), rows[:, int(t >= NX), :])
                                            for t in range(nt)])
            with Stage(core, L + "f") as sf:
                ff = sf.sb("ff", [P, FFN // P, nt * P])
                parts = [slice(0, SEQ)] + ([] if last else [slice(SEQ, ALL)])
                with Stage(core, L + "fh") as sh:
                    h = Pair(sh, KD, nt * P)
                    normed(L + "n2", 3, nt, h)
                    raw = feat[:, :, :].rearrange("p k t -> p (k t)")\
                        .rearrange("p (s h k c) -> p s h k c", s=3, h=2, c=P)
                    gated_up(core, L + "w13", dram["ffn_w13_2"][layer], [h[s] for s in parts],
                             [ff[:, :, s] for s in parts], raw)
                linear(core, L + "w2", dram["ffn_w2_2"][layer], [ff[:, :, :]], "tokens",
                       copy_out(nc, lambda s, t, c, cw: tok[:, t, c:c + cw]))
            with Stage(core, L + "g2") as sg:
                rows = sg.sb("rows", [P, 1 if last else 2, D])
                gate_rows(core, L + "s2", layer, 5, 3, vec, mod, rows, ident)
                add_normed(core, L + "r2", [(tok_tile(t), stream(t), rows[:, int(t >= NX), :])
                                            for t in range(nt)])
            if upto == 8:
                return
        stored = stack.enter_context(nc.semaphore("stored"))
        with core.block() as block:
            @block.sync
            def _(sp):
                sp.dma_start(out[0].rearrange("(t p) d -> p t d", p=P), x[:, :, :]).then_inc(stored, 16)
                sp.wait_ge(stored, 16)


_INS = ["x", "norm_mix_pre", "norm_mix_post", "norm_mlp_pre", "norm_mlp_post", "w_in", "w_out",
        "attn_rel_bias", "hgrn_norm", "rwkv_mu", "rwkv_w0", "rwkv_w2", "rwkv_a0",
        "rwkv_a2", "rwkv_g2", "rwkv_k_k", "rwkv_k_a", "rwkv_r_k", "rwkv_ln_w", "rwkv_ln_b",
        "lru_conv_w", "lru_conv_b", "lru_wa", "lru_ba", "lru_wx", "lru_bx", "lru_lambda", "mlp_w1",
        "mlp_w2", "c_2", "ctx_2", "c_ctx_2", "ada_w_2", "ada_b_2", "norm_g_2", "ffn_w13_2", "ffn_w2_2",
        "ab_w_in_2", "ab_w_out_2", "ab_sink_2", "diff_lambda_2", "diff_subln_g_2", "mla_w_in_2",
        "mla_q_norm_g_2", "mla_kv_norm_g_2", "mla_wq_b_2", "mla_wkv_b_2", "mla_w_out_2"]


def kernel(**inputs):
    import concourse.bacc as bacc
    from concourse.bass_utils import run_bass_kernel_spmd

    nc = bacc.Bacc("TRN2", target_bir_lowering=False, num_devices=1)
    arrays, dram = {}, {}
    for name in _INS:
        a = np.ascontiguousarray(inputs[name])
        arrays[f"in_{name}"] = a
        dram[name] = nc.dram_tensor(f"in_{name}", a.shape, mybir.dt.from_np(a.dtype),
                                    kind="ExternalInput").ap()
    arrays["shape_constants"] = shape_constants()
    dram["consts"] = nc.dram_tensor("shape_constants", (P, N_CONST), F32, kind="ExternalInput").ap()
    dram["bias_ext"] = nc.dram_tensor("bias_ext", (GW // HD, 2 * SEQ), F32, kind="Internal").ap()
    out = nc.dram_tensor("out", (1, SEQ, D), F32, kind="ExternalOutput").ap()
    program(nc, dram, out)
    r = run_bass_kernel_spmd(nc, [arrays], core_ids=[0])
    return r.results[0]["out"]
```

```python
from contextlib import ExitStack, contextmanager

import numpy as np

import concourse.bass as bass
from concourse import mybir

F32 = mybir.dt.float32
F32R = mybir.dt.float32r
ALU = mybir.AluOpType
ACT = mybir.ActivationFunctionType
AX = mybir.AxisListType

P = 128
BANK = 512
D = 1024
KD = D // P
SEQ = 512
CTX = 256
ALL = SEQ + CTX
NX = SEQ // P
NC_ = CTX // P
GW = 256
HD = 64
CH = 64
NCH = SEQ // CH
MLP = 4 * D
FFN = 2816
EPS = 1e-6
NEG = -1e30
REL = 256
THETA = 10000.0
GRID = 64

CONSTS = {}


def _columns():
    at = 0
    for name, n in [("ident", P), ("upper", P), ("lower", P), ("upper_eq", P), ("blk16", P),
                    ("lvl32", P), ("lvl64", P), ("stack", HD), ("anti", P), ("ones64", P),
                    ("keep_before", P), ("keep_after", P), ("rot64", P), ("rot32", P),
                    ("cos64", SEQ), ("sin64", SEQ), ("cos32", SEQ), ("sin32", SEQ),
                    ("restart", SEQ), ("levels", 7 * P)]:
        CONSTS[name] = (at, n)
        at += n
    return at


N_CONST = _columns()


def shape_constants():
    c = np.zeros((P, N_CONST), np.float32)

    def put(name, a):
        at, n = CONSTS[name]
        c[:a.shape[0], at:at + n] = a

    i, j = np.arange(P)[:, None], np.arange(P)[None, :]
    same = (i // HD) == (j // HD)
    put("ident", np.eye(P))
    put("upper", same & (i < j))
    put("lower", same & (i > j))
    put("upper_eq", same & (i <= j))
    put("blk16", i // 16 == j // 16)
    put("lvl32", (i // 32 == j // 32) & (i // 16 != j // 16))
    put("lvl64", (i // 64 == j // 64) & (i // 32 != j // 32))
    put("stack", np.eye(HD)[np.arange(P) % HD])
    put("anti", np.eye(P)[::-1])
    put("ones64", same)
    put("keep_before", np.where(j >= i, 0.0, NEG))
    put("keep_after", np.where(j <= i, 0.0, NEG))

    def rotation(dim, first, reps):
        q = dim // 4
        r = np.zeros((P, P), np.float32)
        cos, sin = np.zeros((P, SEQ)), np.zeros((P, SEQ))
        inv = THETA ** (-np.arange(0, dim // 2, 2, dtype=np.float32) / np.float32(dim // 2))
        inv = inv.astype(np.float32)
        t = np.arange(SEQ)
        for rep in range(reps):
            for axis, pos in enumerate((t // GRID, t % GRID)):
                for k in range(q):
                    a = first + rep * dim + axis * 2 * q + k
                    ang = (pos.astype(np.float32) * inv[k]).astype(np.float32)
                    r[a + q, a] = -1.0
                    r[a, a + q] = 1.0
                    for m in (a, a + q):
                        cos[m], sin[m] = np.cos(ang), np.sin(ang)
        return r, cos, sin

    r, cos, sin = rotation(64, 0, 2)
    put("rot64", r)
    put("cos64", cos)
    put("sin64", sin)
    r, cos, sin = rotation(32, 64, 1)
    put("rot32", r)
    put("cos32", cos)
    put("sin32", sin)
    put("restart", np.broadcast_to(np.arange(SEQ) % CH != 0, (P, SEQ)))
    put("levels", np.concatenate(
        [i == j] + [(i // b == j // b) & (i % b < b // 2) & (j % b >= b // 2)
                    for b in (2, 4, 8, 16, 32, 64)], axis=1))
    return c


VECTORS = [("norm_mix_pre", 8), ("norm_mlp_pre", 8), ("hgrn_norm", 2), ("rwkv_mu", 7), ("rwkv_w0", 2),
           ("rwkv_a0", 2), ("rwkv_k_k", 2), ("rwkv_k_a", 2), ("rwkv_r_k", 2), ("lru_conv_w", 8),
           ("lru_conv_b", 2), ("lru_ba", 2), ("lru_bx", 2), ("lru_lambda", 2), ("c_2", 8),
           ("c_ctx_2", 8), ("norm_g_2", 64), ("ada_b_2", 96), ("mla_q_norm_g_2", 3),
           ("mla_kv_norm_g_2", 2)]
VEC_AT = {}
_at = 0
for _n, _r in VECTORS:
    VEC_AT[_n] = _at
    _at += _r
N_VEC = _at


class Link:

    def __init__(self, sem):
        self.sem, self.n = sem, 0

    def on(self, eng):
        self.eng = eng
        return self

    def __call__(self, ins):
        self.n += 1
        ins.then_inc(self.sem, 1)
        self.eng.wait_ge(self.sem, self.n)


class Core:

    def __init__(self, nc, stack, dram):
        self.nc, self.dram = nc, dram
        self.act_link = Link(stack.enter_context(nc.semaphore("act_link")))
        self.dve_link = Link(stack.enter_context(nc.semaphore("dve_link")))
        self.joins = 0
        self.ended = 0
        self.cleared = []

    @contextmanager
    def block(self):
        with self.nc.Block() as block:
            yield block
        self.ended += 1

    def reusable(self):
        for i, (number, when) in enumerate(self.cleared):
            if self.ended > when:
                return self.cleared.pop(i)[0]
        return None


class Stage:

    def __init__(self, core, name):
        self.core, self.nc, self.name, self.stack = core, core.nc, name, ExitStack()
        self.sems = []

    def __enter__(self):
        self.stack.__enter__()
        return self

    def __exit__(self, *a):
        for s in self.sems:
            self.nc.gpsimd.sem_clear(s)
            self.core.cleared.append((s.num, self.core.ended))
        return self.stack.__exit__(*a)

    def sb(self, name, shape, dt=F32):
        return self.stack.enter_context(self.nc.sbuf_tensor(f"{self.name}_{name}", shape, dt))

    def banks(self, n):
        return [self.stack.enter_context(self.nc.psum_tensor(f"{self.name}_bank{i}", [P, BANK], F32))
                for i in range(n)]

    def sem(self, name):
        num = self.core.reusable()
        s = self.stack.enter_context(self.nc.semaphore(f"{self.name}_{name}", num=num))
        self.sems.append(s)
        return s


def const(core, name):
    at, n = CONSTS[name]
    return core.dram["consts"][:, at:at + n]


def load(core, name, pairs):
    nc = core.nc
    with Stage(core, name) as st, core.block() as block:
        loaded = st.sem("loaded")

        @block.sync
        def _(sp):
            for dst, src in pairs:
                sp.dma_start(dst, src).then_inc(loaded, 16)
            sp.wait_ge(loaded, 16 * len(pairs))


def turn(core, name, groups, ident):
    nc = core.nc
    with Stage(core, name) as st:
        banks = st.banks(4)
        turned, written = st.sem("turned"), st.sem("written")
        with core.block() as block:
            @block.tensor
            def _(pe):
                for g, (blocks, out, scale) in enumerate(groups):
                    if g >= 4:
                        pe.wait_ge(written, g - 3)
                    for b, src in enumerate(blocks):
                        rows = src.shape[0]
                        cols = src.shape[1]
                        last = nc.tensor.transpose(banks[g % 4][0:cols, b * P:b * P + rows], src,
                                                   ident[0:rows, 0:rows])
                    last.then_inc(turned, 1)

            @block.vector
            def _(dve):
                for g, (blocks, out, scale) in enumerate(groups):
                    rows, n, cols = out.shape
                    dve.wait_ge(turned, g + 1)
                    src = banks[g % 4][:, 0:n * P].rearrange("p (b c) -> p b c", b=n)
                    src = src[out.start_partition():out.start_partition() + rows, :, 0:cols]
                    if scale is None:
                        nc.vector.tensor_copy(out, src).then_inc(written, 1)
                    else:
                        nc.vector.tensor_tensor(out, src, scale.to_broadcast([rows, n, cols]),
                                                ALU.mult).then_inc(written, 1)


def invert_mean(core, link, total, width, eps=EPS):
    link(core.nc.vector.tensor_scalar(total, total, 1.0 / width, eps, ALU.mult, ALU.add))
    return core.nc.vector.reciprocal(total, total)


class Join:

    def __init__(self, core, stage, y, pieces):
        self.core, self.y = core, y
        core.joins += 1
        self.pieces = stage.sb(f"join_pieces{core.joins}", [P, pieces, D // BANK])
        self.rstd = stage.sb(f"join_rstd{core.joins}", [P, pieces])

    def square(self, act, ps, s, t, c, cw):
        return self.core.nc.scalar.activation(self.squares[:, t % 2, 0:cw], ps, ACT.Square,
                                              accum_out=self.pieces[:, t, c // BANK:c // BANK + 1])

    def gate(self, dve, ps, s, t, c, cw):
        return self.core.nc.vector.tensor_tensor(self.y(t)[:, c:c + cw], ps,
                                                 self.row(t)[:, c:c + cw], ALU.mult)

    def finish(self, stage, row):
        self.squares, self.row = stage.sb(f"join_squares{self.core.joins}", [P, 2, BANK]), row
        return {"act": self.square, "dve": self.gate}

    def invert(self, dve, link):
        link(self.core.nc.vector.reduce_sum(self.rstd[:, :], self.pieces[:, :, :], AX.X))
        return invert_mean(self.core, link, self.rstd[:, :], D)

    def root(self, act):
        return self.core.nc.scalar.activation(self.rstd[:, :], self.rstd[:, :], ACT.Sqrt)

    def add(self, t, x):
        return self.core.nc.vector.scalar_tensor_tensor(x, self.y(t), self.rstd[:, t:t + 1], x,
                                                        ALU.mult, ALU.add)


def join(core, name, joined, xs):
    with Stage(core, name) as st:
        inverted, rooted = st.sem("inverted"), st.sem("rooted")
        with core.block() as block:
            @block.vector
            def _(dve):
                joined.invert(dve, core.dve_link.on(dve)).then_inc(inverted, 1)
                dve.wait_ge(rooted, 1)
                for t, x in enumerate(xs):
                    joined.add(t, x)

            @block.scalar
            def _(act):
                act.wait_ge(inverted, 1)
                joined.root(act).then_inc(rooted, 1)


def norm_to_features(core, name, jobs, ident, joined=None):
    nc = core.nc
    N = len(jobs)
    with Stage(core, name) as st:
        width = jobs[0][0].shape[1]
        kt = width // P
        banks = st.banks(8)
        squares = st.sb("squares", [P, 2, width])
        total = st.sb("total", [P, N])
        rstd = st.sb("rstd", [P, N])
        diag = st.sb("diag", [P, 2, P])
        full = st.sb("full", [P, 4, 4, P])
        joins, j_inverted, j_rooted = st.sem("joined"), st.sem("j_inverted"), st.sem("j_rooted")
        summed, inverted, rooted, scaled = (st.sem("summed"), st.sem("inverted"), st.sem("rooted"),
                                            st.sem("scaled"))
        turned, valued_a, valued_d = st.sem("turned"), st.sem("valued_a"), st.sem("valued_d")
        hi_done, written = st.sem("hi_done"), st.sem("written")
        parts = [(k0, min(k0 + 4, kt)) for k0 in range(0, kt, 4)]
        NP = len(parts)

        def place(n):
            t, (k0, k1) = n // NP, parts[n % NP]
            return t, k0, k1, full[:, n % 4, 0:k1 - k0, :]

        with core.block() as block:
            @block.scalar
            def _(act):
                def square(t):
                    if joined is not None:
                        act.wait_ge(joins, t + 1)
                    if t >= 2:
                        act.wait_ge(summed, t - 1)
                    nc.scalar.activation(squares[:, t % 2, :], jobs[t][0], ACT.Square,
                                         accum_out=total[:, t:t + 1]).then_inc(summed, 1)

                def root(t):
                    act.wait_ge(inverted, t + 1)
                    nc.scalar.activation(rstd[:, t:t + 1], total[:, t:t + 1], ACT.Sqrt)\
                      .then_inc(rooted, 1)

                def value(t):
                    n = NP * t
                    _, k0, k1, out = place(n)
                    gain, shift = jobs[t][2:4]
                    act.wait_ge(turned, n + 1)
                    if n >= 4:
                        act.wait_ge(written, n - 3)
                    for k in range(k0, k1):
                        last = nc.scalar.activation(
                            out[:, k - k0, :], banks[n % 8][:, (k - k0) * P:(k - k0 + 1) * P],
                            ACT.Identity, scale=gain[:, k:k + 1],
                            bias=0.0 if shift is None else shift[:, k:k + 1])
                    last.then_inc(valued_a, 1)

                def high_parts(t):
                    for n in range(NP * t, NP * (t + 1)):
                        _, k0, k1, src = place(n)
                        if n % NP == 0:
                            act.wait_ge(valued_a, t + 1)
                        else:
                            act.wait_ge(valued_d, t + 1)
                        hi_of(nc, jobs[t][1][0][:, k0:k1, :], src).then_inc(hi_done, 1)

                if joined is not None:
                    act.wait_ge(j_inverted, 1)
                    joined.root(act).then_inc(j_rooted, 1)
                square(0)
                for t in range(N + 1):
                    if t < N:
                        root(t)
                    if t >= 1:
                        value(t - 1)
                        high_parts(t - 1)
                    if t + 1 < N:
                        square(t + 1)

            @block.vector
            def _(dve):
                link = core.dve_link.on(dve)

                def add(t):
                    joined.add(t, jobs[t][0]).then_inc(joins, 1)

                def invert(t):
                    dve.wait_ge(summed, t + 1)
                    invert_mean(core, link, total[:, t:t + 1], width).then_inc(inverted, 1)

                def diagonal(t):
                    dve.wait_ge(rooted, t + 1)
                    if t >= 2:
                        dve.wait_ge(turned, NP * (t - 1))
                    nc.vector.tensor_scalar(diag[:, t % 2, :], ident[:, :], rstd[:, t:t + 1], None,
                                            ALU.mult).then_inc(scaled, 1)

                def value(t):
                    n = NP * t + 1
                    _, k0, k1, out = place(n)
                    gain, shift = jobs[t][2:4]
                    dve.wait_ge(turned, n + 1)
                    ps = banks[n % 8][:, 0:(k1 - k0) * P].rearrange("p (b c) -> p b c", c=P)
                    if n >= 4:
                        dve.wait_ge(written, n - 3)
                    ins = nc.vector.tensor_tensor(
                        out, ps, gain[:, k0:k1].unsqueeze(2).to_broadcast([P, k1 - k0, P]), ALU.mult)
                    if shift is not None:
                        link(ins)
                        ins = nc.vector.tensor_tensor(
                            out, out, shift[:, k0:k1].unsqueeze(2).to_broadcast([P, k1 - k0, P]),
                            ALU.add)
                    ins.then_inc(valued_d, 1)

                def low_parts(t):
                    for n in range(NP * t, NP * (t + 1)):
                        _, k0, k1, src = place(n)
                        hi, lo = jobs[t][1]
                        dve.wait_ge(hi_done, n + 1)
                        lo_of(nc, lo[:, k0:k1, :], src, hi[:, k0:k1, :]).then_inc(written, 1)

                if joined is not None:
                    joined.invert(dve, link).then_inc(j_inverted, 1)
                    dve.wait_ge(j_rooted, 1)
                    for t in range(min(2, N)):
                        add(t)
                for t in range(N + 1):
                    if t < N:
                        invert(t)
                        diagonal(t)
                    if t >= 1 and NP > 1:
                        value(t - 1)
                    if joined is not None and t + 2 < N:
                        add(t + 2)
                    if t >= 1:
                        low_parts(t - 1)

            @block.tensor
            def _(pe):
                for t in range(N):
                    pe.wait_ge(scaled, t + 1)
                    for q, (k0, k1) in enumerate(parts):
                        n = NP * t + q
                        if n >= 8:
                            pe.wait_ge(written, n - 7)
                        for k in range(k0, k1):
                            last = nc.tensor.matmul(banks[n % 8][:, (k - k0) * P:(k - k0 + 1) * P],
                                                    lhsT=jobs[t][0][:, k * P:(k + 1) * P],
                                                    rhs=diag[:, t % 2, :], start=True, stop=True,
                                                    skip_group_check=True)
                        last.then_inc(turned, 1)


W_SLOTS = 3


def hi_of(nc, out, src):
    return nc.scalar.activation(out, src, ACT.Copy)


def lo_of(nc, out, src, hi):
    return nc.vector.tensor_tensor(out, src, hi.bitcast(F32), ALU.subtract)


def three_products(nc, out, lhsT, rhs, k, first, last_):
    for n, (i, j) in enumerate(((0, 0), (0, 1), (1, 0))):
        last = nc.tensor.matmul(out, lhsT=lhsT(i, k), rhs=rhs(j, k), start=first and n == 0,
                                stop=last_ and n == 2)
    return last


class Pair:

    def __init__(self, stage, kt, n):
        self.hi, self.lo = (stage.sb(m, [P, kt, n], F32R) for m in ("hi", "lo"))

    def __getitem__(self, cols):
        return self.hi[:, :, cols], self.lo[:, :, cols]


class Weights:

    def __init__(self, core, stage, name, weight, width=BANK, kchunk=2, col0=0, cols=None, ring=None,
                 half=None):
        self.core, self.K, N = core, *weight.shape
        self.half = half
        if half is not None:
            N //= 2
        self.cols = N - col0 if cols is None else cols
        self.width, self.kchunk, self.col0 = width, min(self.K // P, kchunk), col0
        self.view = weight.rearrange("(k p) n -> p k n", p=P)
        self.ring = stage.sb(name + "_raw", [P, W_SLOTS, self.kchunk, width]) if ring is None else ring
        self.loaded = [stage.sem(f"{name}_loaded{i}") for i in range(W_SLOTS)]
        self.chunks = [(n0, min(width, self.cols - n0), k0, min(k0 + self.kchunk, self.K // P))
                       for n0 in range(0, self.cols, width) for k0 in range(0, self.K // P, self.kchunk)]
        self.sent = 0

    def wait(self, eng, i):
        loads = 1 if self.half is None else min(self.kchunk, self.K // P)
        eng.wait_ge(self.loaded[i % W_SLOTS], 16 * loads * (i // W_SLOTS + 1))

    def slot(self, i):
        n0, w, k0, k1 = self.chunks[i]
        return self.ring[:, i % W_SLOTS, 0:k1 - k0, 0:w]

    def send(self, sp, split=None):
        end = len(self.chunks) if split is not None else min(W_SLOTS, len(self.chunks))
        for i in range(self.sent, end):
            n0, w, k0, k1 = self.chunks[i]
            if i >= W_SLOTS:
                sp.wait_ge(split, i - W_SLOTS + 1)
            if self.half is not None:
                picked = self.view.rearrange("p k (h z) -> p k h z", z=P)[:, :, :, self.half * HD:
                                                                          (self.half + 1) * HD]
                for k in range(k0, k1):
                    sp.dma_start(self.slot(i)[:, k - k0].rearrange("p (h z) -> p h z", z=HD),
                                 picked[:, k, n0 // HD:(n0 + w) // HD])\
                      .then_inc(self.loaded[i % W_SLOTS], 16)
                continue
            c = self.col0 + n0
            sp.dma_start(self.slot(i), self.view[:, k0:k1, c:c + w]).then_inc(self.loaded[i % W_SLOTS], 16)
        self.sent = end

    def ahead(self):
        with self.core.block() as block:
            @block.sync
            def _(sp):
                self.send(sp)
        return self


def linear(core, name, weight, srcs, form, finish, col0=0, cols=None, width=None, kchunk=None,
           engine="act", out_tile=P):
    nc = core.nc
    pre = isinstance(srcs[0], tuple)
    lens = [(s[0] if pre else s).shape[2] for s in srcs]

    def tiles(n0, w):
        if form == "features":
            return [(s, n0 // out_tile + j, n0 + j * out_tile, min(out_tile, w - j * out_tile))
                    for j in range((w + out_tile - 1) // out_tile) for s in range(len(srcs))]
        return [(s, t, n0, w) for s in range(len(srcs)) for t in range(lens[s] // P)]

    with Stage(core, name) as st:
        banks = st.banks(8)
        if not isinstance(weight, Weights):
            weight = Weights(core, st, "w", weight, width or (256 if pre else BANK),
                             kchunk or (8 if pre else 2), col0, cols)
        KT, kchunk, width = weight.K // P, weight.kchunk, weight.width
        chunks = weight.chunks
        NCHK = len(chunks)
        whi = st.sb("whi", [P, 2, kchunk, width], F32R)
        wlo = st.sb("wlo", [P, 2, kchunk, width], F32R)
        if not pre:
            shi = [st.sb(f"shi{s}", [P, 2, kchunk, n], F32R) for s, n in enumerate(lens)]
            slo = [st.sb(f"slo{s}", [P, 2, kchunk, n], F32R) for s, n in enumerate(lens)]
        finish = finish if isinstance(finish, dict) else {engine: finish}
        used, ready = st.sem("used"), st.sem("ready")
        free = {e: st.sem(f"free_{e}") for e in finish}
        last_engine = "dve" if "dve" in finish else "act"
        hi_done, lo_done = st.sem("hi_done"), st.sem("lo_done")
        after, first, n_ready, n_used = [], [], 0, 0
        for n0, w, k0, k1 in chunks:
            first.append(n_ready)
            if k1 == KT:
                n_ready += len(tiles(n0, w))
                after.append((ready, n_ready))
            else:
                n_used += 1
                after.append((used, n_used))

        def parts(i):
            n0, w, k0, k1 = chunks[i]
            n = k1 - k0
            yield weight.slot(i), whi[:, i % 2, 0:n, 0:w], wlo[:, i % 2, 0:n, 0:w]
            if not pre:
                for s, src in enumerate(srcs):
                    yield src[:, k0:k1, :], shi[s][:, i % 2, 0:n, :], slo[s][:, i % 2, 0:n, :]

        def write_out(eng, name, i):
            n0, w, k0, k1 = chunks[i]
            if k1 == KT and name in finish:
                for j, (s, t, c, cw) in enumerate(tiles(n0, w)):
                    g = first[i] + j
                    if name == "dve" and "act" in finish:
                        eng.wait_ge(free["act"], g + 1)
                    else:
                        eng.wait_ge(ready, g + 1)
                    ps = (banks[g % 8][0:cw, 0:lens[s]] if form == "features"
                          else banks[g % 8][:, 0:cw])
                    if g >= 2:
                        eng.wait_ge(free[name], g - 1)
                    finish[name](eng, ps, s, t, c, cw).then_inc(free[name], 1)

        with core.block() as block:
            @block.sync
            def _(sp):
                weight.send(sp, lo_done)

            @block.scalar
            def _(act):
                for i in range(NCHK + 1):
                    if i < NCHK:
                        weight.wait(act, i)
                        if i >= 2:
                            act.wait_ge(*after[i - 2])
                        for src, hi, lo in parts(i):
                            last = hi_of(nc, hi, src)
                        last.then_inc(hi_done, 1)
                    if i >= 1:
                        write_out(act, "act", i - 1)

            @block.vector
            def _(dve):
                for i in range(NCHK + 1):
                    if i < NCHK:
                        dve.wait_ge(hi_done, i + 1)
                        for src, hi, lo in parts(i):
                            last = lo_of(nc, lo, src, hi)
                        last.then_inc(lo_done, 1)
                    if i >= 1:
                        write_out(dve, "dve", i - 1)

            @block.tensor
            def _(pe):
                for i, (n0, w, k0, k1) in enumerate(chunks):
                    pe.wait_ge(lo_done, i + 1)
                    for j, (s, t, c, cw) in enumerate(tiles(n0, w)):
                        g = first[i] + j
                        if k0 == 0 and g >= 8:
                            pe.wait_ge(free[last_engine], g - 7)

                        def wt(part, k):
                            return (whi, wlo)[part][:, i % 2, k - k0, c - n0:c - n0 + cw]

                        def xt(part, k):
                            x = (srcs[s][part][:, k, :] if pre
                                 else (shi, slo)[part][s][:, i % 2, k - k0, :])
                            return x if form == "features" else x[:, t * P:(t + 1) * P]

                        out = (banks[g % 8][0:cw, 0:lens[s]] if form == "features"
                               else banks[g % 8][:, 0:cw])
                        lhsT, rhs = (wt, xt) if form == "features" else (xt, wt)
                        for k in range(k0, k1):
                            last = three_products(nc, out, lhsT, rhs, k, k == 0, k == KT - 1)
                        if k1 == KT:
                            last.then_inc(ready, 1)
                    if k1 < KT:
                        last.then_inc(used, 1)


class GateUpWeights:

    def __init__(self, core, stage, name, w13, raw):
        self.core, self.raw, self.slots = core, raw, raw.shape[1]
        self.view = w13.rearrange("(k p) n -> p k n", p=P)
        self.loaded = [stage.sem(f"{name}_loaded{i}") for i in range(self.slots)]
        self.sent = 0

    def send(self, sp, split=None):
        end = FFN // P if split is not None else self.slots
        for c in range(self.sent, end):
            if c >= self.slots:
                sp.wait_ge(split, c - self.slots + 1)
            for h in range(2):
                sp.dma_start(self.raw[:, c % self.slots, h],
                             self.view[:, :, h * FFN + c * P:h * FFN + (c + 1) * P])\
                  .then_inc(self.loaded[c % self.slots], 16)
        self.sent = end

    def ahead(self):
        with self.core.block() as block:
            @block.sync
            def _(sp):
                self.send(sp)
        return self


def gated_up(core, name, weights, srcs, dsts):
    nc = core.nc
    n_chunks = FFN // P
    slots, raw, loaded = weights.slots, weights.raw, weights.loaded
    ns = len(srcs)
    lens = [s[0].shape[2] for s in srcs]
    pairs = [(c, s) for c in range(n_chunks) for s in range(ns)]
    with Stage(core, name) as st:
        banks = st.banks(8)
        whi = st.sb("whi", [P, 2, 2, KD, P], F32R)
        wlo = st.sb("wlo", [P, 2, 2, KD, P], F32R)
        gate = st.sb("gate", [P, 2, SEQ])
        ready, silu_done, free = st.sem("ready"), st.sem("silu_done"), st.sem("free")
        hi_done, lo_done = st.sem("hi_done"), st.sem("lo_done")
        with core.block() as block:
            @block.sync
            def _(sp):
                weights.send(sp, lo_done)

            @block.tensor
            def _(pe):
                for p, (c, s) in enumerate(pairs):
                    if s == 0:
                        pe.wait_ge(lo_done, c + 1)
                    if p >= 4:
                        pe.wait_ge(free, p - 3)
                    for h in range(2):
                        for k in range(KD):
                            last = three_products(
                                nc, banks[(2 * p + h) % 8][:, 0:lens[s]],
                                lambda part, k: (whi, wlo)[part][:, c % 2, h, k, :],
                                lambda part, k: srcs[s][part][:, k, :], k, k == 0, k == KD - 1)
                    last.then_inc(ready, 1)

            @block.scalar
            def _(act):
                def split(c):
                    act.wait_ge(loaded[c % slots], 32 * (c // slots + 1))
                    if c >= 2:
                        act.wait_ge(ready, ns * (c - 1))
                    hi_of(nc, whi[:, c % 2], raw[:, c % slots]).then_inc(hi_done, 1)

                split(0)
                for p, (c, s) in enumerate(pairs):
                    if s == 0 and c + 1 < n_chunks:
                        split(c + 1)
                    act.wait_ge(ready, p + 1)
                    if p >= 2:
                        act.wait_ge(free, p - 1)
                    n = lens[s]
                    nc.scalar.activation(gate[:, p % 2, 0:n], banks[2 * p % 8][:, 0:n], ACT.Silu)\
                      .then_inc(silu_done, 1)

            @block.vector
            def _(dve):
                def split(c):
                    dve.wait_ge(hi_done, c + 1)
                    lo_of(nc, wlo[:, c % 2], raw[:, c % slots], whi[:, c % 2]).then_inc(lo_done, 1)

                split(0)
                for p, (c, s) in enumerate(pairs):
                    if s == 0 and c + 1 < n_chunks:
                        split(c + 1)
                    dve.wait_ge(silu_done, p + 1)
                    n = lens[s]
                    nc.vector.tensor_tensor(dsts[s][:, c, :], gate[:, p % 2, 0:n],
                                            banks[(2 * p + 1) % 8][:, 0:n], ALU.mult).then_inc(free, 1)


def attend(core, name, jobs, ident, groups=None, key_parts=None):
    nc = core.nc
    NS = 4
    with Stage(core, name) as st:
        wide = [st.stack.enter_context(nc.psum_tensor(f"{name}_scores{b}", [P, 2 * BANK], F32))
                for b in range(2)]
        flip = st.stack.enter_context(nc.psum_tensor(f"{name}_flip", [P, 2 * BANK], F32))
        obank = [st.stack.enter_context(nc.psum_tensor(f"{name}_o{b}", [P, BANK], F32))
                 for b in range(2)]
        E = st.sb("E", [P, 2, ALL])
        ET = st.sb("ET", [P, 2, ALL])
        top = st.sb("top", [P, NS])
        ntop = st.sb("ntop", [P, NS])
        den = st.sb("den", [P, NS])
        esink = st.sb("esink", [P, NS])
        inv = st.sb("inv", [P, NS])
        groups = groups or []
        if groups:
            nq, nk = groups[0][0].shape[1], groups[0][1].shape[1]
            q_parts = [st.sb(f"q_{m}", [P, 2, nq], F32R) for m in ("hi", "lo")]
            k_parts = key_parts or [st.sb(f"k_{m}", [P, 2, nk], F32R) for m in ("hi", "lo")]
            rows_used = groups[0][0].shape[0]
            first_job = [min(i for i, job in enumerate(jobs) if job["group"] == g)
                         for g in range(len(groups))]
        hi_done, lo_done = st.sem("hi_done"), st.sem("lo_done")

        def part(parts, g, i):
            return parts[i][0:rows_used, g % 2, :]

        def split_steps(i):
            return [(g + 1, which) for g in range(len(groups) - 1) for which in range(2)
                    if i == first_job[g] + which]

        scores_ready, max_ready, exp_done = st.sem("scores"), st.sem("max"), st.sem("exp")
        turned, copied, pv_done, out_done = (st.sem("turned"), st.sem("copied"), st.sem("pv"),
                                             st.sem("out"))
        N = len(jobs)

        def n_keys(i):
            return P * len(jobs[i]["values"])

        with core.block() as block:
            @block.tensor
            def _(pe):
                def scores(i):
                    job, S = jobs[i], wide[i % 2]
                    if i >= 2:
                        pe.wait_ge(exp_done, i - 1)
                    pieces, at = [], 0
                    if groups:
                        g = job["group"]
                        if i == first_job[g]:
                            pe.wait_ge(lo_done, 2 * (g + 1))
                        for c, key in job["split"]:
                            for a, b in ((0, 0), (0, 1), (1, 0)):
                                pieces.append((c, key.stop - key.start,
                                               q_parts[a][job["rows"], g % 2, job["columns"]],
                                               k_parts[b][job["rows"], g % 2, key]))
                        pieces += [(c, key.shape[1], job["q"], key) for c, key in job["keys"]]
                    for key in (() if groups else job["keys"]):
                        n, done = key.shape[1], 0
                        while done < n:
                            m = min(n - done, BANK - at % BANK)
                            pieces.append((at, m, job["q"], key[:, done:done + m]))
                            at, done = at + m, done + m
                    extra = [(c, r.shape[1], l, r) for c, l, r in job["bias"]]
                    for b in range(2):
                        mine = [x for x in pieces + extra if x[0] // BANK == b]
                        for x, (c, m, l, r) in enumerate(mine):
                            last = nc.tensor.matmul(S[:, c:c + m], lhsT=l, rhs=r, start=(x == 0),
                                                    stop=(x == len(mine) - 1), skip_group_check=True)
                    last.then_inc(scores_ready, 1)

                def turn_probs(i):
                    pe.wait_ge(exp_done, i + 1)
                    if i >= 1:
                        pe.wait_ge(copied, i)
                    for b in range(n_keys(i) // P):
                        last = nc.tensor.transpose(flip[:, b * P:(b + 1) * P],
                                                   E[:, i % 2, b * P:(b + 1) * P], ident[:, :])
                    last.then_inc(turned, 1)

                def weigh(i):
                    pe.wait_ge(copied, i + 1)
                    if i >= 2:
                        pe.wait_ge(out_done, i - 1)
                    values = jobs[i]["values"]
                    for b, v in enumerate(values):
                        last = nc.tensor.matmul(obank[i % 2][:, 0:v.shape[1]],
                                                lhsT=ET[:, i % 2, b * P:(b + 1) * P], rhs=v,
                                                start=(b == 0), stop=(b == len(values) - 1))
                    last.then_inc(pv_done, 1)

                for i in range(N + 2):
                    if i < N:
                        scores(i)
                    if 1 <= i <= N:
                        turn_probs(i - 1)
                    if i >= 2:
                        weigh(i - 2)

            @block.vector
            def _(dve):
                link = core.dve_link.on(dve)

                def maximum(i):
                    job, s = jobs[i], i % NS
                    dve.wait_ge(scores_ready, i + 1)
                    if job["hide"]:
                        rows, c0, c1 = job["hide"]
                        link(nc.vector.memset(wide[i % 2][rows[0]:rows[1], c0:c1], NEG))
                    link(nc.vector.reduce_max(top[:, s:s + 1], wide[i % 2][:, 0:n_keys(i)], AX.X))
                    if job["sink"] is None:
                        ins = nc.vector.tensor_scalar(ntop[:, s:s + 1], top[:, s:s + 1], -job["scale"],
                                                      None, ALU.mult)
                    else:
                        ins = nc.vector.tensor_scalar(ntop[:, s:s + 1], top[:, s:s + 1], -job["scale"],
                                                      job["sink"], ALU.mult, ALU.min)
                    ins.then_inc(max_ready, 1)

                def copy(i):
                    dve.wait_ge(turned, i + 1)
                    if i >= 2:
                        dve.wait_ge(pv_done, i - 1)
                    nc.vector.tensor_copy(ET[:, i % 2, 0:n_keys(i)], flip[:, 0:n_keys(i)])\
                      .then_inc(copied, 1)

                def result(i):
                    job, s = jobs[i], i % NS
                    o = obank[i % 2][:, 0:job["out"].shape[1]]
                    if job["sink"] is not None:
                        link(nc.vector.tensor_tensor(den[:, s:s + 1], den[:, s:s + 1],
                                                     esink[:, s:s + 1], ALU.add))
                    link(nc.vector.reciprocal(inv[:, s:s + 1], den[:, s:s + 1]))
                    dve.wait_ge(pv_done, i + 1)
                    if job["minus"] is None:
                        nc.vector.tensor_scalar(job["out"], o, inv[:, s:s + 1], None, ALU.mult)\
                          .then_inc(out_done, 1)
                    else:
                        lam, base = job["minus"]
                        link(nc.vector.tensor_scalar(inv[:, s:s + 1], inv[:, s:s + 1], lam, -1.0,
                                                     ALU.mult, ALU.mult))
                        dve.wait_ge(out_done, i)
                        nc.vector.scalar_tensor_tensor(job["out"], o, inv[:, s:s + 1], base, ALU.mult,
                                                       ALU.add).then_inc(out_done, 1)

                for i in range(N + 2):
                    if i < N:
                        maximum(i)
                    if 1 <= i <= N:
                        copy(i - 1)
                    if i >= 2:
                        result(i - 2)

            @block.scalar
            def _(act):
                def split(g, which):
                    if g >= 2:
                        act.wait_ge(scores_ready, first_job[g - 1])
                    hi_of(nc, part((k_parts, q_parts)[which], g, 0), groups[g][1 - which])\
                        .then_inc(hi_done, 1)

                if groups:
                    split(0, 0)
                    split(0, 1)
                for i, job in enumerate(jobs):
                    s = i % NS
                    act.wait_ge(max_ready, i + 1)
                    if i >= 2:
                        act.wait_ge(turned, i - 1)
                    if i >= NS:
                        act.wait_ge(out_done, i - NS + 1)
                    if job["sink"] is not None:
                        nc.scalar.activation(esink[:, s:s + 1], job["sink"], ACT.Exp,
                                             bias=ntop[:, s:s + 1], scale=-1.0)
                    nc.scalar.activation(E[:, i % 2, 0:n_keys(i)], wide[i % 2][:, 0:n_keys(i)], ACT.Exp,
                                         bias=ntop[:, s:s + 1], scale=job["scale"],
                                         accum_out=den[:, s:s + 1]).then_inc(exp_done, 1)
                    for g, which in split_steps(i):
                        split(g, which)

            @block.gpsimd
            def _(pool):
                for n in range(2 * len(groups)):
                    g, which = n // 2, n % 2
                    parts = (k_parts, q_parts)[which]
                    pool.wait_ge(hi_done, n + 1)
                    nc.gpsimd.tensor_tensor(part(parts, g, 1), groups[g][1 - which],
                                            part(parts, g, 0).bitcast(F32), ALU.subtract)\
                      .then_inc(lo_done, 1)


def copy_out(nc, dst):
    def finish(eng, ps, s, t, c, cw):
        return nc.scalar.activation(dst(s, t, c, cw), ps, ACT.Copy)
    return finish


T_QA, T_KA, T_VA = 0, 2, 4
T_QB, T_FB, T_IB, T_GB = 6, 8, 10, 12
T_RWKV = 14
T_XD, T_GD = 21, 23
N_PROJ = 25


def chunk_attention(core, proj, mix, ident, meanwhile):
    nc, dram = core.nc, core.dram
    heads = GW // HD
    EXT = 2 * SEQ
    NB = SEQ // P
    with Stage(core, "ca") as st:
        v_tok = st.sb("v_tok", [P, NX, GW])
        out_tok = st.sb("out_tok", [P, NX, GW])
        ext = st.sb("ext", [heads, EXT])
        hankel = st.sb("hankel", [P, heads, NB, P])
        anti = st.sb("anti", [P, P])
        q8 = st.sb("q8", [P, 2, SEQ])
        loaded, filled, stored = st.sem("loaded"), st.sem("filled"), st.sem("stored")
        with core.block() as block:
            @block.sync
            def _(sp):
                sp.dma_start(ext[:, SEQ - REL - 1:SEQ + REL],
                             dram["attn_rel_bias"][0]).then_inc(loaded, 16)
                sp.dma_start(anti[:, :], const(core, "anti")).then_inc(loaded, 16)
                sp.wait_ge(filled, 1)
                sp.dma_start(dram["bias_ext"][:, :], ext[:, :]).then_inc(stored, 16)
                sp.wait_ge(stored, 16)
                for h in range(heads):
                    src = bass.AP(dram["bias_ext"].tensor, h * EXT + SEQ - P,
                                  [[1, P], [-P, NB], [1, P]])
                    sp.dma_start(hankel[:, h, :, :], src).then_inc(loaded, 16)

            @block.vector
            def _(dve):
                dve.wait_ge(loaded, 32)
                n = SEQ - REL - 1
                nc.vector.tensor_copy(ext[:, 0:n], ext[:, n:n + 1].to_broadcast([heads, n]))
                n = SEQ + REL
                nc.vector.tensor_copy(ext[:, n:EXT],
                                      ext[:, n - 1:n].to_broadcast([heads, EXT - n])).then_inc(filled, 1)
                nc.vector.tensor_scalar(q8[:, :, :], proj[:, T_QA:T_QA + 2, :], HD ** -0.5, None, ALU.mult)
        turn(core, "ca_v", [([proj[:, T_VA + a, t * P:(t + 1) * P] for a in range(2)],
                             v_tok[:, t, :].rearrange("p (a c) -> p a c", a=2), None)
                            for t in range(NX)], ident)
        meanwhile()
        with core.block() as block:
            @block.sync
            def _(sp):
                sp.wait_ge(loaded, 16 * (2 + heads))
        jobs = []
        for h in range(heads):
            rows = slice(HD * (h % 2), HD * (h % 2) + HD)
            for t in range(NX):
                jobs.append(dict(
                    q=q8[rows, h // 2, t * P:(t + 1) * P],
                    keys=[proj[rows, T_KA + h // 2, 0:(t + 1) * P]],
                    bias=[(kb * P, anti[:, :], hankel[:, h, t - kb, :]) for kb in range(t + 1)],
                    hide=((0, CH), t * P + CH, (t + 1) * P),
                    values=[v_tok[:, kb, h * HD:(h + 1) * HD] for kb in range(t + 1)],
                    scale=1.0, sink=None, out=out_tok[:, t, h * HD:(h + 1) * HD], minus=None))
        attend(core, "ca_at", jobs, ident)
        turn(core, "ca_o", [([out_tok[:, t, a * P:(a + 1) * P] for a in range(2)],
                             mix[:, 0:2, t * P:(t + 1) * P], None) for t in range(NX)], ident)


class Conditioning:

    SLOTS, COLS = 2, 256

    def __init__(self, core, stage, silu_c):
        self.core, self.silu_c = core, silu_c
        self.ring = stage.sb("ring", [P, self.SLOTS, KD, self.COLS])
        self.rows = stage.sb("rows", [2, 2, self.COLS])
        self.bank = stage.banks(1)[0]
        self.loaded = [stage.sem(f"loaded{i}") for i in range(self.SLOTS)]
        self.done, self.copied = stage.sem("done"), stage.sem("copied")
        self.stored = [stage.sem(f"stored{i}") for i in range(2)]
        self.chunks = [(layer, c) for layer in range(2) for c in range(0, 6 * D, self.COLS)]
        self.planned = self.sent = self.taken = self.put_out = 0

    def send(self, sp, n):
        self.planned += n
        end = min(self.planned + self.SLOTS, len(self.chunks))
        for i in range(self.sent, end):
            layer, c = self.chunks[i]
            if i >= self.SLOTS:
                sp.wait_ge(self.done, i - self.SLOTS + 1)
            wk = self.core.dram["ada_w_2"][layer].rearrange("(k p) n -> p k n", p=P)
            sp.dma_start(self.ring[:, i % self.SLOTS], wk[:, :, c:c + self.COLS])\
              .then_inc(self.loaded[i % self.SLOTS], 16)
        self.sent = max(self.sent, end)

    def left(self):
        return len(self.chunks) - self.taken

    def take(self, pe, k0=0, k1=KD):
        i = self.taken
        if i == len(self.chunks):
            return
        if k0 == 0:
            pe.wait_ge(self.loaded[i % self.SLOTS], 16 * (i // self.SLOTS + 1))
            if i >= 1:
                pe.wait_ge(self.copied, i)
        for k in range(k0, k1):
            last = self.core.nc.tensor.matmul(self.bank[0:2, 0:self.COLS], lhsT=self.silu_c[:, k, :],
                                              rhs=self.ring[:, i % self.SLOTS, k, :], start=(k == 0),
                                              stop=(k == KD - 1))
        if k1 == KD:
            last.then_inc(self.done, 1)
            self.taken += 1

    def put(self, act):
        i = self.put_out
        if i == len(self.chunks):
            return
        self.put_out += 1
        layer, c = self.chunks[i]
        act.wait_ge(self.done, i + 1)
        if i >= 2:
            act.wait_ge(self.stored[i % 2], 16 * (i // 2))
        self.core.nc.scalar.activation(self.rows[:, i % 2, :], self.bank[0:2, 0:self.COLS], ACT.Copy)\
            .then_inc(self.copied, 1)
        act.wait_ge(self.copied, i + 1)
        at = layer * 6 * D + c
        act.dma_start(self.core.dram["ada_rows"][:, at:at + self.COLS], self.rows[:, i % 2, :])\
           .then_inc(self.stored[i % 2], 16)


def hgrn(core, proj, mix, vec, ident, cond):
    nc = core.nc
    NT = SEQ // P
    LEVELS = 7
    with Stage(core, "hg") as st:
        def pairs(name):
            return st.sb(name, [P, 2, SEQ])

        key, q, cum, qe, kl, o, gate = (pairs(n) for n in ("key", "q", "cum", "qe", "kl", "o", "gate"))
        decay = st.sb("decay", [P, 2, 2, SEQ])
        qd = st.sb("qd", [P, 2, 2, SEQ])
        kd = st.sb("kd", [P, 2, 2, SEQ])
        att = st.sb("att", [P, 4, SEQ])
        i_tok = st.sb("i_tok", [P, 2, NT, P])
        k_tok = st.sb("k_tok", [P, 2, NT, P])
        G = st.sb("G", [P, 2, NCH, P])
        S = st.sb("S", [P, 2, NCH + 1, P])
        total = st.sb("total", [P, 2, NCH])
        levels = st.sb("levels", [P, LEVELS, P])
        restart = st.sb("restart", [P, SEQ])
        ones = st.sb("ones", [P, P])
        f = proj[:, T_FB:T_FB + 2, :]
        load(core, "hg_c", [(levels[:, :, :], const(core, "levels").rearrange("p (l c) -> p l c", c=P)),
                            (ones[:, :], const(core, "ones64")), (restart[:, :], const(core, "restart"))])

        def by_chunk(t):
            return t[:, :, :].rearrange("p a (c t) -> p (a c) t", t=CH)

        logged, gated, cum_done, exped = (st.sem("logged"), st.sem("gated"), st.sem("cum"),
                                          st.sem("exped"))
        with core.block() as block:
            @block.sync
            def _(sp):
                cond.send(sp, 3)

            @block.tensor
            def _(pe):
                for _ in range(3):
                    cond.take(pe)

            @block.scalar
            def _(act):
                link = core.act_link.on(act)
                link(nc.scalar.activation(o[:, :, :], f, ACT.Abs))
                link(nc.scalar.activation(o[:, :, :], o[:, :, :], ACT.Exp, scale=-1.0))
                nc.scalar.activation(o[:, :, :], o[:, :, :], ACT.Ln, bias=1.0).then_inc(logged, 1)
                nc.scalar.activation(key[:, :, :], f, ACT.Sigmoid, scale=-1.0)
                nc.scalar.activation(q[:, :, :], proj[:, T_QB:T_QB + 2, :], ACT.Silu)
                nc.scalar.activation(gate[:, :, :], proj[:, T_GB:T_GB + 2, :], ACT.Silu).then_inc(gated, 1)
                cond.put(act)
                act.wait_ge(cum_done, 1)
                nc.scalar.activation(qe[:, :, :], cum[:, :, :], ACT.Exp)
                nc.scalar.activation(total[:, :, :].rearrange("p a c -> p (a c)").unsqueeze(2),
                                     by_chunk(cum)[:, :, CH - 1:CH], ACT.Exp)
                act.wait_ge(cum_done, 2)
                nc.scalar.activation(kl[:, :, :], kl[:, :, :], ACT.Exp).then_inc(exped, 1)
                for _ in range(2):
                    cond.put(act)

            @block.vector
            def _(dve):
                link = core.dve_link.on(dve)
                V = nc.vector
                V.memset(att[:, :, :], 0.0)
                V.memset(S[:, :, 0, :], 0.0)
                dve.wait_ge(logged, 1)
                link(V.scalar_tensor_tensor(cum[:, :, :], f, 0.0, o[:, :, :], ALU.min, ALU.subtract))
                for a in range(2):
                    ins = V.tensor_tensor_scan(cum[:, a, :], restart[:, :], cum[:, a, :], 0.0, ALU.mult,
                                               ALU.add)
                    link(ins) if a == 0 else ins.then_inc(cum_done, 1)
                dve.wait_ge(cum_done, 1)
                V.tensor_tensor(by_chunk(kl), by_chunk(cum)[:, :, CH - 1:CH].to_broadcast([P, 2 * NCH, CH]),
                                by_chunk(cum), ALU.subtract).then_inc(cum_done, 1)
                dve.wait_ge(gated, 1)
                dve.wait_ge(exped, 1)
                link(V.tensor_tensor(qe[:, :, :], qe[:, :, :], q[:, :, :], ALU.mult))
                link(V.tensor_tensor(kl[:, :, :], kl[:, :, :], key[:, :, :], ALU.mult))
        turn(core, "hg_t", [([src[:, a, t * P:(t + 1) * P] for t in range(NT)], dst[:, a, :, :], None)
                            for a in range(2)
                            for src, dst in ((proj[:, T_IB:T_IB + 2, :], i_tok), (kl, k_tok))], ident)
        differed, decayed, weighted, scored, copied = (st.sem("differed"), st.sem("decayed"),
                                                       st.sem("weighted"), st.sem("scored"),
                                                       st.sem("copied"))
        g_ready, g_done = st.sem("g_ready"), st.sem("g_done")
        with Stage(core, "hgl") as ss:
            banks = ss.banks(6)
            with core.block() as block:
                @block.sync
                def _(sp):
                    cond.send(sp, LEVELS * 2)

                @block.vector
                def _(dve):
                    V = nc.vector

                    def differ(n):
                        b = 1 << n
                        h = b // 2
                        if n >= 3:
                            dve.wait_ge(weighted, 2 * (n - 2))
                        src = cum[:, :, :].rearrange("p a t -> p (a t)").rearrange("p (n b) -> p n b", b=b)
                        dst = decay[:, n % 2].rearrange("p a t -> p (a t)").rearrange("p (n b) -> p n b", b=b)
                        mid = src[:, :, h - 1:h].to_broadcast([P, 2 * SEQ // b, h])
                        V.tensor_tensor(dst[:, :, 0:h], mid, src[:, :, 0:h], ALU.subtract)
                        V.tensor_tensor(dst[:, :, h:b], src[:, :, h:b], mid, ALU.subtract)\
                         .then_inc(differed, 1)

                    def weight(n):
                        dve.wait_ge(decayed, n)
                        if n >= 3:
                            dve.wait_ge(scored, 4 * (n - 1))
                        V.tensor_tensor(qd[:, n % 2], q[:, :, :], decay[:, n % 2], ALU.mult)\
                         .then_inc(weighted, 1)

                    differ(1)
                    for n in range(LEVELS):
                        if n >= 1:
                            weight(n)
                        if n + 1 < LEVELS and n >= 1:
                            differ(n + 1)
                        for b in range(4):
                            dve.wait_ge(scored, 4 * n + b + 1)
                            V.copy_predicated(
                                att[:, b, :].rearrange("p (t c) -> p t c", c=P),
                                levels[:, n:n + 1, :].bitcast(mybir.dt.uint32).to_broadcast([P, NT, P]),
                                banks[b][:, :].rearrange("p (t c) -> p t c", c=P)).then_inc(copied, 1)
                        if n < 2:
                            dve.wait_ge(g_ready, n + 1)
                            for par in range(2):
                                last = V.tensor_tensor(
                                    G[:, n, par::2, :],
                                    banks[4 + par][:, :].rearrange("p (t c) -> p t c", c=P),
                                    ones[:, :].unsqueeze(1).to_broadcast([P, NT, P]), ALU.mult)
                            last.then_inc(g_done, 1)

                @block.gpsimd
                def _(pool):
                    for n in range(1, LEVELS):
                        pool.wait_ge(decayed, n)
                        if n >= 3:
                            pool.wait_ge(scored, 4 * (n - 1))
                        nc.gpsimd.tensor_tensor(kd[:, n % 2], key[:, :, :], decay[:, n % 2], ALU.mult)\
                          .then_inc(weighted, 1)

                @block.scalar
                def _(act):
                    for n in range(1, LEVELS):
                        act.wait_ge(differed, n)
                        nc.scalar.activation(decay[:, n % 2], decay[:, n % 2], ACT.Exp)\
                          .then_inc(decayed, 1)
                        for _ in range(2):
                            cond.put(act)
                    for _ in range(2):
                        cond.put(act)

                @block.tensor
                def _(pe):
                    for n in range(LEVELS):
                        if n >= 1:
                            pe.wait_ge(weighted, 2 * n)
                        qs, ks = (q[:, :, :], key[:, :, :]) if n == 0 else (qd[:, n % 2], kd[:, n % 2])
                        for b in range(4):
                            if n >= 1:
                                pe.wait_ge(copied, 4 * (n - 1) + b + 1)
                            a, r = b // 2, slice((b % 2) * HD, (b % 2 + 1) * HD)
                            for t in range(NT):
                                c = slice(t * P, (t + 1) * P)
                                last = nc.tensor.matmul(banks[b][:, c], lhsT=ks[r, a, c], rhs=qs[r, a, c],
                                                        start=True, stop=True, skip_group_check=True)
                            last.then_inc(scored, 1)
                            if b % 2:
                                cond.take(pe)
                        if n < 2:
                            if n == 1:
                                pe.wait_ge(g_done, 1)
                            for t in range(NT):
                                for par in range(2):
                                    r = slice(par * CH, (par + 1) * CH)
                                    last = nc.tensor.matmul(banks[4 + par][:, t * P:(t + 1) * P],
                                                            lhsT=k_tok[r, n, t, :], rhs=i_tok[r, n, t, :],
                                                            start=True, stop=True, skip_group_check=True)
                            last.then_inc(g_ready, 1)
        within, stated, across, moved = (st.sem("within"), st.sem("stated"), st.sem("across"),
                                         st.sem("moved"))
        squared, meaned, inverted, rooted = (st.sem("squared"), st.sem("meaned"), st.sem("inverted"),
                                             st.sem("rooted"))
        sq, rstd, inter = qd[:, 0], qd[:, 1], kd[:, 0]
        with Stage(core, "hgo") as ss:
            banks = ss.banks(6)
            with core.block() as block:
                @block.sync
                def _(sp):
                    cond.send(sp, 2)

                @block.tensor
                def _(pe):
                    for a in range(2):
                        for h in range(2):
                            for t in range(NT):
                                c = slice(t * P, (t + 1) * P)
                                last = nc.tensor.matmul(banks[a][h * HD:(h + 1) * HD, c],
                                                        lhsT=i_tok[:, a, t, h * HD:(h + 1) * HD],
                                                        rhs=att[:, 2 * a + h, c], start=True, stop=True,
                                                        skip_group_check=True)
                        last.then_inc(within, 1)
                    for _ in range(2):
                        cond.take(pe)
                    for a in range(2):
                        pe.wait_ge(stated, a + 1)
                        for c in range(NCH):
                            last = nc.tensor.matmul(banks[2 + a][:, c * CH:(c + 1) * CH],
                                                    lhsT=S[:, a, c, :], rhs=qe[:, a, c * CH:(c + 1) * CH],
                                                    start=True, stop=True, skip_group_check=True)
                        last.then_inc(across, 1)
                    for a in range(2):
                        pe.wait_ge(squared, a + 1)
                        nc.tensor.matmul(banks[4 + a][:, :], lhsT=ones[:, :], rhs=sq[:, a, :], start=True,
                                         stop=True).then_inc(meaned, 1)

                @block.scalar
                def _(act):
                    for _ in range(2):
                        cond.put(act)
                    for a in range(2):
                        act.wait_ge(across, a + 1)
                        nc.scalar.activation(inter[:, a, :], banks[2 + a][:, :], ACT.Copy)\
                          .then_inc(moved, 1)
                    for a in range(2):
                        act.wait_ge(inverted, a + 1)
                        nc.scalar.activation(rstd[:, a, :], rstd[:, a, :], ACT.Sqrt).then_inc(rooted, 1)

                @block.vector
                def _(dve):
                    link = core.dve_link.on(dve)
                    V = nc.vector
                    for a in range(2):
                        for c in range(NCH - 1):
                            ins = V.scalar_tensor_tensor(S[:, a, c + 1, :], S[:, a, c, :],
                                                         total[:, a, c:c + 1], G[:, a, c, :], ALU.mult,
                                                         ALU.add)
                            link(ins) if c < NCH - 2 else ins.then_inc(stated, 1)
                    for a in range(2):
                        dve.wait_ge(within, a + 1)
                        dve.wait_ge(moved, a + 1)
                        link(V.tensor_tensor(o[:, a, :], banks[a][:, :], inter[:, a, :], ALU.add))
                        V.tensor_tensor(sq[:, a, :], o[:, a, :], o[:, a, :], ALU.mult).then_inc(squared, 1)
                    for a in range(2):
                        dve.wait_ge(meaned, a + 1)
                        link(V.tensor_scalar(rstd[:, a, :], banks[4 + a][:, :], 1.0 / HD, EPS, ALU.mult,
                                             ALU.add))
                        V.reciprocal(rstd[:, a, :], rstd[:, a, :]).then_inc(inverted, 1)
                    for a in range(2):
                        dve.wait_ge(rooted, a + 1)
                        col = VEC_AT["hgrn_norm"] + a
                        link(V.scalar_tensor_tensor(o[:, a, :], o[:, a, :], vec[:, col:col + 1],
                                                    rstd[:, a, :], ALU.mult, ALU.mult))
                        V.tensor_tensor(mix[:, 2 + a, :], o[:, a, :], gate[:, a, :], ALU.mult)


def rglru(core, proj, mix, vec):
    nc, dram = core.nc, core.dram
    with Stage(core, "lru") as st:
        banks = st.banks(4)
        w = st.sb("w", [P, 2, 2, P])
        conv = st.sb("conv", [P, 2, SEQ])
        gates = st.sb("gates", [P, 2, 2, SEQ])
        la = st.sb("la", [P, 2, SEQ])
        a = st.sb("a", [P, 2, SEQ])
        e2 = st.sb("e2", [P, 2, SEQ])
        th = st.sb("th", [P, 2, SEQ])
        u = st.sb("u", [P, 2, SEQ])
        g = st.sb("g", [P, 2, SEQ])
        g3 = st.sb("g3", [P, 2, SEQ])
        sm = st.sb("sm", [P, 8, 2])
        cleared, loaded = st.sem("cleared"), st.sem("loaded")
        conv_done, gated, sigm, decayed = st.sem("conv"), st.sem("gated"), st.sem("sigm"), st.sem("decay")
        exped, lam_done, lam_exp, cubed, tanhed = (st.sem("exped"), st.sem("lam"), st.sem("lam_exp"),
                                                   st.sem("cubed"), st.sem("tanhed"))
        rooted, prod = st.sem("rooted"), st.sem("prod")

        def v(name, i=0, n=2):
            return vec[:, VEC_AT[name] + i:VEC_AT[name] + i + n]

        with core.block() as block:
            @block.sync
            def _(sp):
                sp.wait_ge(cleared, 1)
                for m, name in enumerate(("lru_wa", "lru_wx")):
                    for b in range(4):
                        r = HD * (b % 2)
                        sp.dma_start(w[r:r + HD, m, b // 2, r:r + HD], dram[name][0, b])\
                          .then_inc(loaded, 16)
                sp.wait_ge(loaded, 128)

            @block.tensor
            def _(pe):
                pe.wait_ge(loaded, 128)
                pe.wait_ge(conv_done, 1)
                for m in range(2):
                    for i in range(2):
                        nc.tensor.matmul(banks[2 * m + i][:, :], lhsT=w[:, m, i, :], rhs=conv[:, i, :],
                                         start=True, stop=True).then_inc(gated, 1)

            @block.scalar
            def _(act):
                link = core.act_link.on(act)
                act.wait_ge(lam_done, 1)
                nc.scalar.activation(sm[:, 1, :], sm[:, 0, :], ACT.Exp, scale=-1.0).then_inc(lam_exp, 1)
                for m, b in enumerate(("lru_ba", "lru_bx")):
                    for i in range(2):
                        act.wait_ge(gated, 2 * m + i + 1)
                        nc.scalar.activation(gates[:, m, i, :], banks[2 * m + i][:, :], ACT.Sigmoid,
                                             bias=v(b, i, 1)).then_inc(sigm, 1)
                act.wait_ge(decayed, 1)
                nc.scalar.activation(a[:, :, :], la[:, :, :], ACT.Exp)
                nc.scalar.activation(e2[:, :, :], la[:, :, :], ACT.Exp, scale=2.0)
                nc.scalar.activation(th[:, :, :], la[:, :, :], ACT.Tanh, scale=-1.0).then_inc(exped, 1)
                act.wait_ge(cubed, 1)
                nc.scalar.activation(g3[:, :, :], g3[:, :, :], ACT.Tanh, scale=(2.0 / np.pi) ** 0.5)\
                  .then_inc(tanhed, 1)
                act.wait_ge(prod, 1)
                nc.scalar.activation(e2[:, :, :], e2[:, :, :], ACT.Sqrt).then_inc(rooted, 1)

            @block.vector
            def _(dve):
                link = core.dve_link.on(dve)
                V = nc.vector
                V.memset(w[:, :, :, :], 0.0).then_inc(cleared, 1)
                link(V.tensor_scalar(sm[:, 6, :], v("lru_lambda"), -1.0, None, ALU.mult))
                V.tensor_tensor(sm[:, 0, :], sm[:, 6, :], v("lru_lambda"), ALU.max).then_inc(lam_done, 1)
                x = proj[:, T_XD:T_XD + 2, :]
                for i in range(2):
                    cw = [VEC_AT["lru_conv_w"] + 2 * j + i for j in range(4)]
                    link(V.tensor_scalar(conv[:, i, :], x[:, i, :], vec[:, cw[3]:cw[3] + 1],
                                         v("lru_conv_b", i, 1), ALU.mult, ALU.add))
                    for j in range(3):
                        s = 3 - j
                        link(V.scalar_tensor_tensor(conv[:, i, s:], x[:, i, 0:SEQ - s],
                                                    vec[:, cw[j]:cw[j] + 1], conv[:, i, s:], ALU.mult,
                                                    ALU.add))
                V.sem_inc(conv_done, 1)
                dve.wait_ge(lam_exp, 1)
                link(V.tensor_scalar(sm[:, 2, :], sm[:, 1, :], 2.0, None, ALU.add))
                link(V.reciprocal(sm[:, 2, :], sm[:, 2, :]))
                link(V.tensor_tensor(sm[:, 2, :], sm[:, 2, :], sm[:, 1, :], ALU.mult))
                link(V.tensor_tensor(sm[:, 3, :], sm[:, 2, :], sm[:, 2, :], ALU.mult))
                link(V.tensor_scalar(sm[:, 4, :], sm[:, 3, :], 2.0 / 15, 2.0 / 13, ALU.mult, ALU.add))
                for k in (11, 9, 7, 5, 3, 1):
                    link(V.tensor_tensor(sm[:, 4, :], sm[:, 4, :], sm[:, 3, :], ALU.mult))
                    link(V.tensor_scalar(sm[:, 4, :], sm[:, 4, :], 2.0 / k, None, ALU.add))
                link(V.tensor_tensor(sm[:, 4, :], sm[:, 4, :], sm[:, 2, :], ALU.mult))
                link(V.tensor_scalar(sm[:, 5, :], v("lru_lambda"), -1.0, 0.0, ALU.mult, ALU.max))
                link(V.tensor_tensor(sm[:, 5, :], sm[:, 5, :], sm[:, 4, :], ALU.add))
                link(V.tensor_scalar(sm[:, 5, :], sm[:, 5, :], -8.0, None, ALU.mult))
                dve.wait_ge(sigm, 4)
                for i in range(2):
                    link(V.tensor_scalar(la[:, i, :], gates[:, 0, i, :], sm[:, 5, i:i + 1], None, ALU.mult))
                V.sem_inc(decayed, 1)
                link(V.tensor_tensor(u[:, :, :], gates[:, 1], conv[:, :, :], ALU.mult))
                gd = proj[:, T_GD:T_GD + 2, :]
                link(V.tensor_tensor(g[:, :, :], gd, gd, ALU.mult))
                link(V.tensor_scalar(g[:, :, :], g[:, :, :], 0.044715, 1.0, ALU.mult, ALU.add))
                V.tensor_tensor(g3[:, :, :], g[:, :, :], gd, ALU.mult).then_inc(cubed, 1)
                dve.wait_ge(exped, 1)
                V.scalar_tensor_tensor(e2[:, :, :], e2[:, :, :], 1.0, th[:, :, :], ALU.add, ALU.mult)\
                 .then_inc(prod, 1)
                dve.wait_ge(tanhed, 1)
                link(V.scalar_tensor_tensor(g3[:, :, :], g3[:, :, :], 1.0, gd, ALU.add, ALU.mult))
                dve.wait_ge(rooted, 1)
                link(V.tensor_tensor(u[:, :, :], u[:, :, :], e2[:, :, :], ALU.mult))
                for i in range(2):
                    link(V.tensor_tensor_scan(g[:, i, :], a[:, i, :], u[:, i, :], 0.0, ALU.mult, ALU.add))
                V.scalar_tensor_tensor(mix[:, 6:8, :], g[:, :, :], 0.5, g3[:, :, :], ALU.mult, ALU.mult)


def rwkv(core, proj, mix, vec, ident, cond):
    nc, dram = core.nc, core.dram
    xs = proj[:, T_RWKV:T_RWKV + 7, :]
    free = list(range(0, T_RWKV)) + list(range(T_XD, N_PROJ))

    def two(i):
        at = free[2 * i]
        assert free[2 * i + 1] == at + 1
        return proj[:, at:at + 2, :]

    gate, av, lw, cum, kk, km, ex, ei, en = (two(i) for i in range(9))

    def v(name, i=0, n=2):
        return vec[:, VEC_AT[name] + i:VEC_AT[name] + i + n]

    with Stage(core, "rp") as st:
        banks = st.banks(6)
        diff = st.sb("diff", [P, 7, SEQ])
        lora = st.sb("lora", [P, GW])
        low = st.sb("low", [P, SEQ])
        ones = st.sb("ones", [P, P])
        restart = st.sb("restart", [P, SEQ])
        load(core, "rp_c", [(lora[0:32, :], dram["rwkv_w2"][0]), (lora[32:64, :], dram["rwkv_a2"][0]),
                            (lora[64:128, :], dram["rwkv_g2"][0]), (ones[:, :], const(core, "ones64")),
                            (restart[:, :], const(core, "restart"))])
        differed = st.sem("differed")
        shifted, low_done, lora_done, sigm, ssq, summed = (st.sem("shifted"), st.sem("low"),
                                                           st.sem("lora"), st.sem("sigm"),
                                                           st.sem("ssq"), st.sem("summed"))
        inverted, rooted, cum_done, exped = (st.sem("inverted"), st.sem("rooted"), st.sem("cum"),
                                            st.sem("exped"))
        with core.block() as block:
            @block.sync
            def _(sp):
                cond.send(sp, 4)

            @block.vector
            def _(dve):
                link = core.dve_link.on(dve)
                V = nc.vector
                order = (6, 2, 3, 0, 1, 4, 5)
                V.tensor_scalar(diff[:, :, 0:1], xs[:, :, 0:1], -1.0, None, ALU.mult)\
                 .then_inc(differed, 1)
                for i in order:
                    V.tensor_tensor(diff[:, i, 1:], xs[:, i, 0:SEQ - 1], xs[:, i, 1:], ALU.subtract)\
                     .then_inc(differed, 1)
                    if i == 6:
                        dve.wait_ge(differed, 2)
                        V.scalar_tensor_tensor(xs[:, 6, :], diff[:, 6, :], v("rwkv_mu", 6, 1),
                                               xs[:, 6, :], ALU.mult, ALU.add).then_inc(shifted, 1)
                dve.wait_ge(differed, 8)
                for i in order[1:]:
                    V.scalar_tensor_tensor(xs[:, i, :], diff[:, i, :], v("rwkv_mu", i, 1), xs[:, i, :],
                                           ALU.mult, ALU.add).then_inc(shifted, 1)
                dve.wait_ge(shifted, 7)
                for i in range(2):
                    link(V.tensor_scalar(kk[:, i, :], xs[:, 2 + i, :], v("rwkv_k_k", i, 1), None, ALU.mult))
                    V.tensor_tensor(diff[:, i, :], kk[:, i, :], kk[:, i, :], ALU.mult).then_inc(ssq, 1)
                for i in range(2):
                    dve.wait_ge(summed, i + 1)
                    link(V.tensor_scalar(diff[:, 2 + i, :], banks[4 + i][:, :], 1e-24, None, ALU.max))
                    V.reciprocal(diff[:, 2 + i, :], diff[:, 2 + i, :]).then_inc(inverted, 1)
                dve.wait_ge(sigm, 4)
                for i in range(2):
                    link(V.tensor_scalar(lw[:, i, :], lw[:, i, :], -float(np.exp(-0.5)), None, ALU.mult))
                    V.tensor_tensor_scan(cum[:, i, :], restart[:, :], lw[:, i, :], 0.0, ALU.mult, ALU.add)\
                     .then_inc(cum_done, 1)
                dve.wait_ge(cum_done, 2)
                V.tensor_tensor(diff[:, 4:6, :], cum, lw, ALU.subtract).then_inc(cum_done, 1)
                for i in range(2):
                    link(V.tensor_scalar(km[:, i, :], av[:, i, :], 1.0, v("rwkv_k_a", i, 1), ALU.subtract,
                                         ALU.mult))
                    link(V.scalar_tensor_tensor(km[:, i, :], km[:, i, :], 1.0, xs[:, 2 + i, :], ALU.add,
                                                ALU.mult))
                dve.wait_ge(rooted, 2)
                link(V.tensor_tensor(kk, kk, diff[:, 2:4, :], ALU.mult))
                for i in range(2):
                    V.scalar_tensor_tensor(xs[:, 2 + i, :], km[:, i, :], v("rwkv_r_k", i, 1),
                                           xs[:, i, :], ALU.mult, ALU.mult)
                dve.wait_ge(exped, 3)
                link(V.tensor_tensor(av, av, kk, ALU.mult))
                link(V.tensor_tensor(av, av, en, ALU.mult))
                link(V.tensor_tensor(km, km, en, ALU.mult))
                link(V.scalar_tensor_tensor(kk, kk, -1.0, ex, ALU.mult, ALU.mult))
                link(V.tensor_tensor(xs[:, 0:2, :], xs[:, 0:2, :], ei, ALU.mult))

            @block.scalar
            def _(act):
                cond.put(act)
                act.wait_ge(shifted, 1)
                nc.scalar.activation(low[0:32, :], xs[0:32, 6, :], ACT.Tanh)
                nc.scalar.activation(low[32:64, :], xs[32:64, 6, :], ACT.Copy)
                nc.scalar.activation(low[64:128, :], xs[64:128, 6, :], ACT.Sigmoid).then_inc(low_done, 1)
                for i in range(2):
                    act.wait_ge(lora_done, 1)
                    nc.scalar.activation(lw[:, i, :], banks[i][:, :], ACT.Sigmoid,
                                         bias=v("rwkv_w0", i, 1)).then_inc(sigm, 1)
                    nc.scalar.activation(av[:, i, :], banks[2 + i][:, :], ACT.Sigmoid,
                                         bias=v("rwkv_a0", i, 1)).then_inc(sigm, 1)
                act.wait_ge(lora_done, 2)
                for i in range(2):
                    nc.scalar.activation(gate[:, i, :], banks[4 + i][:, :], ACT.Copy)
                cond.put(act)
                act.wait_ge(cum_done, 3)
                nc.scalar.activation(ex, diff[:, 4:6, :], ACT.Exp).then_inc(exped, 1)
                nc.scalar.activation(ei, cum, ACT.Exp).then_inc(exped, 1)
                nc.scalar.activation(en, cum, ACT.Exp, scale=-1.0).then_inc(exped, 1)
                for i in range(2):
                    act.wait_ge(inverted, i + 1)
                    nc.scalar.activation(diff[:, 2 + i, :], diff[:, 2 + i, :], ACT.Sqrt).then_inc(rooted, 1)
                for _ in range(2):
                    cond.put(act)

            @block.tensor
            def _(pe):
                cond.take(pe)
                for i in range(2):
                    pe.wait_ge(ssq, i + 1)
                    nc.tensor.matmul(banks[4 + i][:, :], lhsT=ones[:, :], rhs=diff[:, i, :], start=True,
                                     stop=True).then_inc(summed, 1)
                pe.wait_ge(low_done, 1)
                for r0, r1, b in ((0, 32, 0), (32, 64, 2), (64, 128, 4)):
                    if b == 4:
                        last.then_inc(lora_done, 1)
                        pe.wait_ge(inverted, 2)
                    for i in range(2):
                        last = nc.tensor.matmul(banks[b + i][:, :], lhsT=lora[r0:r1, i * P:(i + 1) * P],
                                                rhs=low[r0:r1, :], start=True, stop=True)
                last.then_inc(lora_done, 1)
                for _ in range(3):
                    cond.take(pe)
    alpha, beta, kbar, rbar, prod = kk, av, km, xs[:, 0:2, :], xs[:, 2:4, :]
    vals = xs[:, 4:6, :]
    for pair in range(2):
        rwkv_pair(core, pair, dict(alpha=alpha[:, pair], beta=beta[:, pair], kbar=kbar[:, pair],
                                   rbar=rbar[:, pair], prod=prod[:, pair], vals=vals[:, pair],
                                   total=ei[:, pair], gate=gate[:, pair]), mix[:, 4 + pair, :], ident, cond)


def rwkv_pair(core, pair, f, out, ident, cond):
    nc, dram = core.nc, core.dram
    HALF = NCH // 2
    with Stage(core, f"rk{pair}") as st:
        def mats(name, n=P):
            return st.sb(name, [P, NCH, n])

        Ab, Bb, Kb, Rb, Vb, Qb = (mats(n) for n in ("alpha", "beta", "kbar", "rbar", "vals", "prod"))
        A, AT, AkT, RbT, RkT = (mats(n) for n in ("A", "AT", "AkT", "RbT", "RkT"))
        X, XT, Y2, Y2T, C2 = (mats(n) for n in ("X", "XT", "Y2", "Y2T", "C2"))
        V = mats("V", HD)
        AkV, U0 = mats("AkV", HD), mats("U0", HD)
        G = mats("G", HD)
        S = st.sb("S", [P, NCH + 1, HD])
        cons = {}
        for n in ("upper", "lower", "upper_eq", "blk16", "lvl32", "lvl64", "stack"):
            cons[n] = st.sb("c_" + n, [P, CONSTS[n][1]])
        lnw, lnb = st.sb("lnw", [P, HD]), st.sb("lnb", [P, HD])
        ones_col = st.sb("ones_col", [P, 1])
        bonus = st.sb("bonus", [P, NCH])
        stats = st.sb("stats", [P, NCH, 6])
        mv = st.sb("mv", [P, NCH, 2])
        rs = st.sb("rs", [P, NCH])
        ln_rows = [(t[h * HD:(h + 1) * HD, :],
                    bass.AP(dram[n].tensor, pair * P + h * HD, [[0, HD], [1, HD]]))
                   for t, n in ((lnw, "rwkv_ln_w"), (lnb, "rwkv_ln_b")) for h in range(2)]
        load(core, f"rk{pair}_c", [(cons[n][:, :], const(core, n)) for n in cons] + ln_rows)
        with core.block() as block:
            @block.sync
            def _(sp):
                cond.send(sp, 1)

            @block.tensor
            def _(pe):
                cond.take(pe)

            @block.scalar
            def _(act):
                cond.put(act)

            @block.gpsimd
            def _(pool):
                for t in (Ab, Bb, Kb):
                    nc.gpsimd.memset(t[:, :, :], 0.0)

            @block.vector
            def _(dve):
                for t in (Rb, Vb, Qb):
                    nc.vector.memset(t[:, :, :], 0.0)
                nc.vector.memset(S[:, 0, :], 0.0)
                nc.vector.memset(ones_col[:, :], 1.0)
        with core.block() as block:
            @block.sync
            def _(sp):
                cond.send(sp, 2)

            @block.tensor
            def _(pe):
                for _ in range(2):
                    cond.take(pe)

            @block.vector
            def _(dve):
                for h in range(2):
                    r = slice(h * HD, (h + 1) * HD)
                    for t, n in ((Ab, "alpha"), (Bb, "beta"), (Kb, "kbar")):
                        nc.vector.tensor_copy(t[r, :, r], f[n][r, :].rearrange("p (c t) -> p c t", c=NCH))

            @block.scalar
            def _(act):
                for h in range(2):
                    r = slice(h * HD, (h + 1) * HD)
                    for t, n in ((Rb, "rbar"), (Vb, "vals"), (Qb, "prod")):
                        nc.scalar.activation(t[r, :, r], f[n][r, :].rearrange("p (c t) -> p c t", c=NCH),
                                             ACT.Copy)
                    cond.put(act)
        I = ident
        eye = ident[:, :].unsqueeze(1).to_broadcast([P, HALF, P])

        def mask(n):
            return cons[n][:, :].unsqueeze(1).to_broadcast([P, HALF, P])

        MASK, ADD, COPY = "mask", "add", "copy"
        steps = [
            (Bb, Ab, MASK, "upper", AT), (Ab, Bb, MASK, "lower", A),
            (Kb, Ab, MASK, "upper", AkT), (Bb, Rb, MASK, "upper_eq", RbT),
            (Kb, Rb, MASK, "upper_eq", RkT),
            (Vb, cons["stack"], COPY, None, V),
        ]
        products(core, f"rk{pair}_a", steps, mask, cond, 1)
        D1, D1T, C1, C1T = Y2, Y2T, A, AT
        with core.block() as block:
            @block.vector
            def _(dve):
                link = core.dve_link.on(dve)
                full = [P, NCH, P]

                def m(n):
                    return cons[n][:, :].unsqueeze(1).to_broadcast(full)

                E = ident[:, :].unsqueeze(1).to_broadcast(full)
                for src, d, x in ((A, D1, X), (AT, D1T, XT)):
                    link(nc.vector.tensor_tensor(d[:, :, :], src[:, :, :], m("blk16"), ALU.mult))
                    link(nc.vector.tensor_tensor(x[:, :, :], d[:, :, :], E, ALU.add))
                link(nc.vector.tensor_tensor(C2[:, :, :], A[:, :, :], m("lvl64"), ALU.mult))
                link(nc.vector.tensor_tensor(A[:, :, :], A[:, :, :], m("lvl32"), ALU.mult))
                link(nc.vector.tensor_tensor(AT[:, :, :], AT[:, :, :], m("lvl32"), ALU.mult))
        Z, ZT = mats("Z"), mats("ZT")
        W, WT = Ab, mats("WT")
        steps = []
        d, dT, e, eT = D1, D1T, Z, ZT
        for _ in range(3):
            steps += [(dT, d, COPY, None, e), (d, dT, COPY, None, eT),
                      (XT, e, ADD, X, X), (e, XT, ADD, XT, XT)]
            d, dT, e, eT = e, eT, d, dT
        steps += [(C1T, X, COPY, None, d), (C1, XT, COPY, None, dT),
                  (XT, d, ADD, X, e), (X, dT, ADD, XT, eT),
                  (C2, eT, COPY, None, d), (e, d, ADD, eT, X)]
        TT = X
        At, Bt, Kt = XT, Y2T, AT
        steps += [(Ab, I, COPY, None, At), (Bb, I, COPY, None, Bt), (Kb, I, COPY, None, Kt)]
        steps += [(AkT, V, COPY, None, AkV), (TT, AkV, COPY, None, U0),
                  (TT, At, COPY, None, W), (At, TT, COPY, None, WT),
                  (W, Bt, ADD, eye, AkT)]
        M1T = AkT
        products(core, f"rk{pair}_b", steps, mask, cond, 5 - pair)
        total = f["total"].rearrange("p (c t) -> p c t", c=NCH)[:, :, CH - 1:CH]
        with Stage(core, f"rk{pair}_s") as ss:
            banks = ss.banks(7)
            g_ready, g_done, m_ready, s_done = (ss.sem("g_ready"), ss.sem("g_done"), ss.sem("m_ready"),
                                                ss.sem("s_done"))
            u_ready, u_done, y_ready, b_ready = (ss.sem("u_ready"), ss.sem("u_done"), ss.sem("y_ready"),
                                                 ss.sem("b_ready"))
            norm, root, gain_done, turned = (ss.sem("norm"), ss.sem("root"), ss.sem("gain"),
                                             ss.sem("turned"))
            U, Yt = G, U0
            with core.block() as block:
                @block.tensor
                def _(pe):
                    T = nc.tensor
                    for c in range(NCH):
                        g = banks[0][:, c * HD:(c + 1) * HD]
                        T.matmul(g, lhsT=Bt[:, c, :], rhs=U0[:, c, :], start=True, stop=False,
                                 skip_group_check=True)
                        last = T.matmul(g, lhsT=Kt[:, c, :], rhs=V[:, c, :], start=False, stop=True,
                                        skip_group_check=True)
                    last.then_inc(g_ready, 1)
                    for c in range(NCH):
                        last = T.matmul(banks[4][:, c:c + 1], lhsT=Qb[:, c, :], rhs=ones_col[:, 0:1],
                                        start=True, stop=True,
                                        skip_group_check=True)
                    last.then_inc(b_ready, 1)
                    for c in range(NCH):
                        if c >= 1:
                            pe.wait_ge(s_done, c)
                        else:
                            pe.wait_ge(g_done, 1)
                        T.matmul(banks[1 + c % 2][:, 0:HD], lhsT=M1T[:, c, :], rhs=S[:, c, :],
                                 start=True, stop=True).then_inc(m_ready, 1)
                        cond.take(pe, c % 4 * 2, c % 4 * 2 + 2)
                    for c in range(NCH):
                        last = T.matmul(banks[3][:, c * HD:(c + 1) * HD], lhsT=WT[:, c, :],
                                        rhs=S[:, c, :], start=True, stop=True, skip_group_check=True)
                    last.then_inc(u_ready, 1)
                    pe.wait_ge(u_done, 1)
                    for c in range(NCH):
                        y = banks[5][:, c * HD:(c + 1) * HD]
                        T.matmul(y, lhsT=Rb[:, c, :], rhs=S[:, c, :], start=True, stop=False,
                                 skip_group_check=True)
                        T.matmul(y, lhsT=RbT[:, c, :], rhs=U[:, c, :], start=False, stop=False,
                                 skip_group_check=True)
                        last = T.matmul(y, lhsT=RkT[:, c, :], rhs=V[:, c, :], start=False, stop=True,
                                        skip_group_check=True)
                    last.then_inc(y_ready, 1)
                    for _ in range(2):
                        cond.take(pe)
                    pe.wait_ge(gain_done, 1)
                    for c in range(NCH):
                        last = T.matmul(banks[6][:, c * HD:(c + 1) * HD], lhsT=Vb[:, c, :],
                                        rhs=cons["stack"][:, :], start=True, stop=True,
                                        skip_group_check=True)
                    last.then_inc(turned, 1)

                @block.vector
                def _(dve):
                    link = core.dve_link.on(dve)
                    W_ = nc.vector
                    wide = [P, NCH, HD]

                    def bank(i):
                        return banks[i][:, :].rearrange("p (c v) -> p c v", c=NCH)

                    dve.wait_ge(g_ready, 1)
                    W_.tensor_tensor(G[:, :, :], bank(0), total.to_broadcast(wide), ALU.mult)\
                      .then_inc(g_done, 1)
                    dve.wait_ge(g_done, 1)
                    for c in range(NCH):
                        dve.wait_ge(m_ready, c + 1)
                        W_.scalar_tensor_tensor(S[:, c + 1, :], banks[1 + c % 2][:, 0:HD],
                                                total[:, c, :], G[:, c, :], ALU.mult, ALU.add)\
                          .then_inc(s_done, 1)
                    dve.wait_ge(s_done, NCH)
                    dve.wait_ge(u_ready, 1)
                    W_.tensor_tensor(U[:, :, :], bank(3), U0[:, :, :], ALU.add).then_inc(u_done, 1)
                    dve.wait_ge(b_ready, 1)
                    link(W_.tensor_copy(bonus[:, :], banks[4][:, 0:NCH]))
                    dve.wait_ge(y_ready, 1)
                    link(W_.tensor_copy(Yt[:, :, :], bank(5)))
                    for c in range(NCH):
                        last = W_.bn_stats(stats[:, c, :], Yt[:, c, :])
                    link(last)
                    for c in range(NCH):
                        last = W_.bn_aggr(mv[:, c, :], stats[:, c, :])
                    link(last)
                    link(W_.tensor_scalar(rs[:, :], mv[:, :, 1], HD * 1e-5, None, ALU.add))
                    W_.reciprocal(rs[:, :], rs[:, :]).then_inc(norm, 1)
                    link(W_.tensor_tensor(Yt[:, :, :], Yt[:, :, :], mv[:, :, 0:1].to_broadcast(wide),
                                          ALU.subtract))
                    dve.wait_ge(root, 1)
                    link(W_.tensor_tensor(Yt[:, :, :], Yt[:, :, :],
                                          rs[:, :].unsqueeze(2).to_broadcast(wide), ALU.mult))
                    link(W_.tensor_tensor(Yt[:, :, :], Yt[:, :, :],
                                          lnw[:, :].unsqueeze(1).to_broadcast(wide), ALU.mult))
                    link(W_.tensor_tensor(Yt[:, :, :], Yt[:, :, :],
                                          lnb[:, :].unsqueeze(1).to_broadcast(wide), ALU.add))
                    link(W_.tensor_tensor(V[:, :, :], V[:, :, :],
                                          bonus[:, :].unsqueeze(2).to_broadcast(wide), ALU.mult))
                    for h in range(2):
                        r = slice(h * HD, (h + 1) * HD)
                        ins = W_.tensor_tensor(Vb[r, :, r], Yt[r, :, :], V[r, :, :], ALU.add)
                        link(ins) if h == 0 else ins.then_inc(gain_done, 1)
                    dve.wait_ge(turned, 1)
                    W_.tensor_tensor(out, banks[6][:, :], f["gate"], ALU.mult)

                @block.scalar
                def _(act):
                    for _ in range(2):
                        cond.put(act)
                    act.wait_ge(norm, 1)
                    nc.scalar.activation(rs[:, :], rs[:, :], ACT.Sqrt).then_inc(root, 1)
                    for _ in range(2):
                        cond.put(act)

                @block.sync
                def _(sp):
                    cond.send(sp, 4)


def products(core, name, steps, mask, cond, takes):
    nc = core.nc
    HALF = NCH // 2
    with Stage(core, name) as st:
        banks = st.banks(4)
        multiplied, written = st.sem("multiplied"), st.sem("written")
        turns = [(step, h) for step in steps for h in range(2)]
        with core.block() as block:
            @block.sync
            def _(sp):
                cond.send(sp, takes)

            @block.scalar
            def _(act):
                for _ in range(takes):
                    cond.put(act)

            @block.tensor
            def _(pe):
                for n, ((lhsT, rhs, how, arg, dst), h) in enumerate(turns):
                    if n >= 2:
                        pe.wait_ge(written, n - 1)
                    w = dst.shape[2]
                    for c in range(HALF):
                        cc = h * HALF + c
                        last = nc.tensor.matmul(
                            banks[n % 4][:, c * w:(c + 1) * w], lhsT=lhsT[:, cc, :],
                            rhs=rhs[:, cc, :] if len(rhs.shape) == 3 else rhs[:, :], start=True,
                            stop=True, skip_group_check=True)
                    last.then_inc(multiplied, 1)
                    if (n + 1) * takes // len(turns) > n * takes // len(turns):
                        cond.take(pe)

            @block.vector
            def _(dve):
                for n, ((lhsT, rhs, how, arg, dst), h) in enumerate(turns):
                    dve.wait_ge(multiplied, n + 1)
                    w = dst.shape[2]
                    part = slice(h * HALF, (h + 1) * HALF)
                    ps = banks[n % 4][:, 0:HALF * w].rearrange("p (c v) -> p c v", c=HALF)
                    if how == "mask":
                        ins = nc.vector.tensor_tensor(dst[:, part, :], ps, mask(arg), ALU.mult)
                    elif how == "add":
                        other = arg if arg.shape[1] == HALF else arg[:, part, :]
                        ins = nc.vector.tensor_tensor(dst[:, part, :], ps, other, ALU.add)
                    else:
                        ins = nc.vector.tensor_copy(dst[:, part, :], ps)
                    ins.then_inc(written, 1)


def modulation(core, cond, vec, mods, ident):
    nc = core.nc
    n = 2 * 6 * KD
    assert cond.left() == 0, cond.left()
    with Stage(core, "mod") as st:
        rows, turned = st.sb("rows", [n, 2, P]), st.sb("turned", [P, 2, n])
        loaded = st.sem("loaded")
        with core.block() as block:
            @block.sync
            def _(sp):
                for i in range(2):
                    sp.wait_ge(cond.stored[i], 16 * (len(cond.chunks) // 2))
                for s in range(2):
                    sp.dma_start(rows[:, s, :], core.dram["ada_rows"][s].rearrange("(j p) -> j p", p=P))\
                      .then_inc(loaded, 16)
                sp.wait_ge(loaded, 32)
        turn(core, "mod_t", [([rows[:, s, :]], turned[:, s, :].unsqueeze(1), None) for s in range(2)],
             ident)
        with core.block() as block:
            @block.vector
            def _(dve):
                link = core.dve_link.on(dve)
                for layer, mod in enumerate(mods):
                    at = VEC_AT["ada_b_2"] + 48 * layer
                    link(nc.vector.tensor_tensor(
                        mod[:, :, :], turned[:, :, 48 * layer:48 * (layer + 1)],
                        vec[:, at:at + 48].unsqueeze(1).to_broadcast([P, 2, 48]), ALU.add))
                    for which, g in ((1, 0), (4, 2)):
                        for s in range(2):
                            m = mod[:, s, which * KD:(which + 1) * KD]
                            nc.vector.scalar_tensor_tensor(m, m, 1.0, gain_of(vec, layer, g), ALU.add,
                                                           ALU.mult)


def gain_of(vec, layer, i):
    g = VEC_AT["norm_g_2"] + KD * (4 * layer + i)
    return vec[:, g:g + KD]


def gate_rows(core, name, layer, which, i, vec, mod, rows, ident):
    nc = core.nc
    n = rows.shape[1]
    with Stage(core, name) as st:
        banks = st.banks(2 * n)
        gated = st.sb("gated", [P, n, KD])
        gates, spread = st.sem("gates"), st.sem("spread")
        with core.block() as block:
            @block.vector
            def _(dve):
                nc.vector.tensor_tensor(gated[:, :, :], mod[:, 0:n, which * KD:(which + 1) * KD],
                                        gain_of(vec, layer, i).unsqueeze(1).to_broadcast([P, n, KD]),
                                        ALU.mult).then_inc(gates, 1)
                for b in range(2 * n):
                    dve.wait_ge(spread, b + 1)
                    nc.vector.tensor_copy(rows[:, b // 2, (b % 2) * BANK:(b % 2 + 1) * BANK], banks[b][:, :])

            @block.tensor
            def _(pe):
                pe.wait_ge(gates, 1)
                for b in range(2 * n):
                    for k in range(4):
                        kk = (b % 2) * 4 + k
                        last = nc.tensor.matmul(banks[b][:, k * P:(k + 1) * P],
                                                lhsT=gated[:, b // 2, kk:kk + 1].to_broadcast([P, P]),
                                                rhs=ident[:, :], start=True, stop=True,
                                                skip_group_check=True)
                    last.then_inc(spread, 1)


def rotate(core, name, tiles, rot, cos, sin):
    nc = core.nc
    with Stage(core, name) as st:
        banks = st.banks(4)
        r, c, s = st.sb("rot", [P, P]), st.sb("cos", [P, SEQ]), st.sb("sin", [P, SEQ])
        tmp = st.sb("tmp", [P, 2, SEQ])
        load(core, name + "_c", [(r[:, :], const(core, rot)), (c[:, :], const(core, cos)),
                                 (s[:, :], const(core, sin))])
        swapped, scaled, done = st.sem("swapped"), st.sem("scaled"), st.sem("done")
        with core.block() as block:
            @block.tensor
            def _(pe):
                for i, (whole, part) in enumerate(tiles):
                    if i >= 4:
                        pe.wait_ge(done, i - 3)
                    n = whole.shape[0]
                    nc.tensor.matmul(banks[i % 4][0:n, :], lhsT=r[0:n, 0:n], rhs=whole, start=True,
                                     stop=True).then_inc(swapped, 1)

            @block.vector
            def _(dve):
                def rows(i):
                    a = tiles[i][1].start_partition()
                    return slice(a, a + tiles[i][1].shape[0])

                def products(i):
                    q, part = rows(i), tiles[i][1]
                    dve.wait_ge(swapped, i + 1)
                    if i >= 2:
                        dve.wait_ge(done, i - 1)
                    nc.vector.tensor_tensor(tmp[q, i % 2, :], banks[i % 4][q, :], s[q, :], ALU.mult)
                    nc.vector.tensor_tensor(part, part, c[q, :], ALU.mult).then_inc(scaled, 1)

                products(0)
                for i, (whole, part) in enumerate(tiles):
                    if i + 1 < len(tiles):
                        products(i + 1)
                    dve.wait_ge(scaled, i + 1)
                    nc.vector.tensor_tensor(part, part, tmp[rows(i), i % 2, :], ALU.add)\
                      .then_inc(done, 1)


def window_and_diff(core, get_input, o_tok, ident):
    nc, dram = core.nc, core.dram
    T_QAW, T_QD, T_KAW, T_VAW, T_KD, T_VD = 0, 4, 8, 9, 10, 14
    with Stage(core, "ab") as st:
        p = st.sb("p", [P, 18, ALL])
        with Stage(core, "ab_h") as sh:
            ring = o_tok.rearrange("p t d -> p (t d)").rearrange("p (s k c) -> p s k c", s=W_SLOTS,
                                                                 k=KD)
            weights = Weights(core, sh, "ab_in", dram["ab_w_in_2"][0], 256, KD, ring=ring).ahead()
            h = get_input(sh)
            linear(core, "ab_in", weights, [h[0:SEQ], h[SEQ:ALL]], "features",
                   copy_out(nc, lambda s, t, c, cw: p[:, t, SEQ * s:(SEQ, ALL)[s]]))
        v = st.sb("v", [P, NX + NC_, 5 * P])
        turn(core, "ab_v", [g for t in range(NX + NC_) for g in (
            ([p[:, f, t * P:(t + 1) * P] for f in (T_VAW, T_VD, T_VD + 1, T_VD + 2)],
             v[:, t, 0:4 * P].rearrange("p (b c) -> p b c", b=4), None),
            ([p[:, T_VD + 3, t * P:(t + 1) * P]], v[:, t, 4 * P:5 * P].unsqueeze(1), None))], ident)
        rotate(core, "ab_r", [(p[:, f, 0:SEQ],) * 2 for f in (*range(T_QAW, T_KAW + 1),
                                                               *range(T_KD, T_VD))],
               "rot64", "cos64", "sin64")
        small = st.sb("small", [P, 8])
        keep = st.sb("keep", [P, 2, P])
        lv = st.sb("lv", [P, 4, HD])
        lam = st.sb("lam", [P, 4])
        gain = st.sb("gain", [P, P])
        load(core, "ab_c", [(small[:, :], bass.AP(dram["ab_sink_2"].tensor, 0, [[0, P], [1, 8]])),
                            (keep[:, 0, :], const(core, "keep_before")),
                            (keep[:, 1, :], const(core, "keep_after")),
                            (lv[:, :, :], bass.AP(dram["diff_lambda_2"].tensor, 0,
                                                  [[0, P], [HD, 4], [1, HD]])),
                            (gain[:, :], bass.AP(dram["diff_subln_g_2"].tensor, 0, [[0, P], [1, P]]))])
        dots, exps = st.sem("dots"), st.sem("exps")
        lam0 = 0.8 - 0.6
        with core.block() as block:
            @block.vector
            def _(dve):
                link = core.dve_link.on(dve)
                link(nc.vector.tensor_scalar(small[:, :], small[:, :], -1.0, None, ALU.mult))
                for i in range(2):
                    link(nc.vector.tensor_tensor(lv[:, 2 * i, :], lv[:, 2 * i, :], lv[:, 2 * i + 1, :],
                                                 ALU.mult))
                    link(nc.vector.reduce_sum(lam[:, i:i + 1], lv[:, 2 * i, :], AX.X))
                nc.vector.sem_inc(dots, 1)
                dve.wait_ge(exps, 1)
                link(nc.vector.tensor_tensor(lam[:, 2:3], lam[:, 0:1], lam[:, 1:2], ALU.subtract))
                link(nc.vector.tensor_scalar(lam[:, 2:3], lam[:, 2:3], lam0, None, ALU.add))

            @block.scalar
            def _(act):
                act.wait_ge(dots, 1)
                nc.scalar.activation(lam[:, 0:2], lam[:, 0:2], ACT.Exp).then_inc(exps, 1)
        copied, moved = st.sem("copied"), st.sem("moved")
        with core.block() as block:
            @block.sync
            def _(sp):
                sp.dma_start(p[0:HD, T_VAW, :], p[HD:P, T_KAW, :]).then_inc(copied, 16)
                sp.dma_start(p[HD:P, T_VAW, :], p[HD:P, T_KAW, :]).then_inc(copied, 16)
                sp.wait_ge(copied, 32)
                sp.dma_start(p[HD:P, T_KAW, :], p[0:HD, T_KAW, :]).then_inc(moved, 16)
                sp.wait_ge(moved, 16)
        jobs, groups = [], []
        ctx_blocks = list(range(NX, NX + NC_))
        ctx_keys = slice(SEQ, ALL)
        for h in range(8):
            rq = slice(HD * (h % 2), HD * (h % 2) + HD)
            kv = h // 4
            queries, keys = p[:, T_QAW + h // 2, :], p[:, (T_KAW, T_VAW)[kv], :]
            if h % 2 == 0:
                groups.append((queries, keys))
            for t in range(NX + NC_):
                near = [b for b in (t - 1, t, t + 1) if 0 <= b < NX] if t < NX else []
                split, rest, bias = [(0, ctx_keys)], [], []
                at, near_at = (NC_) * P, near[0] * P if near else 0
                if near:
                    split.append((at, slice(near_at, near_at + 2 * P)))
                    if len(near) == 3:
                        rest.append((at + 2 * P, keys[rq, near_at + 2 * P:near_at + 3 * P]))
                    if t >= 1:
                        bias.append((at, ident[:, :], keep[:, 0, :]))
                    if t + 1 < NX:
                        bias.append((at + P * (len(near) - 1), ident[:, :], keep[:, 1, :]))
                cols = slice(t * P, (t + 1) * P)
                jobs.append(dict(group=len(groups) - 1, rows=rq, columns=cols, split=split,
                                 q=queries[rq, cols], keys=rest, bias=bias, hide=None,
                                 values=[v[:, b, kv * HD:(kv + 1) * HD] for b in ctx_blocks + near],
                                 scale=HD ** -0.5, sink=small[:, h:h + 1],
                                 out=o_tok[:, t, h * HD:(h + 1) * HD], minus=None))
        for h in range(4):
            groups.append((p[:, T_QD + h, :], p[:, T_KD + h, :]))
            for t in range(NX + NC_):
                blocks = list(range(NX + NC_)) if t < NX else ctx_blocks
                out = o_tok[:, t, BANK + h * P:BANK + (h + 1) * P]
                for m in range(2):
                    rq = slice(HD * m, HD * m + HD)
                    split = [(0, slice(0, SEQ)), (SEQ, ctx_keys)] if t < NX else [(0, ctx_keys)]
                    jobs.append(dict(group=len(groups) - 1, rows=rq, columns=slice(t * P, (t + 1) * P),
                                     split=split, keys=[], bias=[], hide=None,
                                     values=[v[:, b, (1 + h) * P:(2 + h) * P] for b in blocks],
                                     scale=HD ** -0.5, sink=None, out=out,
                                     minus=(lam[:, 2:3], out) if m else None))
        attend(core, "ab_at", jobs, ident, groups)
        total = st.sb("total", [P, 24])
        sq = st.sb("sq", [P, 4, P])
        summed, inverted, rooted = st.sem("summed"), st.sem("inverted"), st.sem("rooted")
        with core.block() as block:
            cells = [o_tok[:, t, BANK + h * P:BANK + (h + 1) * P] for t in range(NX + NC_)
                     for h in range(4)]

            @block.scalar
            def _(act):
                for i, o in enumerate(cells):
                    if i >= 4:
                        act.wait_ge(summed, i - 3)
                    nc.scalar.activation(sq[:, i % 4, :], o, ACT.Square, accum_out=total[:, i:i + 1])\
                      .then_inc(summed, 1)
                act.wait_ge(inverted, 1)
                nc.scalar.activation(total[:, :], total[:, :], ACT.Sqrt).then_inc(rooted, 1)

            @block.vector
            def _(dve):
                link = core.dve_link.on(dve)
                link(nc.vector.tensor_scalar(gain[:, :], gain[:, :], 1.0 - lam0, None, ALU.mult))
                dve.wait_ge(summed, len(cells))
                invert_mean(core, link, total[:, :], P).then_inc(inverted, 1)
                dve.wait_ge(rooted, 1)
                for i, o in enumerate(cells):
                    nc.vector.scalar_tensor_tensor(o, o, total[:, i:i + 1], gain[:, :], ALU.mult,
                                                   ALU.mult)


def latent(core, get_input, o_tok, v, vec, ident):
    nc, dram = core.nc, core.dram
    QL, KL, NH, NOPE, ROPE = 384, 256, 16, 64, 32
    DK = NOPE + ROPE
    NT = NX + NC_
    with Stage(core, "la") as st:
        pq = Pair(st.stack.enter_context(Stage(core, "la_pq")), 3, SEQ)
        pkv = Pair(st.stack.enter_context(Stage(core, "la_pkv")), 2, ALL)
        rope = st.sb("rope", [DK, ALL])
        wkv = dram["mla_wkv_b_2"][0]

        def slots(memory, at, kchunk, width):
            n = W_SLOTS * kchunk * width
            return memory.rearrange("p t d -> p (t d)")[:, at:at + n]\
                .rearrange("p (s k c) -> p s k c", s=W_SLOTS, k=kchunk)

        w_queries = Weights(core, st, "w_queries", dram["mla_wq_b_2"][0], 2 * DK, 3,
                            ring=slots(o_tok, 0, 3, 2 * DK))
        w_keys = Weights(core, st, "w_keys", wkv, 256, 2, half=0, ring=slots(o_tok, 2 * D, 2, 256))
        w_values = Weights(core, st, "w_values", wkv, 256, 2, half=1,
                           ring=slots(o_tok, 4 * D, 2, 256))
        with Stage(core, "lc") as s3:
            ptok = s3.sb("ptok", [P, NT, QL + KL + ROPE])
            w = dram["mla_w_in_2"][0]
            with Stage(core, "la_h") as sh:
                w_q = Weights(core, sh, "w_q", w, QL, 4, cols=QL,
                              ring=slots(v[:, :, :], 0, 4, QL)).ahead()
                w_k = Weights(core, sh, "w_k", w, KL + ROPE, 2, col0=QL).ahead()
                h = get_input(sh)
                linear(core, "la_q", w_q, [h[0:SEQ]], "tokens",
                       copy_out(nc, lambda s, t, c, cw: ptok[:, t, 0:cw]))
                linear(core, "la_k", w_k, [h[0:ALL]], "tokens",
                       copy_out(nc, lambda s, t, c, cw: ptok[:, t, QL:QL + cw]))
            turn(core, "la_r", [([ptok[:, t, QL + KL - NOPE:QL + KL + ROPE]],
                                 rope[NOPE:DK, t * P:(t + 1) * P].unsqueeze(1), None)
                                for t in range(NT)], ident)
            for weights in (w_queries, w_keys, w_values):
                weights.ahead()
            gq, gk = VEC_AT["mla_q_norm_g_2"], VEC_AT["mla_kv_norm_g_2"]
            norm_to_features(core, "la_nq", [(ptok[:, t, 0:QL], pq[t * P:(t + 1) * P],
                                              vec[:, gq:gq + 3], None) for t in range(NX)], ident)
            norm_to_features(core, "la_nk", [(ptok[:, t, QL:QL + KL], pkv[t * P:(t + 1) * P],
                                              vec[:, gk:gk + 2], None) for t in range(NT)], ident)
        qT = st.sb("qT", [DK, NH, SEQ])
        kT = st.sb("kT", [DK, NH, ALL])
        linear(core, "la_wq", w_queries, [pq[0:SEQ]], "features",
               copy_out(nc, lambda s, t, c, cw: qT[:, t, :]), out_tile=DK)
        srcs = [pkv[0:SEQ], pkv[SEQ:ALL]]

        def keys(eng, ps, s, t, c, cw):
            cols = slice(SEQ * s, (SEQ, ALL)[s])
            nc.scalar.activation(kT[0:NOPE, 2 * t, cols], ps[0:NOPE], ACT.Copy)
            return nc.scalar.activation(kT[0:NOPE, 2 * t + 1, cols], ps[NOPE:P], ACT.Copy)

        linear(core, "la_wk", w_keys, srcs, "features", keys)
        tiles = [(qT[:, h, :], qT[NOPE:DK, h, :]) for h in range(NH)]
        with core.block() as block:
            @block.vector
            def _(dve):
                nc.vector.memset(rope[0:NOPE, :], 0.0)
        tiles.append((rope[:, 0:SEQ], rope[NOPE:DK, 0:SEQ]))
        rotate(core, "la_rot", tiles, "rot32", "cos32", "sin32")
        with core.block() as block:
            @block.vector
            def _(dve):
                for h in range(0, NH, 2):
                    nc.vector.tensor_copy(kT[NOPE:DK, h, :], rope[NOPE:DK, :])

            @block.scalar
            def _(act):
                for h in range(1, NH, 2):
                    nc.scalar.activation(kT[NOPE:DK, h, :], rope[NOPE:DK, :], ACT.Copy)
        linear(core, "la_wv", w_values, [pkv[0:ALL]], "tokens",
               copy_out(nc, lambda s, t, c, cw: v[:, t, c:c + cw]))
        groups = [(qT[:, h, :], kT[:, h, :]) for h in range(NH)]
        jobs = [dict(group=h, rows=slice(0, DK), columns=slice(t * P, (t + 1) * P),
                     split=[(0, slice(0, SEQ)), (SEQ, slice(SEQ, ALL))], keys=[], bias=[], hide=None,
                     values=[v[:, b, h * HD:(h + 1) * HD] for b in range(NT)],
                     scale=DK ** -0.5, sink=None, out=o_tok[:, t, h * HD:(h + 1) * HD], minus=None)
                for h in range(NH) for t in range(NX)]
        key_parts = [m[:, :, :].rearrange("p k t -> p (k t)").rearrange("p (g t) -> p g t", g=2)
                     for m in (pq.hi, pq.lo)]
        attend(core, "la_at", jobs, ident, groups, key_parts)


def program(nc, dram, out):
    with ExitStack() as stack:
        core = Core(nc, stack, dram)

        def sb(name, shape):
            return stack.enter_context(nc.sbuf_tensor(name, shape, F32))

        ident = sb("ident", [P, P])
        vec = sb("vec", [P, N_VEC])
        x = sb("x", [P, NX, D])
        feat = sb("feat", [P, KD, ALL])

        tok = feat[:, :, :].rearrange("p k t -> p (k t)").rearrange("p (t d) -> p t d", d=D)

        n_rows = (N_VEC + P - 1) // P
        with Stage(core, "vec") as st:
            rows_sb = st.sb("rows", [P, n_rows, P])
            cleared, loaded = st.sem("cleared"), st.sem("loaded")
            with core.block() as block:
                @block.vector
                def _(dve):
                    nc.vector.memset(rows_sb[:, :, :], 0.0).then_inc(cleared, 1)

                @block.sync
                def _(sp):
                    sp.dma_start(ident[:, :], const(core, "ident")).then_inc(loaded, 16)
                    sp.dma_start(x[:, :, :], dram["x"][0].rearrange("(t p) d -> p t d", p=P))\
                      .then_inc(loaded, 16)
                    sp.wait_ge(cleared, 1)
                    n = 2
                    for name, rows in VECTORS:
                        at, r = VEC_AT[name], 0
                        while r < rows:
                            m = min(rows - r, P - (at + r) % P)
                            src = bass.AP(dram[name].tensor, r * P, [[P, m], [1, P]])
                            p0 = (at + r) % P
                            sp.dma_start(rows_sb[p0:p0 + m, (at + r) // P, :], src).then_inc(loaded, 16)
                            r, n = r + m, n + 1
                    sp.wait_ge(loaded, 16 * n)
            turn(core, "vec_t", [([rows_sb[:, i, :]],
                                  vec[:, i * P:min(N_VEC, (i + 1) * P)].unsqueeze(1), None)
                                 for i in range(n_rows)], ident)

        def v(name, i=0, n=KD):
            return vec[:, VEC_AT[name] + i:VEC_AT[name] + i + n]

        def tok_tile(t):
            return tok[:, t, :]

        silu_c = sb("silu_c", [P, KD, 2])
        mods = [sb(f"mod{i}", [P, 2, 48]) for i in range(2)]
        with core.block() as block:
            @block.scalar
            def _(act):
                for s, name in enumerate(("c_2", "c_ctx_2")):
                    nc.scalar.activation(silu_c[:, :, s], v(name), ACT.Silu)

        with Stage(core, "m1") as st:
            proj = st.sb("proj", [P, N_PROJ, SEQ])
            with Stage(core, "m0") as s0:
                h = Pair(s0, KD, SEQ)
                weights = Weights(core, s0, "w_in", dram["w_in"][0], 256, KD).ahead()
                norm_to_features(core, "n1", [(x[:, t, :], h[t * P:(t + 1) * P], v("norm_mix_pre"), None)
                                              for t in range(NX)], ident)
                linear(core, "w_in", weights, [h[0:SEQ]], "features",
                       copy_out(nc, lambda s, t, c, cw: proj[:, t, :]))
            mix = feat
            chunk_attention(core, proj, mix[:, :, 0:SEQ], ident,
                            lambda: rglru(core, proj, mix[:, :, 0:SEQ], vec))
            with Stage(core, "ada") as sa:
                cond = Conditioning(core, sa, silu_c)
                hgrn(core, proj, mix[:, :, 0:SEQ], vec, ident, cond)
                rwkv(core, proj, mix[:, :, 0:SEQ], vec, ident, cond)
                modulation(core, cond, vec, mods, ident)
        with Stage(core, "o1") as st:
            row = st.sb("row", [P, 2, D])
            load(core, "o1_c", [(row[:, i, :], bass.AP(dram[n].tensor, 0, [[0, P], [1, D]]))
                                for i, n in enumerate(("norm_mix_post", "norm_mlp_post"))])
            with Stage(core, "mlp") as s2:
                ff = s2.sb("ff", [P, MLP // P, SEQ])
                relu = s2.sb("relu", [P, 2, SEQ])

                def squared_relu(eng, ps, s, t, c, cw):
                    link = core.dve_link.on(eng)
                    link(nc.vector.tensor_scalar(relu[:, t % 2, :], ps, 0.0, None, ALU.max))
                    return nc.vector.tensor_tensor(ff[:, t, :], relu[:, t % 2, :], relu[:, t % 2, :],
                                                   ALU.mult)

                w2 = Weights(core, s2, "w2", dram["mlp_w2"][0]).ahead()
                with Stage(core, "mlph") as s3:
                    h = Pair(s3, KD, SEQ)
                    flat = ff[:, :, :].rearrange("p k t -> p (k t)")
                    y = flat[:, 0:NX * D].rearrange("p (t d) -> p t d", d=D)
                    ring = flat[:, NX * D:NX * D + W_SLOTS * 2 * BANK]\
                        .rearrange("p (s k c) -> p s k c", s=W_SLOTS, k=2)
                    joined = Join(core, s3, lambda t: y[:, t, :], NX)
                    with Stage(core, "j0") as sj:
                        weights = Weights(core, sj, "w_out", dram["w_out"][0], ring=ring)
                        linear(core, "w_out", weights, [feat[:, :, 0:SEQ]], "tokens",
                               joined.finish(sj, lambda t: row[:, 0, :]))
                    weights = Weights(core, s3, "w1", dram["mlp_w1"][0], 256, 4).ahead()
                    norm_to_features(core, "n2", [(x[:, t, :], h[t * P:(t + 1) * P],
                                                   v("norm_mlp_pre"), None) for t in range(NX)],
                                     ident, joined)
                    linear(core, "w1", weights, [h[0:SEQ]], "features", squared_relu,
                           engine="dve")
                joined = Join(core, s2, tok_tile, NX)
                linear(core, "w2", w2, [ff[:, :, :]], "tokens",
                       joined.finish(s2, lambda t: row[:, 1, :]))
                join(core, "r2", joined, [x[:, t, :] for t in range(NX)])

        ctx = sb("ctx", [P, NC_, D])
        load(core, "ctx", [(ctx[:, :, :], dram["ctx_2"][0].rearrange("(t p) d -> p t d", p=P))])
        for layer in range(2):
            last = layer == 1
            nt = NX if last else NX + NC_
            L = f"l{layer}"
            mod = mods[layer]

            def stream(t):
                return x[:, t, :] if t < NX else ctx[:, t - NX, :]

            def normed(name, which, tiles, h, joined=None):
                norm_to_features(core, name, [
                    (stream(t), h[t * P:(t + 1) * P],
                     mod[:, int(t >= NX), (which + 1) * KD:(which + 2) * KD],
                     mod[:, int(t >= NX), which * KD:(which + 1) * KD]) for t in range(tiles)], ident, joined)

            def attention_input(stage):
                h = Pair(stage, KD, ALL)
                normed(L + "n1", 0, NX + NC_, h)
                return h

            if last:
                with Stage(core, "lv") as sv:
                    values = sv.sb("values", [P, NX + NC_, D])
                    latent(core, attention_input, tok, values, vec, ident)
                w_out = dram["mla_w_out_2"][0]
            else:
                window_and_diff(core, attention_input, tok, ident)
                w_out = dram["ab_w_out_2"][0]
            with Stage(core, L + "f") as sf:
                ff = sf.sb("ff", [P, FFN // P, nt * P])
                flat = ff[:, :, :].rearrange("p k t -> p (k t)")
                y = flat[:, 0:nt * D].rearrange("p (t d) -> p t d", d=D)
                oT = flat[:, nt * D:2 * nt * D].rearrange("p (k t) -> p k t", k=KD)
                n_ring = W_SLOTS * 2 * BANK
                ring = flat[:, 2 * nt * D:2 * nt * D + n_ring]\
                    .rearrange("p (s k c) -> p s k c", s=W_SLOTS, k=2)
                joined = Join(core, sf, lambda t: y[:, t, :], nt)
                with Stage(core, L + "o") as so:
                    rows = so.sb("rows", [P, 1 if last else 2, D])
                    weights = Weights(core, so, "wo", w_out, ring=ring).ahead()
                    gate_rows(core, L + "s1", layer, 2, 1, vec, mod, rows, ident)
                    turn(core, L + "t", [([tok[:, t, (4 * g + i) * P:(4 * g + i + 1) * P]
                                           for i in range(4)],
                                          oT[:, 4 * g:4 * g + 4, t * P:(t + 1) * P], None)
                                         for t in range(nt) for g in range(2)], ident)
                    linear(core, L + "wo", weights, [oT], "tokens",
                           joined.finish(so, lambda t: rows[:, int(t >= NX), :]))
                parts = [slice(0, SEQ)] + ([] if last else [slice(SEQ, ALL)])
                with Stage(core, L + "fh") as sh:
                    raw = feat[:, :, :].rearrange("p k t -> p (k t)")\
                        .rearrange("p (s h k c) -> p s h k c", s=3, h=2, c=P)
                    weights = GateUpWeights(core, sh, "w13", dram["ffn_w13_2"][layer], raw).ahead()
                    h = Pair(sh, KD, nt * P)
                    normed(L + "n2", 3, nt, h, joined)
                    gated_up(core, L + "w13", weights, [h[s] for s in parts],
                             [ff[:, :, s] for s in parts])
                rows = sf.sb("rows", [P, 1 if last else 2, D])
                weights = Weights(core, sf, "w2", dram["ffn_w2_2"][layer]).ahead()
                gate_rows(core, L + "s2", layer, 5, 3, vec, mod, rows, ident)
                joined = Join(core, sf, tok_tile, nt)
                linear(core, L + "w2", weights, [ff[:, :, :]], "tokens",
                       joined.finish(sf, lambda t: rows[:, int(t >= NX), :]))
                join(core, L + "r2", joined, [stream(t) for t in range(nt)])
        stored = stack.enter_context(nc.semaphore("stored"))
        with core.block() as block:
            @block.sync
            def _(sp):
                sp.dma_start(out[0].rearrange("(t p) d -> p t d", p=P), x[:, :, :]).then_inc(stored, 16)
                sp.wait_ge(stored, 16)


_INS = ["x", "norm_mix_pre", "norm_mix_post", "norm_mlp_pre", "norm_mlp_post", "w_in", "w_out",
        "attn_rel_bias", "hgrn_norm", "rwkv_mu", "rwkv_w0", "rwkv_w2", "rwkv_a0",
        "rwkv_a2", "rwkv_g2", "rwkv_k_k", "rwkv_k_a", "rwkv_r_k", "rwkv_ln_w", "rwkv_ln_b",
        "lru_conv_w", "lru_conv_b", "lru_wa", "lru_ba", "lru_wx", "lru_bx", "lru_lambda", "mlp_w1",
        "mlp_w2", "c_2", "ctx_2", "c_ctx_2", "ada_w_2", "ada_b_2", "norm_g_2", "ffn_w13_2", "ffn_w2_2",
        "ab_w_in_2", "ab_w_out_2", "ab_sink_2", "diff_lambda_2", "diff_subln_g_2", "mla_w_in_2",
        "mla_q_norm_g_2", "mla_kv_norm_g_2", "mla_wq_b_2", "mla_wkv_b_2", "mla_w_out_2"]


def kernel(**inputs):
    import concourse.bacc as bacc
    from concourse.bass_utils import run_bass_kernel_spmd

    nc = bacc.Bacc("TRN2", target_bir_lowering=False, num_devices=1)
    arrays, dram = {}, {}
    for name in _INS:
        a = np.ascontiguousarray(inputs[name])
        arrays[f"in_{name}"] = a
        dram[name] = nc.dram_tensor(f"in_{name}", a.shape, mybir.dt.from_np(a.dtype),
                                    kind="ExternalInput").ap()
    arrays["shape_constants"] = shape_constants()
    dram["consts"] = nc.dram_tensor("shape_constants", (P, N_CONST), F32, kind="ExternalInput").ap()
    dram["bias_ext"] = nc.dram_tensor("bias_ext", (GW // HD, 2 * SEQ), F32, kind="Internal").ap()
    dram["ada_rows"] = nc.dram_tensor("modulation_rows", (2, 12 * D), F32, kind="Internal").ap()
    out = nc.dram_tensor("out", (1, SEQ, D), F32, kind="ExternalOutput").ap()
    program(nc, dram, out)
    r = run_bass_kernel_spmd(nc, [arrays], core_ids=[0])
    return r.results[0]["out"]
```
